# Optimizing a Trainium2 kernel written in Bass

```python
import math
import jax, jax.numpy as jnp
from jax import lax
import numpy as np

D_MODEL = 1024
BATCH = 1
SEQ = 512
DEPTH = 1

MLA_HEADS = 8
MLA_Q_LORA = 256
MLA_KV_LORA = 128
MLA_NOPE = 64
MLA_ROPE = 32
MLA_V = 64
Q_BLOCK = 128
ROPE_THETA = 10000.0
SWA_HEADS = 8
SWA_KV_HEADS = 2
SWA_HD = 64
WINDOW = 128
BLOCK = 128
REL_BUCKETS = 32
REL_MAX_DIST = 128
MEM_LEN = 256
MEM_HEADS = 4
MEM_HD = 128
N_BRANCH = 3
D_FF = 4 * D_MODEL
EPS = 1e-6

IN_SIZES = (
    MLA_Q_LORA,
    MLA_KV_LORA + MLA_ROPE,
    SWA_HEADS * SWA_HD,
    SWA_KV_HEADS * SWA_HD,
    SWA_KV_HEADS * SWA_HD,
    MEM_HEADS * MEM_HD,
    N_BRANCH * D_MODEL,
)
IN_COLS = sum(IN_SIZES)

kernel_name = "hybrid_mla_swa_mem_gated_block"

def rms_norm(x, g):
    x32 = x.astype(jnp.float32)
    y = x32 * lax.rsqrt(jnp.mean(x32 * x32, axis=-1, keepdims=True) + EPS)
    return y.astype(x.dtype) * g

def split_points():
    pts, acc = [], 0
    for s in IN_SIZES[:-1]:
        acc += s
        pts.append(acc)
    return pts

def rope_tables(seq):
    pos = jnp.arange(seq, dtype=jnp.float32)
    inv = 1.0 / (ROPE_THETA ** (jnp.arange(0, MLA_ROPE, 2, dtype=jnp.float32) / MLA_ROPE))
    ang = pos[:, None] * inv[None, :]
    return jnp.cos(ang), jnp.sin(ang)

def apply_rope(t, cos, sin):
    cos = cos.astype(t.dtype)
    sin = sin.astype(t.dtype)
    t1, t2 = jnp.split(t, 2, axis=-1)
    return jnp.concatenate([t1 * cos - t2 * sin, t2 * cos + t1 * sin], axis=-1)

def t5_bucket(dist):
    n = jnp.maximum(dist, 0)
    max_exact = REL_BUCKETS // 2
    nf = jnp.maximum(n, 1).astype(jnp.float32)
    large = max_exact + (jnp.log(nf / max_exact) / math.log(REL_MAX_DIST / max_exact)
                         * (REL_BUCKETS - max_exact)).astype(jnp.int32)
    large = jnp.minimum(large, REL_BUCKETS - 1)
    return jnp.where(n < max_exact, n, large)

def mla_attention(q_nope, q_rope, k_nope, k_rope, v):
    B, S = q_nope.shape[0], q_nope.shape[1]
    nb = S // Q_BLOCK
    scale = (MLA_NOPE + MLA_ROPE) ** -0.5
    k_pos = jnp.arange(S)

    def to_blocks(t):
        return jnp.moveaxis(t.reshape(B, nb, Q_BLOCK, *t.shape[2:]), 1, 0)

    def one_block(args):
        qn, qr, i = args
        s = (jnp.einsum('bqhd,bkhd->bhqk', qn, k_nope)
             + jnp.einsum('bqhd,bkd->bhqk', qr, k_rope)).astype(jnp.float32) * scale
        q_pos = i * Q_BLOCK + jnp.arange(Q_BLOCK)
        s = jnp.where(k_pos[None, :] <= q_pos[:, None], s, -jnp.inf)
        p = jax.nn.softmax(s, axis=-1).astype(v.dtype)
        return jnp.einsum('bhqk,bkhd->bqhd', p, v)

    out = lax.map(one_block, (to_blocks(q_nope), to_blocks(q_rope), jnp.arange(nb)))
    return jnp.moveaxis(out, 0, 1).reshape(B, S, MLA_HEADS * MLA_V)

def swa_attention(q, k, v, rel_bias, sinks):
    B, S = q.shape[0], q.shape[1]
    nb = S // BLOCK
    G, R = SWA_KV_HEADS, SWA_HEADS // SWA_KV_HEADS
    qb = q.reshape(B, nb, BLOCK, G, R, SWA_HD)
    kb = k.reshape(B, nb, BLOCK, G, SWA_HD)
    vb = v.reshape(B, nb, BLOCK, G, SWA_HD)

    def with_prev(t):
        prev = jnp.pad(t, ((0, 0), (1, 0), (0, 0), (0, 0), (0, 0)))[:, :-1]
        return jnp.concatenate([prev, t], axis=2)

    kk, vv = with_prev(kb), with_prev(vb)
    s = jnp.einsum('bnqgrd,bnkgd->bngrqk', qb, kk).astype(jnp.float32) * (SWA_HD ** -0.5)

    qi = jnp.arange(BLOCK)[:, None]
    kj = jnp.arange(2 * BLOCK)[None, :]
    dist = qi + BLOCK - kj
    bias = rel_bias.astype(jnp.float32)[t5_bucket(dist)]
    bias = jnp.transpose(bias, (2, 0, 1)).reshape(G, R, BLOCK, 2 * BLOCK)
    band = (dist >= 0) & (dist < WINDOW)
    has_prev = (jnp.arange(nb) > 0)[:, None, None] | (kj >= BLOCK)[None]
    valid = band[None] & has_prev
    s = jnp.where(valid[None, :, None, None], s + bias, -jnp.inf)

    sink = jnp.broadcast_to(sinks.astype(jnp.float32).reshape(1, 1, G, R, 1, 1),
                            s.shape[:-1] + (1,))
    p = jax.nn.softmax(jnp.concatenate([s, sink], axis=-1), axis=-1)[..., :-1].astype(v.dtype)
    o = jnp.einsum('bngrqk,bnkgd->bnqgrd', p, vv)
    return o.reshape(B, S, SWA_HEADS * SWA_HD)

def mem_attention(q, km, vm):
    B, S = q.shape[0], q.shape[1]
    s = jnp.einsum('bshd,bmhd->bhsm', q, km).astype(jnp.float32) * (MEM_HD ** -0.5)
    p = jax.nn.softmax(s, axis=-1).astype(vm.dtype)
    return jnp.einsum('bhsm,bmhd->bshd', p, vm).reshape(B, S, MEM_HEADS * MEM_HD)

def setup_inputs(seed: int = 0) -> dict:
    key = jax.random.key(seed)
    ks = jax.random.split(key, 24)

    def nrm(k, shape, scale):
        return jax.random.normal(k, shape, jnp.float32) * scale

    def gain(k, shape):
        return 1.0 + 0.02 * jax.random.normal(k, shape, jnp.float32)

    L, D = DEPTH, D_MODEL
    return {
        "x": nrm(ks[0], (BATCH, SEQ, D), 1.0),
        "mem": nrm(ks[1], (BATCH, MEM_LEN, D), 1.0),
        "rel_bias": nrm(ks[2], (REL_BUCKETS, SWA_HEADS), 0.5),
        "attn_norm": gain(ks[3], (L, D)),
        "mem_norm": gain(ks[4], (L, D)),
        "w_in": nrm(ks[5], (L, D, IN_COLS), D ** -0.5),
        "b_gate": nrm(ks[6], (L, N_BRANCH * D), 0.02),
        "mla_q_norm": gain(ks[7], (L, MLA_Q_LORA)),
        "w_uq": nrm(ks[8], (L, MLA_Q_LORA, MLA_HEADS * (MLA_NOPE + MLA_ROPE)), MLA_Q_LORA ** -0.5),
        "mla_kv_norm": gain(ks[9], (L, MLA_KV_LORA)),
        "w_ukv": nrm(ks[10], (L, MLA_KV_LORA, MLA_HEADS * (MLA_NOPE + MLA_V)), MLA_KV_LORA ** -0.5),
        "attn_sinks": nrm(ks[11], (L, SWA_HEADS), 0.5),
        "w_mem_kv": nrm(ks[12], (L, D, 2 * MEM_HEADS * MEM_HD), D ** -0.5),
        "w_o_mla": nrm(ks[13], (L, MLA_HEADS * MLA_V, D), (MLA_HEADS * MLA_V) ** -0.5),
        "w_o_swa": nrm(ks[14], (L, SWA_HEADS * SWA_HD, D), (SWA_HEADS * SWA_HD) ** -0.5),
        "w_o_mem": nrm(ks[15], (L, MEM_HEADS * MEM_HD, D), (MEM_HEADS * MEM_HD) ** -0.5),
        "w_out": nrm(ks[16], (L, D, D), D ** -0.5),
        "mlp_norm": gain(ks[17], (L, D)),
        "w_up": nrm(ks[18], (L, D, D_FF), D ** -0.5),
        "w_down": nrm(ks[19], (L, D_FF, D), D_FF ** -0.5),
        "final_norm": gain(ks[20], (D,)),
    }

def reference(x, mem, rel_bias, attn_norm, mem_norm, w_in, b_gate, mla_q_norm, w_uq,
              mla_kv_norm, w_ukv, attn_sinks, w_mem_kv, w_o_mla, w_o_swa, w_o_mem,
              w_out, mlp_norm, w_up, w_down, final_norm):
    B, S, D = x.shape
    cos, sin = rope_tables(S)
    pts = split_points()

    for l in range(DEPTH):
        h = rms_norm(x, attn_norm[l])
        proj = h @ w_in[l]
        c_q, kv_a, q_s, k_s, v_s, q_m, gates = jnp.split(proj, pts, axis=-1)

        c_q = rms_norm(c_q, mla_q_norm[l])
        q = (c_q @ w_uq[l]).reshape(B, S, MLA_HEADS, MLA_NOPE + MLA_ROPE)
        q_nope = q[..., :MLA_NOPE]
        q_pe = apply_rope(q[..., MLA_NOPE:], cos[:, None, :], sin[:, None, :])
        c_kv = rms_norm(kv_a[..., :MLA_KV_LORA], mla_kv_norm[l])
        k_pe = apply_rope(kv_a[..., MLA_KV_LORA:], cos, sin)
        kv = (c_kv @ w_ukv[l]).reshape(B, S, MLA_HEADS, MLA_NOPE + MLA_V)
        o_mla = mla_attention(q_nope, q_pe, kv[..., :MLA_NOPE], k_pe, kv[..., MLA_NOPE:])

        o_swa = swa_attention(q_s.reshape(B, S, SWA_HEADS, SWA_HD),
                              k_s.reshape(B, S, SWA_KV_HEADS, SWA_HD),
                              v_s.reshape(B, S, SWA_KV_HEADS, SWA_HD),
                              rel_bias, attn_sinks[l])

        mn = rms_norm(mem, mem_norm[l])
        kvm = (mn @ w_mem_kv[l]).reshape(mem.shape[0], MEM_LEN, 2, MEM_HEADS, MEM_HD)
        o_mem = mem_attention(q_m.reshape(B, S, MEM_HEADS, MEM_HD), kvm[:, :, 0], kvm[:, :, 1])

        g = jax.nn.sigmoid(gates + b_gate[l]).reshape(B, S, N_BRANCH, D)
        y = (g[..., 0, :] * (o_mla @ w_o_mla[l])
             + g[..., 1, :] * (o_swa @ w_o_swa[l])
             + g[..., 2, :] * (o_mem @ w_o_mem[l]))
        x = x + y @ w_out[l]

        h = rms_norm(x, mlp_norm[l])
        x = x + jnp.square(jax.nn.relu(h @ w_up[l])) @ w_down[l]

    return rms_norm(x, final_norm)


_drawn_inputs = setup_inputs


def setup_inputs(seed=0):
    import zlib

    import numpy as np

    out = dict(_drawn_inputs(seed))
    spreads = {}
    factors = {'attn_norm': 8.0,
     'mem_norm': 8.0,
     'b_gate': 8.0,
     'mla_q_norm': 8.0,
     'mla_kv_norm': 8.0,
     'attn_sinks': 169.847,
     'mlp_norm': 9.898,
     'final_norm': 25.964}
    for name, (base, spread) in spreads.items():
        noise = np.random.default_rng([zlib.crc32(name.encode()), seed]).standard_normal(out[name].shape)
        drawn = base * np.exp(spread * noise) if base else spread * noise
        out[name] = __import__('jax').numpy.asarray(drawn.astype(out[name].dtype))
    for name, factor in factors.items():
        out[name] = (out[name] * factor).astype(out[name].dtype)
    return out
```

```python
from contextlib import ExitStack

import numpy as np

import concourse.bass as bass
from concourse import mybir

F32 = mybir.dt.float32
F32R = mybir.dt.float32r
ALU = mybir.AluOpType
ACT = mybir.ActivationFunctionType
AX_X = mybir.AxisListType.X
ds = bass.ds

P = 128
D = 1024
S = 512
M = 256
KD = D // P
QT = S // P
FF = 4 * D
EPS = 1e-6
NEG = -(2.0 ** 100)
HM, DM = 4, 128
HS, DS = 8, 64
HA, NOPE, ROPE, DV = 8, 64, 32, 64
QK = NOPE + ROPE
QL, KVL = 256, 128
PAIRS = HS // 2
BUCKETS = 32
TOE = 3 * P

COL_KV = QL
COL_QS = COL_KV + KVL + ROPE
COL_KS = COL_QS + HS * DS
COL_QM = COL_KS + 2 * 2 * DS
COL_G = COL_QM + HM * DM
MLA, SWA, MEM = range(3)

BLK = 2048
SHARES = {1: (48,), 2: (16, 32), 3: (16, 16, 16)}

B_MEM = 0
B_KVS = B_MEM + 3 * HM
B_WO_MEM = B_KVS + 1
B_SWA = B_WO_MEM + 2
B_MLAP = B_SWA + 2 * PAIRS
B_WO_SWA = B_MLAP + 2
B_MLA = B_WO_SWA + 2
B_WO_MLA = B_MLA + HA
B_WOUT = B_WO_MLA + 2
B_UP = B_WOUT + D // 256
B_DOWN = B_UP + FF // 256
B_END = B_DOWN + FF // 256

T_MEM = 0
T_KVS = T_MEM + 5 * HM
T_WO_MEM = T_KVS + 2
T_SWA = T_WO_MEM + KD
T_WO_SWA = T_SWA + 3 * PAIRS
T_MLA = T_WO_SWA + KD
T_WO_MLA = T_MLA + 4 * HA
T_UP = T_WO_MLA + KD

H_MEM = 0
H_KVS = 3 * HM
H_SWA = H_KVS + 2
H_MLA = H_SWA + PAIRS

U_MEM = 0
U_SWA = 2 * HM
U_MLA = U_SWA + QT * PAIRS
U_END = U_MLA + QT * HA
E_MEM, E_SWA, E_MLA = 0, HM, HM + PAIRS
E_END = E_MLA + HA

G_X, G_MEM, G_MLA, G_H2 = 0, KD, 2 * KD, 2 * KD + 4

C_ID, C_MASK, C_COST, C_SINT, C_COS, C_SIN, C_END = np.cumsum([0, P, P, 64, 64, S, S]).tolist()


def ring(c, per, i):
    return c % 2, c // 2 + (per // 2) * i


def wait(eng, sem, value):
    if not isinstance(value, int) or value > 0:
        eng.wait_ge(sem, value)


def hybrid_layer(nc, x, mem, rel_bias, attn_norm, mem_norm, w_in, b_gate, mla_q_norm, w_uq,
                 mla_kv_norm, w_ukv, attn_sinks, w_mem_kv, w_o_mla, w_o_swa, w_o_mem, w_out,
                 mlp_norm, w_up, w_down, final_norm, consts, toeplitz, out):
    ctx = ExitStack()
    with ctx:
        place = [-(-nc.sbuf_base // 32) * 32]

        def sb(name, width, dt=F32, at=None):
            off = place[0] if at is None else at
            if at is None:
                place[0] += -(-4 * width // 32) * 32
            t = nc.alloc_sbuf_tensor_at(name, [P, width], dt, offset=off)
            return t[:, :], off

        def sem(name):
            return ctx.enter_context(nc.semaphore(name))

        w_hi = sb("w_hi", 2 * BLK, F32R)[0].rearrange("p (s n) -> p s n", s=2)
        w_lo = sb("w_lo", 2 * BLK, F32R)[0].rearrange("p (s n) -> p s n", s=2)
        h_hi_flat, h_hi_at = sb("h_hi", KD * S, F32R)
        h_lo_flat, h_lo_at = sb("h_lo", KD * S, F32R)
        h_hi = h_hi_flat.rearrange("p (k n) -> p k n", k=KD)
        h_lo = h_lo_flat.rearrange("p (k n) -> p k n", k=KD)
        attn, attn_at = sb("attn", 17408, F32R)

        def part(lo, n):
            return attn[:, lo:lo + n]

        o_hi = part(0, 2048).rearrange("p (k n) -> p k n", k=4)
        o_lo = part(2048, 2048).rearrange("p (k n) -> p k n", k=4)
        pt_hi, pt_lo = part(4096, 2048), part(6144, 2048)
        q_hi = part(8192, 1024).rearrange("p (s n) -> p s n", s=2)
        q_lo = part(9216, 1024).rearrange("p (s n) -> p s n", s=2)
        v_hi = part(10240, 512).rearrange("p (k n) -> p k n", k=4)
        v_lo = part(10752, 512).rearrange("p (k n) -> p k n", k=4)
        km_hi, km_lo = part(11264, M), part(11264 + M, M)
        mn_hi = part(11776, 2048).rearrange("p (k n) -> p k n", k=KD)
        mn_lo = part(13824, 2048).rearrange("p (k n) -> p k n", k=KD)
        kz_hi = part(11264, 1024).rearrange("p (g n) -> p g n", g=2)
        kz_lo = part(12288, 1024).rearrange("p (g n) -> p g n", g=2)
        bias_hi = part(13312, 2048).rearrange("p (g r n) -> p g r n", g=2, r=PAIRS)
        bias_lo = part(15360, 2048).rearrange("p (g r n) -> p g r n", g=2, r=PAIRS)
        ka_hi = part(11264, 1024).rearrange("p (s n) -> p s n", s=2)
        ka_lo = part(12288, 1024).rearrange("p (s n) -> p s n", s=2)
        cq_hi = part(13312, 1024).rearrange("p (k n) -> p k n", k=2)
        cq_lo = part(14336, 1024).rearrange("p (k n) -> p k n", k=2)
        ckv_hi, ckv_lo = part(15360, 512), part(15872, 512)
        act_sq = sb("act_sq", FF // P * S, F32, at=attn_at)[0]
        mem_sb = act_sq[:, 8192:8192 + 2 * D].rearrange("p (t n) -> p t n", t=2)
        yr_hi = sb("yr_hi", 2 * 1024, F32R, at=h_hi_at)[0].rearrange("p (s n) -> p s n", s=2)
        yr_lo = sb("yr_lo", 2 * 1024, F32R, at=h_lo_at)[0].rearrange("p (s n) -> p s n", s=2)

        raw = sb("raw", 2 * BLK)[0].rearrange("p (s n) -> p s n", s=2)
        xg, xg_at = sb("xg", QT * D)
        x_sb = xg.rearrange("p (t n) -> p t n", t=QT)
        gate = xg.rearrange("p (m n) -> p m n", m=KD)
        ybuf, y_at = sb("ybuf", QT * D)
        ar_hi = sb("ar_hi", 2 * 1024, F32R, at=y_at)[0].rearrange("p (s n) -> p s n", s=2)
        ar_lo = sb("ar_lo", 2 * 1024, F32R, at=y_at + 4 * 2 * 1024)[0].rearrange("p (s n) -> p s n", s=2)
        y = ybuf.rearrange("p (m n) -> p m n", m=KD)
        h2 = ybuf.rearrange("p (t n) -> p t n", t=QT)
        frep = ybuf[:, 0:HS * TOE].rearrange("p (h n) -> p h n", h=HS)
        scratch, _ = sb("scratch", BLK)
        toe = scratch[:, 0:2 * TOE]
        bias_raw = scratch
        kvq = scratch[:, 0:4 * 416].rearrange("p (t n) -> p t n", t=QT)
        rope_a, rope_b = scratch[:, 0:S], scratch[:, S:2 * S]
        fgain = scratch[:, 0:D]
        relu = scratch[:, D:2 * D].rearrange("p (s n) -> p s n", s=2)
        probs_flat, _ = sb("probs", 2 * S)
        probs = probs_flat.rearrange("p (s n) -> p s n", s=2)
        junk = probs_flat
        tmp = sb("tmp", 2 * S)[0].rearrange("p (s n) -> p s n", s=2)
        con, _ = sb("con", C_END)
        ident = con[:, C_ID:C_ID + P]
        cos_t = con[:, C_COST:C_COST + 64].rearrange("p (t n) -> p t n", t=QT)
        sin_t = con[:, C_SINT:C_SINT + 64].rearrange("p (t n) -> p t n", t=QT)
        cos_f, sin_f = con[:, C_COS:C_COS + S], con[:, C_SIN:C_SIN + S]
        ident_r, mask_r = sb("ident_r", P, F32R)[0], sb("mask_r", P, F32R)[0]
        kpad = sb("kpad", QT * QK)[0].rearrange("p (t n) -> p t n", t=QT)
        rtmp = sb("rtmp", 4 * 64)[0].rearrange("p (a t n) -> p a t n", a=4, t=QT)
        g_attn, g_mem, g_mlp = sb("g_attn", KD)[0], sb("g_mem", KD)[0], sb("g_mlp", KD)[0]
        g_q, g_kv = sb("g_q", 2)[0], sb("g_kv", 1)[0]
        hb, hb_raw = sb("hb", 3 * KD)[0], sb("hb_raw", 3 * KD)[0]
        sinks, nsinks = sb("sinks", HS)[0], sb("nsinks", HS)[0].rearrange("p (g r) -> p g r", g=2)
        rel = sb("rel", HS)[0]
        half_neg = sb("half_neg", 8)[0]
        sumsq, rstd = sb("sumsq", 24)[0], sb("rstd", 24)[0]
        mx = sb("mx", 4)[0].rearrange("p (s g) -> p s g", s=2)
        negm = sb("negm", 4)[0].rearrange("p (s g) -> p s g", s=2)
        snk = sb("snk", 4)[0].rearrange("p (s g) -> p s g", s=2)
        esnk = sb("esnk", 4)[0].rearrange("p (s g) -> p s g", s=2)
        rsum = sb("rsum", 4)[0].rearrange("p (s g) -> p s g", s=2)
        tot = sb("tot", 4)[0].rearrange("p (s g) -> p s g", s=2)
        rinv = sb("rinv", 4)[0].rearrange("p (s g) -> p s g", s=2)

        ps = ctx.enter_context(nc.psum_tensor("ps", [P, 8 * 512], F32))

        def bank(n, lo=0, hi=512):
            return ps[:, 512 * n + lo:512 * n + hi]

        bias_rows = nc.dram_tensor("bias_rows", [P, HS, TOE], F32)

        const_in, toe_in, x_in, mem_in = sem("const_in"), sem("toe_in"), sem("x_in"), sem("mem_in")
        raw_in = [sem("raw_in0"), sem("raw_in1")]
        w_hi_done, w_lo_done = sem("w_hi_done"), sem("w_lo_done")
        tile_ready = sem("tile_ready")
        tile_done = [sem("tile_done0"), sem("tile_done1")]
        tile_hi = sem("tile_hi")
        tp_ready, tp_hi, tp_lo = sem("tp_ready"), sem("tp_hi"), sem("tp_lo")
        sq_done, ms_done, rstd_done, xn_done = sem("sq_done"), sem("ms_done"), sem("rstd_done"), sem("xn_done")
        s_ready, mx_done, neg_done, exp_done = sem("s_ready"), sem("mx_done"), sem("neg_done"), sem("exp_done")
        nsk_done, tot_done, rinv_done, p_done = sem("nsk_done"), sem("tot_done"), sem("rinv_done"), sem("p_done")
        t_ready, pt_hi_done, pt_lo_done = sem("t_ready"), sem("pt_hi_done"), sem("pt_lo_done")
        o_ready, o_hi_done, o_lo_done = sem("o_ready"), sem("o_hi_done"), sem("o_lo_done")
        fbank_ready, frep_done, rows_out, bias_in = sem("fbank_ready"), sem("frep_done"), sem("rows_out"), sem("bias_in")
        idr_done, small_done, nhalf_done = sem("idr_done"), sem("small_done"), sem("nhalf_done")
        bias_hi_done, bias_lo_done, kz_zero = sem("bias_hi_done"), sem("bias_lo_done"), sem("kz_zero")
        pre_ready, pre_copied, kr_step = sem("pre_ready"), sem("pre_copied"), sem("kr_step")
        rope_step = sem("rope_step")
        y_done, x_again = sem("y_done"), sem("x_again")
        s_hi_done, s_lo_done, acc_step, added = sem("s_hi_done"), sem("s_lo_done"), sem("acc_step"), sem("added")
        relu_done, sq_act, fgain_in, out_ready, out_done = (
            sem("relu_done"), sem("sq_act"), sem("fgain_in"), sem("out_ready"), sem("out_done"))

        win = w_in[0].rearrange("(k p) n -> p k n", p=P)
        wmk = w_mem_kv[0].rearrange("(k p) n -> p k n", p=P)
        wuq = w_uq[0].rearrange("(k p) n -> p k n", p=P)
        wup = w_up[0].rearrange("(k p) n -> p k n", p=P)
        wdn = w_down[0].rearrange("(k p) n -> p k n", p=P)
        wou = w_out[0].rearrange("(k p) n -> p k n", p=P)
        wo = {MLA: w_o_mla[0].rearrange("(k p) n -> p k n", p=P),
              MEM: w_o_mem[0].rearrange("(k p) n -> p k n", p=P)}
        wo_s = w_o_swa[0].rearrange("(g r d) n -> g d r n", g=2, r=PAIRS)
        xv = x[0].rearrange("(t p) n -> t p n", p=P)
        mv = mem[0].rearrange("(t p) n -> t p n", p=P)
        ov = out[0].rearrange("(t p) n -> t p n", p=P)

        def col(v):
            return v.rearrange("(k p) -> p k", p=P)

        def row(v, n):
            return bass.AP(v.tensor, v.offset, [[0, P], [1, n]])

        block = ctx.enter_context(nc.Block())

        @block.sync
        def _(sp):
            def small(dst, src):
                sp.dma_start(dst, src).then_inc(const_in, 16)

            def fetch(c, per, i, pieces):
                slot, _ = ring(c, per, i)
                wait(sp, w_lo_done, c - 1 + per * i)
                found = pieces(raw[:, slot, :])
                for (dst, src), share in zip(found, SHARES[len(found)]):
                    sp.dma_start(dst, src).then_inc(raw_in[slot], share)

            def cols(r, at, view, c0, n, k=KD):
                return r[:, at:at + k * n].rearrange("p (k c) -> p k c", k=k), view[:, :, ds(c0, n)]

            def gate_cols(r, at, branch, m):
                return cols(r, at, win, COL_G + branch * D + P * m, P)

            def fetch_wo(branch, b):
                for half in range(2):
                    c0 = half * 512
                    if branch == SWA:
                        fetch(b + half, 0, 0, lambda r: [
                            (r[64 * g:64 * g + 64, :].rearrange("p (k c) -> p k c", k=4),
                             wo_s[g][:, :, c0:c0 + 512]) for g in range(2)])
                    else:
                        fetch(b + half, 0, 0, lambda r: [cols(r, 0, wo[branch], c0, 512, 4)])

            sp.dma_start(con, consts).then_inc(toe_in, 16)
            sp.dma_start(toe, toeplitz).then_inc(toe_in, 16)
            sp.dma_start(rel[0:BUCKETS, :], rel_bias).then_inc(toe_in, 16)
            for t in range(QT):
                sp.dma_start(x_sb[:, t, :], xv[t]).then_inc(x_in, 16)
            with nc.allow_non_contiguous_dma(reason="gains as columns: a few KiB in all"):
                small(g_attn, col(attn_norm[0]))
                for t in range(2):
                    sp.dma_start(mem_sb[:, t, :], mv[t]).then_inc(mem_in, 16)
                small(g_mem, col(mem_norm[0]))
                small(hb_raw, col(b_gate[0]))
                small(sinks, row(attn_sinks[0], HS))
                small(g_mlp, col(mlp_norm[0]))
                small(g_q, col(mla_q_norm[0]))
                small(g_kv, col(mla_kv_norm[0]))
            for h in range(HM):
                b = B_MEM + 3 * h
                fetch(b, 0, 0, lambda r: [cols(r, 0, win, COL_QM + DM * h, P), cols(r, 1024, wmk, DM * h, P)])
                fetch(b + 1, 0, 0, lambda r: [cols(r, 0, wmk, HM * DM + DM * h, P),
                                              gate_cols(r, 1024, MEM, 2 * h)])
                fetch(b + 2, 0, 0, lambda r: [gate_cols(r, 0, MEM, 2 * h + 1)])
                if h == 0:
                    sp.wait_ge(frep_done, HS)
                    sp.dma_start(bias_rows.ap(), frep).then_inc(rows_out, 16)
                    sp.wait_ge(rows_out, 16)
                    sp.dma_start(bias_raw.rearrange("p (h n) -> p h n", h=HS),
                                 bass.AP(bias_rows, P - 1, [[HS * TOE - 1, P], [TOE, HS], [1, 2 * P]])
                                 ).then_inc(bias_in, 16)
            fetch(B_KVS, 0, 0, lambda r: [cols(r, 0, win, COL_KS, P), cols(r, 1024, win, COL_KS + P, P)])
            fetch_wo(MEM, B_WO_MEM)
            with sp.Fori(0, PAIRS // 2) as i:
                for c in range(2):
                    fetch(B_SWA + 2 * c, 4, i, lambda r: [
                        (r[:, 0:1024].rearrange("p (k c) -> p k c", k=KD)[:, :, 64 * g:64 * g + 64],
                         win[:, :, ds(COL_QS + 256 * g + 64 * c + 128 * i, 64)]) for g in range(2)
                    ] + [gate_cols(r, 1024, SWA, 4 * i + 2 * c)])
                    fetch(B_SWA + 2 * c + 1, 4, i, lambda r: [gate_cols(r, 0, SWA, 4 * i + 2 * c + 1)])
            for half in range(2):
                fetch(B_MLAP + half, 0, 0, lambda r: [
                    (r[:, 0:4 * 416].rearrange("p (k c) -> p k c", k=4), win[:, 4 * half:4 * half + 4, 0:416])])
            fetch_wo(SWA, B_WO_SWA)
            with sp.Fori(0, HA // 2) as i:
                fetch(B_MLA, 2, i, lambda r: [cols(r, 0, wuq, 2 * QK * i, QK, 2),
                                              (r[:, 192:448], w_ukv[0][:, ds(256 * i, 256)]),
                                              gate_cols(r, 448, MLA, 2 * i)])
                fetch(B_MLA + 1, 2, i, lambda r: [cols(r, 0, wuq, 2 * QK * i + QK, QK, 2),
                                                  gate_cols(r, 448, MLA, 2 * i + 1)])
            fetch_wo(MLA, B_WO_MLA)
            sp.wait_ge(y_done, 2 * KD)
            for t in range(QT):
                sp.dma_start(x_sb[:, t, :], xv[t]).then_inc(x_again, 16)
            sp.dma_start(fgain, row(final_norm, D)).then_inc(fgain_in, 16)

            def rows(view, k):
                return lambda r: [(r.rearrange("p (k c) -> p k c", k=2), view[:, ds(k, 2), :])]

            with sp.Fori(0, D // 512) as i:
                for c in range(2):
                    fetch(B_WOUT + c, 2, i, rows(wou, 4 * i + 2 * c))
            with sp.Fori(0, FF // 512) as i:
                for c in range(2):
                    fetch(B_UP + c, 2, i, lambda r: [cols(r, 0, wup, 512 * i + 256 * c, 256)])
            with sp.Fori(0, FF // 512) as i:
                for c in range(2):
                    fetch(B_DOWN + c, 2, i, rows(wdn, 4 * i + 2 * c))
            for t in range(QT):
                sp.wait_ge(out_ready, t + 1)
                sp.dma_start(ov[t], x_sb[:, t, :]).then_inc(out_done, 16)
            sp.wait_ge(out_done, 16 * QT)

        BATCHES = [(0, 4), (4, 6), (6, 14)] + [(14 + t, 15 + t) for t in range(2 * QT)]

        def w(buf, slot, at, k, n, c0=0, cn=P):
            return buf[:, slot, at + k * n + c0:at + k * n + c0 + cn]

        @block.gpsimd
        def _(pool):
            pool.memset(half_neg, -0.5).then_inc(nhalf_done, 1)
            pool.memset(kpad, 0.0).then_inc(nhalf_done, 1)
            pool.wait_ge(nhalf_done, 1)

            def rsqrt(n):
                a, b = BATCHES[n]
                pool.wait_ge(ms_done, n + 1 if n < 2 else n + 2)
                pool.tensor_tensor(rstd[:, a:b], rstd[:, a:b], half_neg[:, 0:b - a],
                                   ALU.pow).then_inc(rstd_done, 1)

            rsqrt(0)
            rsqrt(1)
            pool.wait_ge(tile_ready, T_KVS + 1)
            for buf in (kz_hi, kz_lo):
                pool.memset(buf[64:128, 0, :].bitcast(F32), 0.0).then_inc(kz_zero, 1)
                pool.memset(buf[0:64, 1, :].bitcast(F32), 0.0).then_inc(kz_zero, 1)
            for n in range(2, len(BATCHES)):
                rsqrt(n)

        @block.scalar
        def _(act):
            def split(c, per=0, i=0):
                slot, turn = ring(c, per, i)
                act.wait_ge(raw_in[slot], 48 * (turn + 1))
                act.activation(w_hi[:, slot, :], raw[:, slot, :], ACT.Copy).then_inc(w_hi_done, 1)

            def ready(c, per=0, i=0):
                act.wait_ge(tile_ready, c + 1 + per * i)
                return c % 2

            def square(n, src):
                wait(act, sq_done, n)
                act.activation(junk[:, 0:src.shape[-1]], src, ACT.Square,
                               accum_out=sumsq[:, n:n + 1]).then_inc(sq_done, 1)

            def tp_part(g, dst, src, gain):
                act.wait_ge(tp_ready, g + 1)
                act.activation(dst, src, ACT.Copy, scale=gain).then_inc(tp_hi, 1)

            def tanh(m, branch, c, per=0, i=0):
                bk = ready(c, per, i)
                act.activation(gate[:, ds(m, 1), :], bank(bk).rearrange("p (m n) -> p m n", m=1), ACT.Tanh,
                               bias=hb[:, ds(branch * KD + m, 1)], scale=0.5).then_inc(tile_done[bk], 1)

            def exps(u, per, i, groups, n, scale, sink=False):
                s = u % 2
                act.wait_ge(neg_done, u + 1 + per * i)
                if sink:
                    act.activation(esnk[:, s, :], snk[:, s, :], ACT.Exp)
                for g in range(groups):
                    last = act.activation(probs[:, s, g * n:(g + 1) * n], bank(2 + s, g * n, (g + 1) * n), ACT.Exp,
                                          bias=negm[:, s, g:g + 1], scale=scale, accum_out=rsum[:, s, g:g + 1])
                last.then_inc(exp_done, 1)

            def pt(u, per, i, dst, src):
                act.wait_ge(t_ready, u + 1 + per * i)
                act.activation(dst, src, ACT.Copy).then_inc(pt_hi_done, 1)

            act.wait_ge(toe_in, 48)
            act.activation(ident_r, ident, ACT.Copy).then_inc(idr_done, 1)
            act.activation(mask_r, con[:, C_MASK:C_MASK + P], ACT.Copy).then_inc(idr_done, 1)
            for t in range(QT):
                act.wait_ge(x_in, 16 * QT)
                square(t, x_sb[:, t, :])
            split(0)
            act.wait_ge(mem_in, 32)
            for t in range(2):
                square(QT + t, mem_sb[:, t, :])
            act.wait_ge(const_in, 16 * 7)
            for k in range(KD):
                tp_part(G_X + k, h_hi[:, k, :], bank(k), g_attn[:, k:k + 1])
            split(1)
            for k in range(KD):
                tp_part(G_MEM + k, mn_hi[:, k, :], bank(k, 0, M), g_mem[:, k:k + 1])
            act.wait_ge(small_done, 1)

            for h in range(HM):
                t0, u0, b = T_MEM + 5 * h, U_MEM + 2 * h, B_MEM + 3 * h
                bk = ready(t0)
                act.activation(q_hi[:, h % 2, :], bank(bk), ACT.Copy).then_inc(tile_hi, 1)
                bk = ready(t0 + 1)
                act.activation(km_hi, bank(bk, 0, M), ACT.Copy).then_inc(tile_hi, 1)
                split(b + 2)
                bk = ready(t0 + 2)
                act.activation(v_hi[:, 0:2, :], bank(bk, 0, M).rearrange("p (k n) -> p k n", k=2),
                               ACT.Copy).then_inc(tile_hi, 1)
                tanh(2 * h, MEM, t0 + 3)
                exps(u0, 0, 0, 2, M, DM ** -0.5)
                exps(u0 + 1, 0, 0, 2, M, DM ** -0.5)
                split(b + 3)
                for n in range(2):
                    pt(u0 + n, 0, 0, pt_hi[:, 512 * n:512 * n + 512], bank(4 + n))
                tanh(2 * h + 1, MEM, t0 + 4)
                split(b + 4)
                act.wait_ge(o_ready, E_MEM + h + 1)
                act.activation(o_hi[:, h, :], bank(6 + h % 2), ACT.Copy).then_inc(o_hi_done, 1)

            bk = ready(T_KVS)
            act.activation(kz_hi[0:64, 0, :], bank(bk)[0:64, :], ACT.Copy)
            act.activation(kz_hi[64:128, 1, :], bank(bk)[64:128, :], ACT.Copy).then_inc(tile_hi, 1)
            bk = ready(T_KVS + 1)
            act.activation(v_hi, bank(bk).rearrange("p (k n) -> p k n", k=4), ACT.Copy).then_inc(tile_hi, 1)
            split(B_KVS + 2)
            act.wait_ge(bias_in, 16)
            act.activation(bias_hi, bias_raw.rearrange("p (g r n) -> p g r n", g=2, r=PAIRS),
                           ACT.Copy).then_inc(bias_hi_done, 1)
            ready(T_WO_MEM + 3)
            split(B_WO_MEM + 2)
            ready(T_WO_MEM + 7)
            split(B_WO_MEM + 3)
            for slot in range(2):
                act.wait_ge(tile_done[slot], (T_WO_MEM + KD) // 2)

            with act.Fori(0, PAIRS // 2) as i:
                for c in range(2):
                    t0, u0, b = T_SWA + 3 * c, U_SWA + 4 * c, B_SWA + 2 * c
                    bk = ready(t0, 6, i)
                    act.activation(q_hi[:, c, :], bank(bk), ACT.Copy).then_inc(tile_hi, 1)
                    tanh(2 * c + 4 * i, SWA, t0 + 1, 6, i)

                    def e(n):
                        exps(u0 + n, 8, i, 2, P if n == 0 else 2 * P, DS ** -0.5, True)

                    def p(n):
                        lo = 256 if n == 0 else 0
                        pt(u0 + n, 8, i, pt_hi[:, 512 * n + lo:512 * n + 512], bank(4 + n % 2, lo, 512))

                    e(0)
                    e(1)
                    split(b + 2, 4, i)
                    p(0)
                    e(2)
                    p(1)
                    e(3)
                    p(2)
                    p(3)
                    tanh(2 * c + 1 + 4 * i, SWA, t0 + 2, 6, i)
                    split(b + 3, 4, i)
                    act.wait_ge(o_ready, E_SWA + c + 1 + 2 * i)
                    for g in range(2):
                        r = slice(64 * g, 64 * g + 64)
                        last = act.activation(o_hi[r, ds(2 * i + c, 1), :],
                                              bank(6 + g)[r, :].rearrange("p (m n) -> p m n", m=1), ACT.Copy)
                    last.then_inc(o_hi_done, 1)

            act.wait_ge(pre_ready, 1)
            split(B_MLAP + 2)
            act.wait_ge(bias_lo_done, 1)
            for t in range(QT):
                act.wait_ge(pre_ready, t + 2)
                act.activation(kvq[:, t, :], bank(2 + t, 0, 416), ACT.Copy).then_inc(pre_copied, 1)
            split(B_MLAP + 3)
            act.wait_ge(pre_copied, QT)
            for t in range(QT):
                square(6 + t, kvq[:, t, 0:QL])
            for t in range(QT):
                square(10 + t, kvq[:, t, QL:QL + KVL])
            ready(T_WO_SWA + 3)
            split(B_WO_SWA + 2)
            ready(T_WO_SWA + 7)
            split(B_WO_SWA + 3)
            for k in range(2):
                tp_part(G_MLA + k, cq_hi[:, k, :], bank(2 + k), g_q[:, k:k + 1])
            tp_part(G_MLA + 2, ckv_hi, bank(4), g_kv[:, 0:1])
            act.wait_ge(tp_ready, G_MLA + 4)
            act.activation(ka_hi[64:96, 0, :], bank(5)[64:96, :], ACT.Copy)
            act.activation(ka_hi[64:96, 1, :], bank(5)[64:96, :], ACT.Copy).then_inc(tp_hi, 1)
            act.wait_ge(y_done, KD)

            with act.Fori(0, HA // 2) as i:
                t0, u0, b = T_MLA, U_MLA, B_MLA
                for n in range(2):
                    bk = ready(t0 + n, 8, i)
                    act.activation(v_hi[:, 2 * n:2 * n + 2, :], bank(bk, 0, 256).rearrange("p (k n) -> p k n", k=2),
                                   ACT.Copy).then_inc(tile_hi, 1)
                for c in range(2):
                    bk = ready(t0 + 2 + c, 8, i)
                    act.activation(ka_hi[0:64, c, :], bank(bk)[0:64, :], ACT.Copy).then_inc(tile_hi, 1)

                def query(c):
                    bk = ready(t0 + 4 + 2 * c, 8, i)
                    act.activation(q_hi[0:64, c, :], bank(bk)[0:64, :], ACT.Copy).then_inc(tile_hi, 1)
                    act.wait_ge(rope_step, 3 * (c + 1) + 6 * i)
                    act.activation(q_hi[64:96, c, :], rope_b[64:96, :], ACT.Copy).then_inc(tile_hi, 1)

                def e(c, n):
                    exps(u0 + 4 * c + n, 8, i, 1, P * (n + 1), QK ** -0.5)

                def p(c, n):
                    pt(u0 + 4 * c + n, 8, i,
                       pt_hi.rearrange("p (k q) -> p k q", k=4)[:, 0:n + 1, P * n:P * n + P],
                       bank(4 + n % 2, 0, P * (n + 1)).rearrange("p (k q) -> p k q", q=P))

                def o(c):
                    r = slice(64 * c, 64 * c + 64)
                    act.wait_ge(o_ready, E_MLA + c + 1 + 2 * i)
                    act.activation(o_hi[r, ds(i, 1), :], bank(6 + c)[r, :].rearrange("p (m n) -> p m n", m=1),
                                   ACT.Copy).then_inc(o_hi_done, 1)

                query(0)
                e(0, 0)
                e(0, 1)
                tanh(2 * i, MLA, t0 + 5, 8, i)
                split(b + 2, 2, i)
                query(1)
                p(0, 0)
                e(0, 2)
                p(0, 1)
                e(0, 3)
                p(0, 2)
                e(1, 0)
                p(0, 3)
                e(1, 1)
                o(0)
                p(1, 0)
                e(1, 2)
                p(1, 1)
                e(1, 3)
                p(1, 2)
                p(1, 3)
                tanh(2 * i + 1, MLA, t0 + 7, 8, i)
                split(b + 3, 2, i)
                o(1)

            def split_s(n, ring_hi, src, scale, c=0, per=0, i=0):
                act.activation(ring_hi[:, c % 2, :], src[:, ds(1024 * n, 1024)], ACT.Copy,
                               scale=scale).then_inc(s_hi_done, 1)

            ready(T_WO_MLA + 3)
            split(B_WO_MLA + 2)
            ready(T_WO_MLA + 7)
            split(B_WO_MLA + 3)
            act.wait_ge(y_done, 2 * KD)
            for n in range(2):
                split_s(n, yr_hi, ybuf, 0.5, n)
            for n in range(4):
                act.wait_ge(acc_step, 4 * (n + 1))
                if n < 2:
                    split_s(n + 2, yr_hi, ybuf, 0.5, n)
                split(B_WOUT + n + 2)
            for t in range(QT):
                act.wait_ge(added, t + 1)
                square(14 + t, x_sb[:, t, :])
            for k in range(KD):
                tp_part(G_H2 + k, h_hi[:, k, :], bank(k), g_mlp[:, k:k + 1])

            def up(i):
                for c in range(4):
                    slot, turn = ring(T_UP + c, 4, i)
                    ready(T_UP + c, 4, i)
                    wait(act, sq_act, c - 1 + 4 * i)
                    act.activation(relu[:, c % 2, :], bank(slot), ACT.Relu).then_inc(tile_done[slot], 1)
                    if c % 2:
                        split(B_UP + 2 + c // 2, 2, i)

            up(0)
            with act.Fori(1, FF // 512 - 1) as i:
                up(i)
            act.wait_ge(tp_ready, G_H2 + KD)
            for n in range(2):
                act.wait_ge(sq_act, 2 * n + 2)
                split_s(n, ar_hi, act_sq, 1.0, n)
            up(FF // 512 - 1)
            act.wait_ge(sq_act, FF // P)
            with act.Fori(0, FF // 512 - 1) as i:
                for c in range(2):
                    act.wait_ge(acc_step, 16 + 4 * (c + 1) + 8 * i)
                    split_s(2 * i + c + 2, ar_hi, act_sq, 1.0, c)
                    split(B_DOWN + 2 + c, 2, i)
            for t in range(QT):
                act.wait_ge(added, QT + t + 1)
                square(14 + QT + t, x_sb[:, t, :])

        @block.vector
        def _(dve):
            def f(ap):
                return ap.bitcast(F32)

            def split(c, per=0, i=0):
                slot, _ = ring(c, per, i)
                dve.wait_ge(w_hi_done, c + 1 + per * i)
                dve.tensor_tensor(w_lo[:, slot, :], raw[:, slot, :], f(w_hi[:, slot, :]),
                                  ALU.subtract).then_inc(w_lo_done, 1)

            def lo(n, per, i, dst, src, hi, bk):
                dve.wait_ge(tile_hi, n + 1 + per * i)
                dve.tensor_tensor(dst, src, f(hi), ALU.subtract).then_inc(tile_done[bk], 1)

            def tp_part(g, dst, src, gain, hi):
                dve.wait_ge(tp_hi, g + 1)
                dve.scalar_tensor_tensor(dst, src, gain, f(hi), ALU.mult, ALU.subtract).then_inc(tp_lo, 1)

            def mean_sq(n_sq, a, b, width, n_ms):
                dve.wait_ge(sq_done, n_sq)
                dve.tensor_scalar(rstd[:, a:b], sumsq[:, a:b], 1.0 / width, EPS, ALU.mult,
                                  ALU.add).then_inc(ms_done, 1)

            def peak(u, per, i, groups, n, scale, r=None):
                s = u % 2
                dve.wait_ge(s_ready, u + 1 + per * i)
                dve.tensor_reduce(mx[:, s, 0:groups], bank(2 + s, 0, groups * n).rearrange("p (g n) -> p g n", n=n),
                                  AX_X, ALU.max).then_inc(mx_done, 1)
                dve.wait_ge(mx_done, u + 1 + per * i)
                if r is None:
                    dve.tensor_scalar(negm[:, s, 0:groups], mx[:, s, 0:groups], -scale, None,
                                      ALU.mult).then_inc(neg_done, 1)
                    return
                sink = nsinks[:, :, ds(r, 1)]
                dve.scalar_tensor_tensor(negm[:, s:s + 1, :].rearrange("p a g -> p g a"),
                                         mx[:, s:s + 1, :].rearrange("p a g -> p g a"), -scale, sink,
                                         ALU.mult, ALU.min).then_inc(nsk_done, 1)
                dve.wait_ge(nsk_done, u - U_SWA + 1 + per * i)
                dve.tensor_tensor(snk[:, s:s + 1, :].rearrange("p a g -> p g a"),
                                  negm[:, s:s + 1, :].rearrange("p a g -> p g a"), sink,
                                  ALU.subtract).then_inc(neg_done, 1)

            def norm(u, per, i, groups, n, sink=False):
                s = u % 2
                dve.wait_ge(exp_done, u + 1 + per * i)
                den = rsum
                if sink:
                    dve.tensor_tensor(tot[:, s, :], rsum[:, s, :], esnk[:, s, :], ALU.add).then_inc(tot_done, 1)
                    dve.wait_ge(tot_done, u - U_SWA + 1 + per * i)
                    den = tot
                dve.reciprocal(rinv[:, s, 0:groups], den[:, s, 0:groups]).then_inc(rinv_done, 1)
                dve.wait_ge(rinv_done, u + 1 + per * i)
                for g in range(groups):
                    block_p = probs[:, s, g * n:(g + 1) * n]
                    last = dve.tensor_scalar(block_p, block_p, rinv[:, s, g:g + 1], None, ALU.mult)
                last.then_inc(p_done, 1)

            def pt(u, per, i, dst, src, hi):
                dve.wait_ge(pt_hi_done, u + 1 + per * i)
                dve.tensor_tensor(dst, src, f(hi), ALU.subtract).then_inc(pt_lo_done, 1)

            def merge(t0, first):
                for m in range(KD):
                    slot, turn = ring(t0 + m, 0, 0)
                    dve.wait_ge(tile_ready, t0 + m + 1)
                    if first:
                        dve.scalar_tensor_tensor(y[:, m, :], gate[:, m, :], 1.0, bank(slot), ALU.add,
                                                 ALU.mult).then_inc(tile_done[slot], 1)
                        continue
                    dve.scalar_tensor_tensor(tmp[:, m % 2, :], gate[:, m, :], 1.0, bank(slot), ALU.add,
                                             ALU.mult).then_inc(tile_done[slot], 1)
                    dve.wait_ge(tile_done[slot], turn + 1)
                    dve.tensor_tensor(y[:, m, :], y[:, m, :], tmp[:, m % 2, :], ALU.add).then_inc(y_done, 1)

            for h in range(HS):
                dve.wait_ge(fbank_ready, h + 1)
                dve.scalar_tensor_tensor(frep[:, h, :], bank(h, 0, TOE), DS ** 0.5, toe[:, TOE:2 * TOE],
                                         ALU.mult, ALU.add).then_inc(frep_done, 1)
            mean_sq(4, 0, 4, D, 1)
            dve.wait_ge(rstd_done, 1)
            for t in range(QT):
                dve.tensor_scalar(x_sb[:, t, :], x_sb[:, t, :], rstd[:, t:t + 1], None,
                                  ALU.mult).then_inc(xn_done, 1)
            split(0)
            mean_sq(6, 4, 6, D, 2)
            dve.wait_ge(rstd_done, 2)
            for t in range(2):
                dve.tensor_scalar(mem_sb[:, t, :], mem_sb[:, t, :], rstd[:, 4 + t:5 + t], None,
                                  ALU.mult).then_inc(xn_done, 1)
            dve.wait_ge(const_in, 16 * 7)
            dve.tensor_scalar(hb, hb_raw, 0.5, None, ALU.mult).then_inc(small_done, 1)
            dve.tensor_scalar(nsinks, sinks.rearrange("p (g r) -> p g r", g=2), -1.0, None,
                              ALU.mult).then_inc(small_done, 1)
            dve.wait_ge(small_done, 2)
            for k in range(KD):
                tp_part(G_X + k, h_lo[:, k, :], bank(k), g_attn[:, k:k + 1], h_hi[:, k, :])
            split(1)
            for k in range(KD):
                tp_part(G_MEM + k, mn_lo[:, k, :], bank(k, 0, M), g_mem[:, k:k + 1], mn_hi[:, k, :])

            for h in range(HM):
                t0, u0, b, n0 = T_MEM + 5 * h, U_MEM + 2 * h, B_MEM + 3 * h, H_MEM + 3 * h
                lo(n0, 0, 0, q_lo[:, h % 2, :], bank(t0 % 2), q_hi[:, h % 2, :], t0 % 2)
                lo(n0 + 1, 0, 0, km_lo, bank((t0 + 1) % 2, 0, M), km_hi, (t0 + 1) % 2)
                split(b + 2)
                lo(n0 + 2, 0, 0, v_lo[:, 0:2, :], bank(t0 % 2, 0, M).rearrange("p (k n) -> p k n", k=2),
                   v_hi[:, 0:2, :], t0 % 2)
                for n in range(2):
                    peak(u0 + n, 0, 0, 2, M, DM ** -0.5)
                for n in range(2):
                    norm(u0 + n, 0, 0, 2, M)
                split(b + 3)
                for n in range(2):
                    at = slice(512 * n, 512 * n + 512)
                    pt(u0 + n, 0, 0, pt_lo[:, at], bank(4 + n), pt_hi[:, at])
                split(b + 4)
                dve.wait_ge(o_hi_done, E_MEM + h + 1)
                dve.tensor_tensor(o_lo[:, h, :], bank(6 + h % 2), f(o_hi[:, h, :]),
                                  ALU.subtract).then_inc(o_lo_done, 1)

            bk = T_KVS % 2
            dve.wait_ge(tile_hi, H_KVS + 1)
            dve.tensor_tensor(kz_lo[0:64, 0, :], bank(bk)[0:64, :], f(kz_hi[0:64, 0, :]), ALU.subtract)
            dve.tensor_tensor(kz_lo[64:128, 1, :], bank(bk)[64:128, :], f(kz_hi[64:128, 1, :]),
                              ALU.subtract).then_inc(tile_done[bk], 1)
            bk = (T_KVS + 1) % 2
            lo(H_KVS + 1, 0, 0, v_lo, bank(bk).rearrange("p (k n) -> p k n", k=4), v_hi, bk)
            split(B_KVS + 2)
            dve.wait_ge(bias_hi_done, 1)
            dve.tensor_tensor(bias_lo, bias_raw.rearrange("p (g r n) -> p g r n", g=2, r=PAIRS), f(bias_hi),
                              ALU.subtract).then_inc(bias_lo_done, 1)
            dve.wait_ge(rows_out, 16)
            merge(T_WO_MEM, True)
            split(B_WO_MEM + 2)
            split(B_WO_MEM + 3)

            with dve.Fori(0, PAIRS // 2) as i:
                for c in range(2):
                    t0, u0, b = T_SWA + 3 * c, U_SWA + 4 * c, B_SWA + 2 * c
                    lo(H_SWA + c, 2, i, q_lo[:, c, :], bank(t0 % 2), q_hi[:, c, :], t0 % 2)

                    def pk(n):
                        peak(u0 + n, 8, i, 2, P if n == 0 else 2 * P, DS ** -0.5, 2 * i + c)

                    def nm(n):
                        norm(u0 + n, 8, i, 2, P if n == 0 else 2 * P, True)

                    def p(n):
                        z = 256 if n == 0 else 0
                        at = slice(512 * n + z, 512 * n + 512)
                        pt(u0 + n, 8, i, pt_lo[:, at], bank(4 + n % 2, z, 512), pt_hi[:, at])

                    pk(0)
                    pk(1)
                    nm(0)
                    nm(1)
                    split(b + 2, 4, i)
                    p(0)
                    pk(2)
                    nm(2)
                    p(1)
                    pk(3)
                    nm(3)
                    p(2)
                    p(3)
                    split(b + 3, 4, i)
                    dve.wait_ge(o_hi_done, E_SWA + c + 1 + 2 * i)
                    for g in range(2):
                        r = slice(64 * g, 64 * g + 64)
                        last = dve.tensor_tensor(o_lo[r, ds(2 * i + c, 1), :],
                                                 bank(6 + g)[r, :].rearrange("p (m n) -> p m n", m=1),
                                                 f(o_hi[r, ds(2 * i + c, 1), :]), ALU.subtract)
                    last.then_inc(o_lo_done, 1)

            split(B_MLAP + 2)
            split(B_MLAP + 3)
            dve.wait_ge(pre_copied, QT)
            t1, t2 = kvq[:, :, 384:400], kvq[:, :, 400:416]
            for n, (a, b) in enumerate(((t1, cos_t), (t2, sin_t), (t2, cos_t), (t1, sin_t))):
                dve.tensor_tensor(rtmp[:, n, :, :], a, b, ALU.mult).then_inc(kr_step, 1)
            dve.wait_ge(kr_step, 4)
            dve.wait_ge(nhalf_done, 2)
            dve.tensor_tensor(kpad[:, :, 64:80], rtmp[:, 0, :, :], rtmp[:, 1, :, :], ALU.subtract).then_inc(kr_step, 1)
            dve.tensor_tensor(kpad[:, :, 80:96], rtmp[:, 2, :, :], rtmp[:, 3, :, :], ALU.add).then_inc(kr_step, 1)
            mean_sq(10, 6, 10, QL, 3)
            mean_sq(14, 10, 14, KVL, 4)
            dve.wait_ge(rstd_done, 3)
            for t in range(QT):
                for n, (a, b) in enumerate(((0, QL), (QL, QL + KVL))):
                    dve.tensor_scalar(kvq[:, t, a:b], kvq[:, t, a:b], rstd[:, 6 + 4 * n + t:7 + 4 * n + t], None,
                                      ALU.mult).then_inc(xn_done, 1)
            merge(T_WO_SWA, False)
            split(B_WO_SWA + 2)
            split(B_WO_SWA + 3)
            for k in range(2):
                tp_part(G_MLA + k, cq_lo[:, k, :], bank(2 + k), g_q[:, k:k + 1], cq_hi[:, k, :])
            tp_part(G_MLA + 2, ckv_lo, bank(4), g_kv[:, 0:1], ckv_hi)
            dve.wait_ge(tp_hi, G_MLA + 4)
            for c in range(2):
                last = dve.tensor_tensor(ka_lo[64:96, c, :], bank(5)[64:96, :], f(ka_hi[64:96, c, :]), ALU.subtract)
            last.then_inc(tp_lo, 1)

            with dve.Fori(0, HA // 2) as i:
                t0, u0, b, n0 = T_MLA, U_MLA, B_MLA, H_MLA
                for n in range(2):
                    bk = (t0 + n) % 2
                    lo(n0 + n, 8, i, v_lo[:, 2 * n:2 * n + 2, :],
                       bank(bk, 0, 256).rearrange("p (k n) -> p k n", k=2), v_hi[:, 2 * n:2 * n + 2, :], bk)
                for c in range(2):
                    bk = (t0 + 2 + c) % 2
                    lo(n0 + 2 + c, 8, i, ka_lo[0:64, c, :], bank(bk)[0:64, :], ka_hi[0:64, c, :], bk)

                def query(c):
                    bk = (t0 + 4 + 2 * c) % 2
                    dve.wait_ge(tile_hi, n0 + 5 + 2 * c + 8 * i)
                    dve.tensor_tensor(q_lo[0:64, c, :], bank(bk)[0:64, :], f(q_hi[0:64, c, :]), ALU.subtract)
                    dve.stream_shuffle(rope_a[64:96, :], bank(bk)[64:96, :],
                                       [(p + 16) % 32 for p in range(32)]).then_inc(rope_step, 1)
                    dve.tensor_tensor(rope_b[64:96, :], bank(bk)[64:96, :], cos_f[64:96, :], ALU.mult)
                    dve.wait_ge(rope_step, 3 * c + 1 + 6 * i)
                    dve.tensor_tensor(rope_a[64:96, :], rope_a[64:96, :], sin_f[64:96, :],
                                      ALU.mult).then_inc(rope_step, 1)
                    dve.wait_ge(rope_step, 3 * c + 2 + 6 * i)
                    dve.tensor_tensor(rope_b[64:96, :], rope_b[64:96, :], rope_a[64:96, :],
                                      ALU.add).then_inc(rope_step, 1)
                    lo(n0 + 5 + 2 * c, 8, i, q_lo[64:96, c, :], rope_b[64:96, :], q_hi[64:96, c, :], bk)

                def pk(c, n):
                    peak(u0 + 4 * c + n, 8, i, 1, P * (n + 1), QK ** -0.5)

                def nm(c, n):
                    norm(u0 + 4 * c + n, 8, i, 1, P * (n + 1))

                def p(c, n):
                    at = (slice(None), slice(0, n + 1), slice(P * n, P * n + P))
                    pt(u0 + 4 * c + n, 8, i, pt_lo.rearrange("p (k q) -> p k q", k=4)[at],
                       bank(4 + n % 2, 0, P * (n + 1)).rearrange("p (k q) -> p k q", q=P),
                       pt_hi.rearrange("p (k q) -> p k q", k=4)[at])

                def o(c):
                    r = slice(64 * c, 64 * c + 64)
                    dve.wait_ge(o_hi_done, E_MLA + c + 1 + 2 * i)
                    dve.tensor_tensor(o_lo[r, ds(i, 1), :], bank(6 + c)[r, :].rearrange("p (m n) -> p m n", m=1),
                                      f(o_hi[r, ds(i, 1), :]), ALU.subtract).then_inc(o_lo_done, 1)

                query(0)
                pk(0, 0)
                pk(0, 1)
                nm(0, 0)
                nm(0, 1)
                split(b + 2, 2, i)
                query(1)
                p(0, 0)
                pk(0, 2)
                nm(0, 2)
                p(0, 1)
                pk(0, 3)
                nm(0, 3)
                p(0, 2)
                pk(1, 0)
                nm(1, 0)
                p(0, 3)
                pk(1, 1)
                nm(1, 1)
                o(0)
                p(1, 0)
                pk(1, 2)
                nm(1, 2)
                p(1, 1)
                pk(1, 3)
                nm(1, 3)
                p(1, 2)
                p(1, 3)
                split(b + 3, 2, i)
                o(1)

            merge(T_WO_MLA, False)
            split(B_WO_MLA + 2)
            split(B_WO_MLA + 3)

            def split_s(n, ring_hi, ring_lo, src, scale, count, slot):
                dve.wait_ge(s_hi_done, count)
                part_n = src[:, ds(1024 * n, 1024)]
                if scale == 1.0:
                    ins = dve.tensor_tensor(ring_lo[:, slot, :], part_n, f(ring_hi[:, slot, :]), ALU.subtract)
                else:
                    ins = dve.scalar_tensor_tensor(ring_lo[:, slot, :], part_n, scale, f(ring_hi[:, slot, :]),
                                                   ALU.mult, ALU.subtract)
                ins.then_inc(s_lo_done, 1)

            dve.wait_ge(y_done, 2 * KD)
            for n in range(2):
                split_s(n, yr_hi, yr_lo, ybuf, 0.5, n + 1, n)
            for n in range(4):
                if n < 2:
                    split_s(n + 2, yr_hi, yr_lo, ybuf, 0.5, n + 3, n)
                split(B_WOUT + n + 2)

            def add(t, steps):
                dve.wait_ge(acc_step, steps + t + 1)
                dve.tensor_tensor(x_sb[:, t, :], x_sb[:, t, :], ps[:, 1024 * t:1024 * t + 1024],
                                  ALU.add).then_inc(added, 1)

            dve.wait_ge(x_again, 16 * QT)
            for t in range(QT):
                add(t, 12)
            for t in range(QT):
                mean_sq(15 + t, 14 + t, 15 + t, D, 5 + t)
            for t in range(QT):
                dve.wait_ge(rstd_done, 4 + t)
                dve.tensor_scalar(h2[:, t, :], x_sb[:, t, :], rstd[:, 14 + t:15 + t], None,
                                  ALU.mult).then_inc(xn_done, 1)
            for k in range(KD):
                tp_part(G_H2 + k, h_lo[:, k, :], bank(k), g_mlp[:, k:k + 1], h_hi[:, k, :])

            def up(i):
                for c in range(4):
                    slot, turn = ring(T_UP + c, 4, i)
                    dve.wait_ge(tile_done[slot], turn + 1)
                    dve.tensor_tensor(act_sq[:, ds(2048 * i + 512 * c, 512)], relu[:, c % 2, :], relu[:, c % 2, :],
                                      ALU.mult).then_inc(sq_act, 1)
                    if c % 2:
                        split(B_UP + 2 + c // 2, 2, i)

            up(0)
            with dve.Fori(1, FF // 512 - 1) as i:
                up(i)
            for n in range(2):
                split_s(n, ar_hi, ar_lo, act_sq, 1.0, 5 + n, n)
            up(FF // 512 - 1)
            dve.wait_ge(sq_act, FF // P)
            with dve.Fori(0, FF // 512 - 1) as i:
                for c in range(2):
                    split_s(2 * i + c + 2, ar_hi, ar_lo, act_sq, 1.0, 7 + c + 2 * i, c)
                    split(B_DOWN + 2 + c, 2, i)
            dve.wait_ge(fgain_in, 16)
            for t in range(QT):
                add(t, 16 + 60)
            for t in range(QT):
                mean_sq(15 + QT + t, 14 + QT + t, 15 + QT + t, D, 9 + t)
            for t in range(QT):
                dve.wait_ge(rstd_done, 4 + QT + t)
                dve.scalar_tensor_tensor(x_sb[:, t, :], x_sb[:, t, :], rstd[:, 18 + t:19 + t], fgain,
                                         ALU.mult, ALU.mult).then_inc(out_ready, 1)

        @block.tensor
        def _(pe):
            def need(c, per=0, i=0):
                pe.wait_ge(w_lo_done, c + 1 + per * i)
                return c % 2

            def bank_of(c, per=0, i=0):
                slot, turn = ring(c, per, i)
                wait(pe, tile_done[slot], turn)
                return slot

            def have(c, per=0, i=0):
                slot, turn = ring(c, per, i)
                pe.wait_ge(tile_done[slot], turn + 1)

            def mm3(dst, a, b, first, last):
                pe.matmul(dst, a[0], b[1], start=first, stop=False, skip_group_check=True)
                pe.matmul(dst, a[1], b[0], start=False, stop=False, skip_group_check=True)
                return pe.matmul(dst, a[0], b[0], start=False, stop=last, skip_group_check=True)

            def wpair(slot, at, k, n, c0=0, cn=P):
                return w(w_hi, slot, at, k, n, c0, cn), w(w_lo, slot, at, k, n, c0, cn)

            def hpair(k):
                return h_hi[:, k, :], h_lo[:, k, :]

            def project(bk, slot, at, k0=0, k1=KD, n=P, c0=0):
                for k in range(k0, k1):
                    last = mm3(bank(bk), wpair(slot, at, k, n, c0), hpair(k), k == 0, k == KD - 1)
                if k1 == KD:
                    last.then_inc(tile_ready, 1)

            def t_bank(u, per, i):
                pe.wait_ge(p_done, u + 1 + per * i)
                wait(pe, pt_lo_done, u - 1 + per * i)

            def s_bank(u, per, i):
                wait(pe, exp_done, u - 1 + per * i)

            pe.wait_ge(toe_in, 48)
            for h in range(HS):
                pe.matmul(bank(h, 0, TOE), rel[0:BUCKETS, h:h + 1].to_broadcast([BUCKETS, P]), toe[0:BUCKETS, 0:TOE],
                          start=True, stop=True).then_inc(fbank_ready, 1)
            for k in range(KD):
                if k == 0:
                    pe.wait_ge(xn_done, QT)
                pe.wait_ge(frep_done, k + 1)
                for t in range(QT):
                    last = pe.transpose(bank(k, P * t, P * t + P), x_sb[:, t, P * k:P * k + P], ident)
                last.then_inc(tp_ready, 1)
            for k in range(KD):
                if k == 0:
                    pe.wait_ge(xn_done, QT + 2)
                pe.wait_ge(tp_lo, k + 1)
                for t in range(2):
                    last = pe.transpose(bank(k, P * t, P * t + P), mem_sb[:, t, P * k:P * k + P], ident)
                last.then_inc(tp_ready, 1)

            def out_proj(b, t0):
                for m in range(KD):
                    slot = need(b + m // 4)
                    bk = bank_of(t0 + m)
                    for k in range(4):
                        last = mm3(bank(bk), wpair(slot, 0, k, 512, P * (m % 4)), (o_hi[:, k, :], o_lo[:, k, :]),
                                   k == 0, k == 3)
                    last.then_inc(tile_ready, 1)

            pe.wait_ge(tp_lo, 2 * KD)
            for h in range(HM):
                t0, u0, b, e = T_MEM + 5 * h, U_MEM + 2 * h, B_MEM + 3 * h, E_MEM + h
                slot = need(b)
                project(bank_of(t0), slot, 0)
                bk = bank_of(t0 + 1)
                for k in range(KD):
                    last = mm3(bank(bk, 0, M), wpair(slot, 1024, k, P), (mn_hi[:, k, :], mn_lo[:, k, :]),
                               k == 0, k == KD - 1)
                last.then_inc(tile_ready, 1)
                slot = need(b + 1)
                bk = bank_of(t0 + 2)
                for t in range(2):
                    tk = slice(P * t, P * t + P)
                    for k in range(KD):
                        last = mm3(bank(bk, P * t, P * t + P), (mn_hi[:, k, tk], mn_lo[:, k, tk]),
                                   wpair(slot, 0, k, P), k == 0, k == KD - 1)
                last.then_inc(tile_ready, 1)
                project(bank_of(t0 + 3), slot, 1024)
                have(t0 + 1)
                for n in range(2):
                    s_bank(u0 + n, 0, 0)
                    for t in range(2):
                        tk = slice(P * (2 * n + t), P * (2 * n + t + 1))
                        last = mm3(bank(2 + n, M * t, M * t + M), (q_hi[:, h % 2, tk], q_lo[:, h % 2, tk]),
                                   (km_hi, km_lo), True, True)
                    last.then_inc(s_ready, 1)
                slot, bk = need(b + 2), bank_of(t0 + 4)
                project(bk, slot, 0, 0, 5)
                for n in range(2):
                    t_bank(u0 + n, 0, 0)
                    for k in range(2):
                        for t in range(2):
                            last = pe.transpose(bank(4 + n, 256 * k + P * t, 256 * k + P * t + P),
                                                probs[:, n, M * t + P * k:M * t + P * k + P], ident)
                    last.then_inc(t_ready, 1)
                project(bk, slot, 0, 5, 8)
                pe.wait_ge(pt_lo_done, u0 + 2)
                wait(pe, o_lo_done, e)
                ptk = [buf[:, 0:1024].rearrange("p (u k q) -> p k u q", u=2, k=2) for buf in (pt_hi, pt_lo)]
                for k in range(2):
                    last = mm3(bank(6 + h % 2).rearrange("p (u q) -> p u q", u=2), (v_hi[:, k, :], v_lo[:, k, :]),
                               [a[:, k, :, :] for a in ptk], k == 0, k == 1)
                last.then_inc(o_ready, 1)

            slot = need(B_KVS)
            project(bank_of(T_KVS), slot, 0)
            bk = bank_of(T_KVS + 1)
            for t in range(QT):
                tk = slice(P * t, P * t + P)
                for k in range(KD):
                    last = mm3(bank(bk, P * t, P * t + P), (h_hi[:, k, tk], h_lo[:, k, tk]),
                               wpair(slot, 1024, k, P), k == 0, k == KD - 1)
            last.then_inc(tile_ready, 1)
            pe.wait_ge(o_lo_done, E_SWA)
            out_proj(B_WO_MEM, T_WO_MEM)
            pe.wait_ge(bias_lo_done, 1)
            pe.wait_ge(kz_zero, 4)
            pe.wait_ge(idr_done, 2)

            with pe.Fori(0, PAIRS // 2) as i:
                for c in range(2):
                    t0, u0, b = T_SWA + 3 * c, U_SWA + 4 * c, B_SWA + 2 * c
                    slot = need(b, 4, i)
                    project(bank_of(t0, 6, i), slot, 0)
                    project(bank_of(t0 + 1, 6, i), slot, 1024)
                    have(t0, 6, i)

                    def scores(n):
                        s_bank(u0 + n, 8, i)
                        wd = P if n == 0 else 2 * P
                        k0 = max(P * (n - 1), 0)
                        dst = bank(2 + n % 2, 0, 2 * wd).rearrange("p (g n) -> p g n", g=2)
                        for j, buf in enumerate((bias_lo, bias_hi)):
                            pe.matmul(dst, ident_r, buf[:, :, ds(2 * i + c, 1), 2 * P - wd:2 * P]
                                      .rearrange("p g r n -> p g (r n)"), start=j == 0, stop=False,
                                      skip_group_check=True)
                        tk = slice(P * n, P * n + P)
                        mm3(dst, (q_hi[:, c, tk], q_lo[:, c, tk]), (kz_hi[:, :, k0:k0 + wd], kz_lo[:, :, k0:k0 + wd]),
                            False, True).then_inc(s_ready, 1)

                    def turn_p(n):
                        t_bank(u0 + n, 8, i)
                        wd = P if n == 0 else 2 * P
                        for s in range(1 if n == 0 else 0, 2):
                            for g in range(2):
                                a = g * wd + (0 if n == 0 else P * s)
                                last = pe.transpose(bank(4 + n % 2, 256 * s + P * g, 256 * s + P * g + P),
                                                    probs[:, n % 2, a:a + P], ident)
                        last.then_inc(t_ready, 1)

                    scores(0)
                    scores(1)
                    slot, bk = need(b + 1, 4, i), bank_of(t0 + 2, 6, i)
                    project(bk, slot, 0, 0, 2)
                    turn_p(0)
                    scores(2)
                    project(bk, slot, 0, 2, 4)
                    turn_p(1)
                    scores(3)
                    project(bk, slot, 0, 4, 6)
                    turn_p(2)
                    project(bk, slot, 0, 6, 7)
                    turn_p(3)
                    project(bk, slot, 0, 7, 8)
                    pe.wait_ge(pt_lo_done, u0 + 4 + 8 * i)
                    pe.wait_ge(o_lo_done, E_SWA + c + 2 * i)
                    ptg = [buf.rearrange("p (m g q) -> p g m q", g=2, q=P) for buf in (pt_hi, pt_lo)]
                    for k in range(QT):
                        n = 2 if k < QT - 1 else 1
                        for g in range(2):
                            last = mm3(bank(6 + g, P * k, P * (k + n)).rearrange("p (m q) -> p m q", q=P),
                                       (v_hi[:, k, :], v_lo[:, k, :]),
                                       [a[:, g, 2 * k + 1:2 * k + 1 + n, :] for a in ptg], k == 0, k == QT - 1)
                    last.then_inc(o_ready, 1)

            pe.wait_ge(exp_done, U_MLA)
            pe.wait_ge(pt_lo_done, U_MLA)
            for half in range(2):
                slot = need(B_MLAP + half)
                for t in range(QT):
                    tk = slice(P * t, P * t + P)
                    for k in range(4):
                        kk = 4 * half + k
                        last = mm3(bank(2 + t, 0, 416), (h_hi[:, kk, tk], h_lo[:, kk, tk]),
                                   wpair(slot, 0, k, 416, 0, 416), kk == 0, kk == KD - 1)
                    if half == 1 or t == QT - 1:
                        last.then_inc(pre_ready, 1)
            pe.wait_ge(o_lo_done, E_MLA)
            out_proj(B_WO_SWA, T_WO_SWA)
            pe.wait_ge(pre_copied, QT)
            pe.wait_ge(xn_done, QT + 2 + 2 * QT)
            pe.wait_ge(kr_step, 6)
            for k in range(3):
                for t in range(QT):
                    last = pe.transpose(bank(2 + k, P * t, P * t + P), kvq[:, t, P * k:P * k + P], ident)
                last.then_inc(tp_ready, 1)
            for t in range(QT):
                last = pe.transpose(bank(5, P * t, P * t + P)[0:QK, :], kpad[:, t, :], ident)
            last.then_inc(tp_ready, 1)
            pe.wait_ge(tp_lo, G_H2)

            with pe.Fori(0, HA // 2) as i:
                t0, u0, b = T_MLA, U_MLA, B_MLA
                slot = need(b, 2, i)
                ckv = (ckv_hi, ckv_lo)
                vw = [buf[:, slot, 192:448].rearrange("p (h t c) -> p h t c", h=2, t=2)[:, :, 1, :]
                      for buf in (w_hi, w_lo)]
                for n in range(2):
                    bk = bank_of(t0 + n, 8, i)
                    for k in range(2):
                        tk = slice(P * (2 * n + k), P * (2 * n + k + 1))
                        last = mm3(bank(bk, P * k, P * k + P).rearrange("p (h c) -> p h c", h=2),
                                   [a[:, tk] for a in ckv], vw, True, True)
                    last.then_inc(tile_ready, 1)
                for c in range(2):
                    mm3(bank(bank_of(t0 + 2 + c, 8, i)), wpair(slot, 192, c, P), ckv, True,
                        True).then_inc(tile_ready, 1)

                def query(c, slot):
                    bk = bank_of(t0 + 4 + 2 * c, 8, i)
                    for k in range(2):
                        last = mm3(bank(bk)[0:QK, :], wpair(slot, 0, k, QK, 0, QK),
                                   (cq_hi[:, k, :], cq_lo[:, k, :]), k == 0, k == 1)
                    last.then_inc(tile_ready, 1)

                def scores(c, n):
                    s_bank(u0 + 4 * c + n, 8, i)
                    tk, kw = slice(P * n, P * n + P), P * (n + 1)
                    mm3(bank(2 + n % 2, 0, kw), (q_hi[0:QK, c, tk], q_lo[0:QK, c, tk]),
                        (ka_hi[0:QK, c, 0:kw], ka_lo[0:QK, c, 0:kw]), True, False)
                    pe.matmul(bank(2 + n % 2, P * n, P * n + P), ident_r, mask_r, start=False, stop=True,
                              skip_group_check=True).then_inc(s_ready, 1)

                def turn_p(c, n):
                    t_bank(u0 + 4 * c + n, 8, i)
                    for k in range(n + 1):
                        last = pe.transpose(bank(4 + n % 2, P * k, P * k + P), probs[:, n % 2, P * k:P * k + P], ident)
                    last.then_inc(t_ready, 1)

                def values(c):
                    pe.wait_ge(pt_lo_done, u0 + 4 * c + 4 + 8 * i)
                    pe.wait_ge(o_lo_done, E_MLA + c + 2 * i)
                    for k in range(QT):
                        at = slice(512 * k + P * k, 512 * k + 512)
                        last = mm3(bank(6 + c, P * k, 512), (v_hi[:, k, :], v_lo[:, k, :]), (pt_hi[:, at], pt_lo[:, at]),
                                   k == 0, k == QT - 1)
                    last.then_inc(o_ready, 1)

                query(0, slot)
                bk = bank_of(t0 + 5, 8, i)
                project(bk, slot, 448, 0, 4)
                have(t0 + 4, 8, i)
                scores(0, 0)
                scores(0, 1)
                project(bk, slot, 448, 4, 8)
                slot = need(b + 1, 2, i)
                query(1, slot)
                bk = bank_of(t0 + 7, 8, i)
                turn_p(0, 0)
                scores(0, 2)
                project(bk, slot, 448, 0, 1)
                turn_p(0, 1)
                scores(0, 3)
                project(bk, slot, 448, 1, 2)
                turn_p(0, 2)
                have(t0 + 6, 8, i)
                scores(1, 0)
                project(bk, slot, 448, 2, 3)
                turn_p(0, 3)
                scores(1, 1)
                project(bk, slot, 448, 3, 4)
                values(0)
                turn_p(1, 0)
                scores(1, 2)
                project(bk, slot, 448, 4, 5)
                turn_p(1, 1)
                scores(1, 3)
                project(bk, slot, 448, 5, 6)
                turn_p(1, 2)
                project(bk, slot, 448, 6, 7)
                turn_p(1, 3)
                project(bk, slot, 448, 7, 8)
                values(1)

            pe.wait_ge(o_lo_done, E_END)
            out_proj(B_WO_MLA, T_WO_MLA)

            def accumulate(c, per, i, s_hi, s_lo, s_count, first=False, last=False):
                slot = need(c, per, i)
                pe.wait_ge(s_lo_done, s_count)
                n = (c - B_WOUT) % 2
                for t in range(QT):
                    for half in range(2):
                        for k in range(2):
                            a = slice(512 * k + P * t, 512 * k + P * t + P)
                            ins = mm3(bank(2 * t + half), (s_hi[:, n, a], s_lo[:, n, a]),
                                      wpair(slot, 0, k, D, 512 * half, 512), first and k == 0, last and k == 1)
                    ins.then_inc(acc_step, 1)

            pe.wait_ge(tile_done[0], T_UP // 2)
            pe.wait_ge(tile_done[1], T_UP // 2)
            for n in range(D // 256):
                accumulate(B_WOUT + n, 0, 0, yr_hi, yr_lo, n + 1, n == 0, n == D // 256 - 1)
            pe.wait_ge(added, QT)
            pe.wait_ge(xn_done, 3 * QT + 2 + QT)
            for k in range(KD):
                for t in range(QT):
                    last = pe.transpose(bank(k, P * t, P * t + P), h2[:, t, P * k:P * k + P], ident)
                last.then_inc(tp_ready, 1)
            pe.wait_ge(tp_lo, G_H2 + KD)
            with pe.Fori(0, FF // 512) as i:
                for c in range(2):
                    slot = need(B_UP + c, 2, i)
                    for m in range(2):
                        project(bank_of(T_UP + 2 * c + m, 4, i), slot, 0, n=256, c0=P * m)
            pe.wait_ge(tile_done[0], T_UP // 2 + FF // 256)
            pe.wait_ge(tile_done[1], T_UP // 2 + FF // 256)
            for c in range(2):
                accumulate(B_DOWN + c, 0, 0, ar_hi, ar_lo, 5 + c, c == 0)
            with pe.Fori(1, FF // 512 - 1) as i:
                for c in range(2):
                    accumulate(B_DOWN + c, 2, i, ar_hi, ar_lo, 5 + c + 2 * i)
            for c in range(2):
                accumulate(B_END - 2 + c, 0, 0, ar_hi, ar_lo, 5 + FF // 256 - 2 + c, last=c == 1)


def constants():
    con = np.zeros((P, C_END), np.float32)
    con[:, C_ID:C_ID + P] = np.eye(P)
    con[:, C_MASK:C_MASK + P] = np.where(np.arange(P)[None, :] <= np.arange(P)[:, None], 0.0, NEG)
    pos = np.arange(S, dtype=np.float32)
    inv = (1.0 / (np.float32(10000.0) ** (np.arange(0, ROPE, 2, dtype=np.float32) / ROPE))).astype(np.float32)
    ang = pos[:, None] * inv[None, :]
    cos, sin = np.cos(ang), np.sin(ang)
    con[:, C_COST:C_COST + 64] = cos.reshape(QT, P, 16).transpose(1, 0, 2).reshape(P, 64)
    con[:, C_SINT:C_SINT + 64] = sin.reshape(QT, P, 16).transpose(1, 0, 2).reshape(P, 64)
    con[64:80, C_COS:C_COS + S] = con[80:96, C_COS:C_COS + S] = cos.T
    con[64:80, C_SIN:C_SIN + S] = -sin.T
    con[80:96, C_SIN:C_SIN + S] = sin.T
    dist = 2 * P - 1 - np.arange(TOE)
    inside = (dist >= 0) & (dist < P)
    n = np.maximum(dist, 1)
    exact = BUCKETS // 2
    large = exact + (np.log(n.astype(np.float32) / exact) / np.float32(np.log(P / exact))
                     * (BUCKETS - exact)).astype(np.int32)
    bucket = np.where(dist < exact, np.maximum(dist, 0), np.minimum(large, BUCKETS - 1))
    toe = np.zeros((P, 2 * TOE), np.float32)
    toe[0:BUCKETS, 0:TOE] = (bucket[None, :] == np.arange(BUCKETS)[:, None]) & inside[None, :]
    toe[:, TOE:] = np.where(inside, 0.0, NEG)[None, :]
    return con, toe


_INS = ["x", "mem", "rel_bias", "attn_norm", "mem_norm", "w_in", "b_gate", "mla_q_norm", "w_uq", "mla_kv_norm",
        "w_ukv", "attn_sinks", "w_mem_kv", "w_o_mla", "w_o_swa", "w_o_mem", "w_out", "mlp_norm", "w_up", "w_down",
        "final_norm"]


def kernel(**inputs):
    import concourse.bacc as _bacc
    from concourse.bass_utils import run_bass_kernel_spmd as _run

    nc = _bacc.Bacc("TRN2", target_bir_lowering=False, num_devices=1)
    given = {name: np.ascontiguousarray(inputs[name]) for name in _INS}
    given["consts"], given["toeplitz"] = constants()
    arrays, args = {}, []
    for name, a in given.items():
        arrays[f"in_{name}_dram"] = a
        args.append(nc.dram_tensor(f"in_{name}_dram", a.shape, mybir.dt.from_np(a.dtype), kind="ExternalInput").ap())
    args.append(nc.dram_tensor("out_0_dram", (1, S, D), F32, kind="ExternalOutput").ap())
    hybrid_layer(nc, *args)
    r = _run(nc, [arrays], core_ids=[0])
    return r.results[0]["out_0_dram"]
```

```python
from contextlib import ExitStack

import numpy as np

import concourse.bass as bass
from concourse import mybir

F32 = mybir.dt.float32
F32R = mybir.dt.float32r
ALU = mybir.AluOpType
ACT = mybir.ActivationFunctionType
AX_X = mybir.AxisListType.X
ds = bass.ds

P = 128
D = 1024
S = 512
M = 256
KD = D // P
QT = S // P
FF = 4 * D
EPS = 1e-6
NEG = -(2.0 ** 100)
HM, DM = 4, 128
HS, DS = 8, 64
HA, NOPE, ROPE, DV = 8, 64, 32, 64
QK = NOPE + ROPE
QL, KVL = 256, 128
PAIRS = HS // 2
BUCKETS = 32
TOE = 3 * P

COL_KV = QL
COL_QS = COL_KV + KVL + ROPE
COL_KS = COL_QS + HS * DS
COL_QM = COL_KS + 2 * 2 * DS
COL_G = COL_QM + HM * DM
MLA, SWA, MEM = range(3)

BLK = 2048
N_MLAP, N_A, N_GATE = 4 * 416, 2 * 2 * QK + 2 * P + D, D
SHARES = {1: (48,), 2: (16, 32), 3: (16, 16, 16)}

B_MEM = 0
B_KVS = B_MEM + 2 + 2 * HM
B_WO_MEM = B_KVS + 1
B_SWA = B_WO_MEM + 2
B_MLAP = B_SWA + 2 * PAIRS
B_WO_SWA = B_MLAP + 2
B_MLA = B_WO_SWA + 2
B_WO_MLA = B_MLA + HA
B_WOUT = B_WO_MLA + 2
B_UP = B_WOUT + D // 256
B_DOWN = B_UP + FF // 256
B_END = B_DOWN + FF // 256

T_MEM = 0
T_KVS = T_MEM + 4 * HM
T_WO_MEM = T_KVS + 2
T_SWA = T_WO_MEM + KD
T_WO_SWA = T_SWA + 3 * PAIRS
T_MLA = T_WO_SWA + KD
T_WO_MLA = T_MLA + 4 * HA
T_UP = T_WO_MLA + KD

H_MEM = 0
H_KVS = 2 * HM
H_SWA = H_KVS + 1
H_MLA = H_SWA + PAIRS

U_MEM = 0
U_SWA = 2 * HM
U_MLA = U_SWA + QT * PAIRS
U_END = U_MLA + QT * HA
E_MEM, E_SWA, E_MLA = 0, HM, HM + PAIRS
E_END = E_MLA + HA

MT = M // P
TURNS = MT + QT

R_MLA, R_H2, R_END = np.cumsum([3 * TURNS, 4, 2 * QT]).tolist()
N_MLA, N_H2 = np.cumsum([KD * TURNS, 4]).tolist()

Q_MEM, Q_X, Q_CQ, Q_CKV, Q_X1, Q_X2, Q_END = np.cumsum([0, MT, QT, QT, QT, QT, 2 * QT]).tolist()

C_ID, C_MASK, C_COST, C_SINT, C_COS, C_SIN, C_END = np.cumsum([0, P, P, 64, 64, S, S]).tolist()


def ring(c, per, i):
    return c % 2, c // 2 + (per // 2) * i


def wait(eng, sem, value):
    if not isinstance(value, int) or value > 0:
        eng.wait_ge(sem, value)


def hybrid_layer(nc, x, mem, rel_bias, attn_norm, mem_norm, w_in, b_gate, mla_q_norm, w_uq,
                 mla_kv_norm, w_ukv, attn_sinks, w_mem_kv, w_o_mla, w_o_swa, w_o_mem, w_out,
                 mlp_norm, w_up, w_down, final_norm, consts, toeplitz, out):
    ctx = ExitStack()
    with ctx:
        place = [-(-nc.sbuf_base // 32) * 32]

        def sb(name, width, dt=F32, at=None):
            off = place[0] if at is None else at
            if at is None:
                place[0] += -(-4 * width // 32) * 32
            t = nc.alloc_sbuf_tensor_at(name, [P, width], dt, offset=off)
            return t[:, :], off

        def sem(name):
            return ctx.enter_context(nc.semaphore(name))

        w_hi = sb("w_hi", 2 * BLK, F32R)[0].rearrange("p (s n) -> p s n", s=2)
        w_lo = sb("w_lo", 2 * BLK, F32R)[0].rearrange("p (s n) -> p s n", s=2)
        h_hi_flat, h_hi_at = sb("h_hi", KD * S, F32R)
        h_lo_flat, _ = sb("h_lo", KD * S, F32R)
        h_hi = h_hi_flat.rearrange("p (k n) -> p k n", k=KD)
        h_lo = h_lo_flat.rearrange("p (k n) -> p k n", k=KD)
        attn, attn_at = sb("attn", 17408, F32R)

        def part(lo, n):
            return attn[:, lo:lo + n]

        o_hi = part(0, 2048).rearrange("p (k n) -> p k n", k=4)
        o_lo = part(2048, 2048).rearrange("p (k n) -> p k n", k=4)
        pt_hi, pt_lo = part(4096, 2048), part(6144, 2048)
        q_hi = part(8192, 1024).rearrange("p (s n) -> p s n", s=2)
        q_lo = part(9216, 1024).rearrange("p (s n) -> p s n", s=2)
        v_hi = part(10240, 512).rearrange("p (k n) -> p k n", k=4)
        v_lo = part(10752, 512).rearrange("p (k n) -> p k n", k=4)
        vm_hi = part(10240, 1024).rearrange("p (t n) -> p t n", t=MT)
        vm_lo = part(15872, 1024).rearrange("p (t n) -> p t n", t=MT)
        km_hi, km_lo = part(11264, M), part(11264 + M, M)
        mn_hi = part(11776, 2048).rearrange("p (k n) -> p k n", k=KD)
        mn_lo = part(13824, 2048).rearrange("p (k n) -> p k n", k=KD)
        kz_hi = part(11264, 1024).rearrange("p (g n) -> p g n", g=2)
        kz_lo = part(12288, 1024).rearrange("p (g n) -> p g n", g=2)
        bias_hi = part(13312, 2048).rearrange("p (g r n) -> p g r n", g=2, r=PAIRS)
        bias_lo = part(15360, 2048).rearrange("p (g r n) -> p g r n", g=2, r=PAIRS)
        ka_hi = part(11264, 1024).rearrange("p (s n) -> p s n", s=2)
        ka_lo = part(12288, 1024).rearrange("p (s n) -> p s n", s=2)
        cq_hi = part(13312, 1024).rearrange("p (k n) -> p k n", k=2)
        cq_lo = part(14336, 1024).rearrange("p (k n) -> p k n", k=2)
        ckv_hi, ckv_lo = part(15360, 512), part(15872, 512)
        act_sq = sb("act_sq", FF // P * S, F32, at=attn_at)[0]
        mem_sb = act_sq[:, 8192:8192 + 2 * D].rearrange("p (t n) -> p t n", t=2)
        yr_hi = part(4096, 2048).rearrange("p (s n) -> p s n", s=2)
        yr_lo = part(6144, 2048).rearrange("p (s n) -> p s n", s=2)

        raw = sb("raw", 2 * BLK)[0].rearrange("p (s n) -> p s n", s=2)
        xg, xg_at = sb("xg", QT * D)
        x_sb = xg.rearrange("p (t n) -> p t n", t=QT)
        gate = xg.rearrange("p (m n) -> p m n", m=KD)
        ybuf, y_at = sb("ybuf", QT * D)
        ar_hi = sb("ar_hi", 2 * 1024, F32R, at=y_at)[0].rearrange("p (s n) -> p s n", s=2)
        ar_lo = sb("ar_lo", 2 * 1024, F32R, at=y_at + 4 * 2 * 1024)[0].rearrange("p (s n) -> p s n", s=2)
        fin = sb("fin", QT * D, at=h_hi_at)[0].rearrange("p (t n) -> p t n", t=QT)
        y = ybuf.rearrange("p (m n) -> p m n", m=KD)
        frep = ybuf[:, 0:HS * TOE].rearrange("p (h n) -> p h n", h=HS)
        scratch, _ = sb("scratch", BLK)
        toe = scratch[:, 0:TOE]
        bias_raw = scratch
        kvq = scratch[:, 0:4 * 416].rearrange("p (t n) -> p t n", t=QT)
        rope_a, rope_b = scratch[:, 0:S], scratch[:, S:2 * S]
        fgain = scratch[:, 0:D]
        relu = scratch[:, D:2 * D].rearrange("p (s n) -> p s n", s=2)
        probs_flat, _ = sb("probs", 2 * S)
        probs = probs_flat.rearrange("p (s n) -> p s n", s=2)
        junk = probs_flat
        tmp_flat, tmp_at = sb("tmp", 2 * S)
        tmp = tmp_flat.rearrange("p (s n) -> p s n", s=2)
        toe_r = sb("toe_r", TOE, F32R, at=tmp_at)[0]
        rel_hi, rel_lo = sb("rel_hi", HS, F32R)[0], sb("rel_lo", HS, F32R)[0]
        con, _ = sb("con", C_END)
        ident = con[:, C_ID:C_ID + P]
        cos_t = con[:, C_COST:C_COST + 64].rearrange("p (t n) -> p t n", t=QT)
        sin_t = con[:, C_SINT:C_SINT + 64].rearrange("p (t n) -> p t n", t=QT)
        cos_f, sin_f = con[:, C_COS:C_COS + S], con[:, C_SIN:C_SIN + S]
        ident_r, mask_r = sb("ident_r", P, F32R)[0], sb("mask_r", P, F32R)[0]
        kpad = sb("kpad", QT * QK)[0].rearrange("p (t n) -> p t n", t=QT)
        rtmp = sb("rtmp", 4 * 64)[0].rearrange("p (a t n) -> p a t n", a=4, t=QT)
        g_attn, g_mem, g_mlp = sb("g_attn", KD)[0], sb("g_mem", KD)[0], sb("g_mlp", KD)[0]
        g_q, g_kv = sb("g_q", 2)[0], sb("g_kv", 1)[0]
        hb, hb_raw = sb("hb", 3 * KD)[0], sb("hb_raw", 3 * KD)[0]
        sinks, nsinks = sb("sinks", HS)[0], sb("nsinks", HS)[0].rearrange("p (g r) -> p g r", g=2)
        rel = sb("rel", HS)[0]
        half_neg = sb("half_neg", 8)[0]
        sumsq, rstd = sb("sumsq", Q_END)[0], sb("rstd", Q_END)[0]
        mx = sb("mx", 4)[0].rearrange("p (s g) -> p s g", s=2)
        negm = sb("negm", 4)[0].rearrange("p (s g) -> p s g", s=2)
        snk = sb("snk", 4)[0].rearrange("p (s g) -> p s g", s=2)
        esnk = sb("esnk", 4)[0].rearrange("p (s g) -> p s g", s=2)
        rsum = sb("rsum", 4)[0].rearrange("p (s g) -> p s g", s=2)
        tot = sb("tot", 4)[0].rearrange("p (s g) -> p s g", s=2)
        rinv = sb("rinv", 4)[0].rearrange("p (s g) -> p s g", s=2)

        ps = ctx.enter_context(nc.psum_tensor("ps", [P, 8 * 512], F32))

        def bank(n, lo=0, hi=512):
            return ps[:, 512 * n + lo:512 * n + hi]

        bias_rows = nc.dram_tensor("bias_rows", [P, HS, TOE], F32)

        const_in, toe_in = sem("const_in"), sem("toe_in")
        ident_in, tab_in, gain_in = sem("ident_in"), sem("tab_in"), sem("gain_in")
        tokens_in = [sem(f"tokens_in{n}") for n in range(TURNS)]
        vs_turned, vs_hi_done, vs_lo_done = sem("vs_turned"), sem("vs_hi_done"), sem("vs_lo_done")
        vm_ready, vm_hi_done, vm_lo_done = sem("vm_ready"), sem("vm_hi_done"), sem("vm_lo_done")
        inv_step, rel_step = sem("inv_step"), sem("rel_step")
        raw_in = [sem("raw_in0"), sem("raw_in1")]
        w_hi_done, w_lo_done = sem("w_hi_done"), sem("w_lo_done")
        tile_ready = sem("tile_ready")
        tile_done = [sem("tile_done0"), sem("tile_done1")]
        tile_hi = sem("tile_hi")
        tp_ready, tp_hi, tp_lo = sem("tp_ready"), sem("tp_hi"), sem("tp_lo")
        sq_done, ms_done, rstd_done, xn_done = sem("sq_done"), sem("ms_done"), sem("rstd_done"), sem("xn_done")
        s_ready, mx_done, neg_done, exp_done = sem("s_ready"), sem("mx_done"), sem("neg_done"), sem("exp_done")
        nsk_done, tot_done, rinv_done, p_done = sem("nsk_done"), sem("tot_done"), sem("rinv_done"), sem("p_done")
        t_ready, pt_hi_done, pt_lo_done = sem("t_ready"), sem("pt_hi_done"), sem("pt_lo_done")
        o_ready, o_hi_done, o_lo_done = sem("o_ready"), sem("o_hi_done"), sem("o_lo_done")
        fbank_ready, frep_done, rows_out, bias_in = sem("fbank_ready"), sem("frep_done"), sem("rows_out"), sem("bias_in")
        idr_done, small_done, nhalf_done = sem("idr_done"), sem("small_done"), sem("nhalf_done")
        bias_hi_done, bias_lo_done, kz_zero = sem("bias_hi_done"), sem("bias_lo_done"), sem("kz_zero")
        pre_ready, pre_copied, kr_step = sem("pre_ready"), sem("pre_copied"), sem("kr_step")
        rope_step, q_done = sem("rope_step"), sem("q_done")
        y_done, x_again = sem("y_done"), sem("x_again")
        s_hi_done, s_lo_done, acc_step, added = sem("s_hi_done"), sem("s_lo_done"), sem("acc_step"), sem("added")
        sq_act, fgain_in, gained = sem("sq_act"), sem("fgain_in"), sem("gained")
        out_left, out_right, out_done = sem("out_left"), sem("out_right"), sem("out_done")

        win = w_in[0].rearrange("(k p) n -> p k n", p=P)
        wmk = w_mem_kv[0].rearrange("(k p) n -> p k n", p=P)
        wuq = w_uq[0].rearrange("(k p) n -> p k n", p=P)
        wup = w_up[0].rearrange("(k p) n -> p k n", p=P)
        wdn = w_down[0].rearrange("(k p) n -> p k n", p=P)
        wou = w_out[0].rearrange("(k p) n -> p k n", p=P)
        wo = {MLA: w_o_mla[0].rearrange("(k p) n -> p k n", p=P),
              MEM: w_o_mem[0].rearrange("(k p) n -> p k n", p=P)}
        wo_s = w_o_swa[0].rearrange("(g r d) n -> g d r n", g=2, r=PAIRS)
        xv = x[0].rearrange("(t p) n -> t p n", p=P)
        mv = mem[0].rearrange("(t p) n -> t p n", p=P)
        ov = out[0].rearrange("(t p) n -> t p n", p=P)

        def col(v):
            return v.rearrange("(k p) -> p k", p=P)

        def row(v, n):
            return bass.AP(v.tensor, v.offset, [[0, P], [1, n]])

        token_rows = [mem_sb[:, t, :] for t in range(MT)] + [x_sb[:, t, :] for t in range(QT)]

        block = ctx.enter_context(nc.Block())

        @block.sync
        def _(sp):
            def fetch(c, per, i, pieces):
                slot, _ = ring(c, per, i)
                wait(sp, w_lo_done, c - 1 + per * i)
                found = pieces(raw[:, slot, :])
                for (dst, src), share in zip(found, SHARES[len(found)]):
                    sp.dma_start(dst, src).then_inc(raw_in[slot], share)

            def cols(r, at, view, c0, n, k=KD):
                return r[:, at:at + k * n].rearrange("p (k c) -> p k c", k=k), view[:, :, ds(c0, n)]

            def gate_cols(r, at, branch, m):
                return cols(r, at, win, COL_G + branch * D + P * m, P)

            def fetch_wo(branch, b):
                for half in range(2):
                    c0 = half * 512
                    if branch == SWA:
                        fetch(b + half, 0, 0, lambda r: [
                            (r[64 * g:64 * g + 64, :].rearrange("p (k c) -> p k c", k=4),
                             wo_s[g][:, :, c0:c0 + 512]) for g in range(2)])
                    else:
                        fetch(b + half, 0, 0, lambda r: [cols(r, 0, wo[branch], c0, 512, 4)])

            sp.dma_start(con[:, 0:C_MASK], consts[:, 0:C_MASK]).then_inc(ident_in, 16)

            def fetch_tokens(n):
                src = mv[n] if n < MT else xv[n - MT]
                sp.dma_start(token_rows[n], src).then_inc(tokens_in[n], 16)

            def fetch_vm(half):
                fetch(B_MEM + half, 0, 0, lambda r: [
                    (r.rearrange("p (k c) -> p k c", k=4), wmk[:, 4 * half:4 * half + 4, HM * DM:2 * HM * DM])])

            fetch_tokens(0)
            fetch_tokens(1)
            fetch_vm(0)
            for n in range(MT, TURNS):
                fetch_tokens(n)
            fetch_vm(1)
            for h in range(HM):
                b = B_MEM + 2 + 2 * h
                fetch(b, 0, 0, lambda r: [cols(r, 0, win, COL_QM + DM * h, P), cols(r, 1024, wmk, DM * h, P)])
                if h == 0:
                    sp.dma_start(toe[0:BUCKETS + 1, :], toeplitz).then_inc(toe_in, 16)
                    sp.dma_start(con[:, C_MASK:C_COS], consts[:, C_MASK:C_COS]).then_inc(tab_in, 16)
                    sp.dma_start(con[64:96, C_COS:C_END], consts[64:96, C_COS:C_END]).then_inc(tab_in, 16)
                fetch(b + 1, 0, 0, lambda r: [gate_cols(r, 0, MEM, 2 * h), gate_cols(r, 1024, MEM, 2 * h + 1)])
                if h == 1:
                    sp.wait_ge(frep_done, HS)
                    sp.dma_start(bias_rows.ap(), frep).then_inc(rows_out, 16)
                if h == 2:
                    sp.wait_ge(rows_out, 16)
                    sp.dma_start(bias_raw.rearrange("p (h n) -> p h n", h=HS),
                                 bass.AP(bias_rows, P - 1, [[HS * TOE - 1, P], [TOE, HS], [1, 2 * P]])
                                 ).then_inc(bias_in, 16)
            fetch(B_KVS, 0, 0, lambda r: [cols(r, 0, win, COL_KS, P), cols(r, 1024, win, COL_KS + P, P)])
            fetch_wo(MEM, B_WO_MEM)
            with sp.Fori(0, PAIRS // 2) as i:
                for c in range(2):
                    fetch(B_SWA + 2 * c, 4, i, lambda r: [
                        (r[:, 0:1024].rearrange("p (k c) -> p k c", k=KD)[:, :, 64 * g:64 * g + 64],
                         win[:, :, ds(COL_QS + 256 * g + 64 * c + 128 * i, 64)]) for g in range(2)
                    ] + [gate_cols(r, 1024, SWA, 4 * i + 2 * c)])
                    fetch(B_SWA + 2 * c + 1, 4, i, lambda r: [gate_cols(r, 0, SWA, 4 * i + 2 * c + 1)])
            for half in range(2):
                fetch(B_MLAP + half, 0, 0, lambda r: [
                    (r[:, 0:4 * 416].rearrange("p (k c) -> p k c", k=4), win[:, 4 * half:4 * half + 4, 0:416])])
            fetch_wo(SWA, B_WO_SWA)
            with sp.Fori(0, HA // 2) as i:
                fetch(B_MLA, 2, i, lambda r: [cols(r, 0, wuq, 2 * QK * i, 2 * QK, 2),
                                              (r[:, 4 * QK:4 * QK + 2 * P], w_ukv[0][:, ds(2 * P * i, 2 * P)]),
                                              gate_cols(r, N_A - D, MLA, 2 * i)])
                fetch(B_MLA + 1, 2, i, lambda r: [gate_cols(r, 0, MLA, 2 * i + 1)])
            fetch_wo(MLA, B_WO_MLA)

            def rows(view, k):
                return lambda r: [(r.rearrange("p (k c) -> p k c", k=2), view[:, ds(k, 2), :])]

            with sp.Fori(0, D // 512) as i:
                for c in range(2):
                    fetch(B_WOUT + c, 2, i, rows(wou, 4 * i + 2 * c))
            with sp.Fori(0, FF // 512) as i:
                for c in range(2):
                    fetch(B_UP + c, 2, i, lambda r: [cols(r, 0, wup, 512 * i + 256 * c, 256)])
            with sp.Fori(0, FF // 512) as i:
                for c in range(2):
                    fetch(B_DOWN + c, 2, i, rows(wdn, 4 * i + 2 * c))
            for t in range(QT):
                for half, scaled in enumerate((out_left, out_right)):
                    sp.wait_ge(scaled, t + 1)
                    a = slice(512 * half, 512 * half + 512)
                    sp.dma_start(ov[t][:, a], fin[:, t, a]).then_inc(out_done, 16)
            sp.wait_ge(out_done, 32 * QT)

        BATCHES = ([(n, n + 1, n + 1) for n in range(TURNS)] + [(Q_CQ, Q_X1, TURNS + 2)]
                   + [(Q_X2 + t, Q_X2 + t + 1, TURNS + 4 + 2 * t) for t in range(QT)])
        BATCH_MLA, BATCH_X2 = TURNS, TURNS + 1

        def turned_bank(n, k):
            return bank(3 * (n % 2) + k % 3, P * (k // 3), P * (k // 3) + P)

        def turned_x(t, k):
            return bank(2 * t + k % 2, P * (k // 2), P * (k // 2) + P)

        def w(buf, slot, at, k, n, c0=0, cn=P):
            return buf[:, slot, at + k * n + c0:at + k * n + c0 + cn]

        @block.gpsimd
        def _(pool):
            pool.memset(rel[BUCKETS:BUCKETS + 1, :], 1.0).then_inc(rel_step, 1)
            pool.wait_ge(rel_step, 1)
            pool.memset(half_neg, -0.5).then_inc(nhalf_done, 1)
            pool.memset(kpad, 0.0).then_inc(nhalf_done, 1)
            pool.wait_ge(nhalf_done, 1)

            def rsqrt(n):
                a, b, count = BATCHES[n]
                pool.wait_ge(ms_done, count)
                pool.tensor_tensor(rstd[:, a:b], rstd[:, a:b], half_neg[:, 0:b - a],
                                   ALU.pow).then_inc(rstd_done, 1)

            for n in range(BATCH_MLA):
                rsqrt(n)
            pool.wait_ge(tile_ready, T_KVS + 1)
            for buf in (kz_hi, kz_lo):
                pool.memset(buf[64:128, 0, :].bitcast(F32), 0.0).then_inc(kz_zero, 1)
                pool.memset(buf[0:64, 1, :].bitcast(F32), 0.0).then_inc(kz_zero, 1)
            rsqrt(BATCH_MLA)
            with pool.Fori(0, HA) as j:
                pool.wait_ge(rope_step, 3 * j + 1)
                pool.tensor_tensor(rope_a[64:96, :], rope_a[64:96, :], sin_f[64:96, :],
                                   ALU.mult).then_inc(rope_step, 1)
                pool.wait_ge(rope_step, 3 * j + 2)
                pool.tensor_tensor(rope_b[64:96, :], rope_b[64:96, :], rope_a[64:96, :],
                                   ALU.add).then_inc(rope_step, 1)
            for n in range(BATCH_X2, len(BATCHES)):
                rsqrt(n)

        @block.scalar
        def _(act):
            def split(c, per=0, i=0, n=BLK, start=0, stop=None):
                slot, turn = ring(c, per, i)
                stop = n if stop is None else stop
                if start == 0:
                    act.wait_ge(raw_in[slot], 48 * (turn + 1))
                ins = act.activation(w_hi[:, slot, start:stop], raw[:, slot, start:stop], ACT.Copy)
                if stop == n:
                    ins.then_inc(w_hi_done, 1)

            def ready(c, per=0, i=0):
                act.wait_ge(tile_ready, c + 1 + per * i)
                return c % 2

            def square(n, src):
                wait(act, sq_done, n)
                act.activation(junk[:, 0:src.shape[-1]], src, ACT.Square,
                               accum_out=sumsq[:, n:n + 1]).then_inc(sq_done, 1)

            def tp_part(g, dst, src, gain):
                act.wait_ge(tp_ready, g + 1)
                act.activation(dst, src, ACT.Copy, scale=gain).then_inc(tp_hi, 1)

            def turned(t, r0, n0, banks, place, dst, gain):
                for k in range(KD):
                    if k >= banks:
                        act.wait_ge(tp_lo, n0 + k - banks + 1)
                    tp_part(r0 + k % banks, dst[:, k, P * t:P * t + P], place(k), gain[:, k:k + 1])

            def turned_in(n):
                act.wait_ge(gain_in, 32)
                t, dst, gain = (n, mn_hi, g_mem) if n < MT else (n - MT, h_hi, g_attn)
                turned(t, 3 * n, KD * n, 3, lambda k: turned_bank(n, k), dst, gain)

            def tanh(m, branch, c, per=0, i=0):
                bk = ready(c, per, i)
                act.activation(gate[:, ds(m, 1), :], bank(bk).rearrange("p (m n) -> p m n", m=1), ACT.Tanh,
                               bias=hb[:, ds(branch * KD + m, 1)], scale=0.5).then_inc(tile_done[bk], 1)

            def exps(u, per, i, groups, n, scale, sink=False):
                s = u % 2
                act.wait_ge(neg_done, u + 1 + per * i)
                if sink:
                    act.activation(esnk[:, s, :], snk[:, s, :], ACT.Exp)
                for g in range(groups):
                    last = act.activation(probs[:, s, g * n:(g + 1) * n], bank(2 + s, g * n, (g + 1) * n), ACT.Exp,
                                          bias=negm[:, s, g:g + 1], scale=scale, accum_out=rsum[:, s, g:g + 1])
                last.then_inc(exp_done, 1)

            def pt(u, per, i, dst, src):
                act.wait_ge(t_ready, u + 1 + per * i)
                act.activation(dst, src, ACT.Copy).then_inc(pt_hi_done, 1)

            with nc.allow_non_contiguous_dma(reason="gains as columns: a few KiB in all"):
                act.dma_start(g_mem, col(mem_norm[0])).then_inc(gain_in, 16)
                act.dma_start(g_attn, col(attn_norm[0])).then_inc(gain_in, 16)

            def square_in(n):
                act.wait_ge(tokens_in[n], 16)
                square(n, token_rows[n])

            square_in(0)
            square_in(1)
            turned_in(0)
            square_in(2)
            turned_in(1)
            split(0)
            square_in(3)
            with nc.allow_non_contiguous_dma(reason="gains as columns: a few KiB in all"):
                act.dma_start(rel[0:BUCKETS, :], rel_bias).then_inc(toe_in, 16)
                for dst, src in ((hb_raw, col(b_gate[0])), (sinks, row(attn_sinks[0], HS)),
                                 (g_mlp, col(mlp_norm[0])), (g_q, col(mla_q_norm[0])),
                                 (g_kv, col(mla_kv_norm[0]))):
                    act.dma_start(dst, src).then_inc(const_in, 16)
            turned_in(2)
            square_in(4)
            turned_in(3)
            square_in(5)
            turned_in(4)
            split(1)
            turned_in(5)
            split(2)
            for t in range(MT):
                act.wait_ge(vm_ready, t + 1)
                act.activation(vm_hi[:, t, :], bank(6 + t), ACT.Copy).then_inc(vm_hi_done, 1)
            split(3)
            act.wait_ge(tab_in, 32)
            act.wait_ge(toe_in, 32)
            act.wait_ge(rel_step, 1)
            act.activation(rel_hi[0:BUCKETS + 1, :], rel[0:BUCKETS + 1, :], ACT.Copy).then_inc(rel_step, 1)
            act.activation(toe_r[0:BUCKETS + 1, :], toe[0:BUCKETS + 1, :], ACT.Copy).then_inc(rel_step, 1)
            act.activation(ident_r, ident, ACT.Copy).then_inc(idr_done, 1)
            act.activation(mask_r, con[:, C_MASK:C_MASK + P], ACT.Copy).then_inc(idr_done, 1)
            act.wait_ge(small_done, 1)

            for h in range(HM):
                t0, u0, b = T_MEM + 4 * h, U_MEM + 2 * h, B_MEM + 2 + 2 * h
                bk = ready(t0)
                act.activation(q_hi[:, h % 2, :], bank(bk), ACT.Copy).then_inc(tile_hi, 1)
                bk = ready(t0 + 1)
                act.activation(km_hi, bank(bk, 0, M), ACT.Copy).then_inc(tile_hi, 1)
                exps(u0, 0, 0, 2, M, DM ** -0.5)
                exps(u0 + 1, 0, 0, 2, M, DM ** -0.5)
                tanh(2 * h, MEM, t0 + 2)
                for n in range(2):
                    pt(u0 + n, 0, 0, pt_hi[:, 512 * n:512 * n + 512], bank(4 + n))
                split(b + 2)
                tanh(2 * h + 1, MEM, t0 + 3)
                split(b + 3)
                act.wait_ge(o_ready, E_MEM + h + 1)
                act.activation(o_hi[:, h, :], bank(6 + h % 2), ACT.Copy).then_inc(o_hi_done, 1)

            bk = ready(T_KVS)
            act.activation(kz_hi[0:64, 0, :], bank(bk)[0:64, :], ACT.Copy)
            act.activation(kz_hi[64:128, 1, :], bank(bk)[64:128, :], ACT.Copy).then_inc(tile_hi, 1)
            act.wait_ge(bias_in, 16)
            act.activation(bias_hi, bias_raw.rearrange("p (g r n) -> p g r n", g=2, r=PAIRS),
                           ACT.Copy).then_inc(bias_hi_done, 1)
            bk = ready(T_KVS + 1)
            act.activation(tmp[:, 0, :], bank(bk), ACT.Copy).then_inc(tile_done[bk], 1)
            split(B_KVS + 2)
            act.wait_ge(vs_turned, 1)
            act.activation(v_hi, bank(4).rearrange("p (k n) -> p k n", k=4), ACT.Copy).then_inc(vs_hi_done, 1)
            ready(T_WO_MEM + 3)
            split(B_WO_MEM + 2)
            ready(T_WO_MEM + 7)
            split(B_WO_MEM + 3)
            for slot in range(2):
                act.wait_ge(tile_done[slot], (T_WO_MEM + KD) // 2)

            with act.Fori(0, PAIRS // 2) as i:
                for c in range(2):
                    t0, u0, b = T_SWA + 3 * c, U_SWA + 4 * c, B_SWA + 2 * c
                    bk = ready(t0, 6, i)
                    act.activation(q_hi[:, c, :], bank(bk), ACT.Copy).then_inc(tile_hi, 1)

                    def e(n):
                        exps(u0 + n, 8, i, 2, P if n == 0 else 2 * P, DS ** -0.5, True)

                    def p(n):
                        lo = 256 if n == 0 else 0
                        pt(u0 + n, 8, i, pt_hi[:, 512 * n + lo:512 * n + 512], bank(4 + n % 2, lo, 512))

                    e(0)
                    e(1)
                    p(0)
                    e(2)
                    p(1)
                    tanh(2 * c + 4 * i, SWA, t0 + 1, 6, i)
                    e(3)
                    split(b + 2, 4, i, stop=BLK // 2)
                    p(2)
                    split(b + 2, 4, i, start=BLK // 2)
                    p(3)
                    tanh(2 * c + 1 + 4 * i, SWA, t0 + 2, 6, i)
                    split(b + 3, 4, i, n=N_GATE if c == 0 else N_MLAP)
                    act.wait_ge(o_ready, E_SWA + c + 1 + 2 * i)
                    for g in range(2):
                        r = slice(64 * g, 64 * g + 64)
                        last = act.activation(o_hi[r, ds(2 * i + c, 1), :],
                                              bank(6 + g)[r, :].rearrange("p (m n) -> p m n", m=1), ACT.Copy)
                    last.then_inc(o_hi_done, 1)

            act.wait_ge(pre_ready, 1)
            split(B_MLAP + 2)
            act.wait_ge(bias_lo_done, 1)
            for t in range(QT):
                act.wait_ge(pre_ready, t + 2)
                act.activation(kvq[:, t, :], bank(2 + t, 0, 416), ACT.Copy).then_inc(pre_copied, 1)
            split(B_MLAP + 3)
            act.wait_ge(pre_copied, QT)
            for t in range(QT):
                square(Q_CQ + t, kvq[:, t, 0:QL])
            for t in range(QT):
                square(Q_CKV + t, kvq[:, t, QL:QL + KVL])
            ready(T_WO_SWA + 3)
            split(B_MLA, n=N_A)
            for k in range(2):
                tp_part(R_MLA + k, cq_hi[:, k, :], bank(2 + k), g_q[:, k:k + 1])
            tp_part(R_MLA + 2, ckv_hi, bank(4), g_kv[:, 0:1])
            act.wait_ge(tp_ready, R_MLA + 4)
            act.activation(ka_hi[64:96, 0, :], bank(5)[64:96, :], ACT.Copy)
            act.activation(ka_hi[64:96, 1, :], bank(5)[64:96, :], ACT.Copy).then_inc(tp_hi, 1)
            def key(n, c, per=0, i=0):
                bk = ready(n, per, i)
                act.activation(ka_hi[0:64, c, :], bank(bk)[0:64, :], ACT.Copy).then_inc(tile_hi, 1)

            def query(n, c, per=0, i=0):
                bk = ready(n, per, i)
                act.activation(q_hi[0:64, c, :], bank(bk)[0:64, :], ACT.Copy).then_inc(tile_hi, 1)

            def rotary(j, c):
                act.wait_ge(rope_step, 3 + 3 * j)
                act.activation(q_hi[64:96, c, :], rope_b[64:96, :], ACT.Copy).then_inc(tile_hi, 1)

            ready(T_WO_SWA + 7)
            split(B_MLA + 1, n=N_GATE)
            key(T_MLA, 0)
            query(T_MLA + 1, 0)
            act.wait_ge(y_done, KD)

            def two_heads(i, final=False):
                t0, u0, b = T_MLA + 2, U_MLA, B_MLA
                for n in range(2):
                    bk = ready(t0 + n, 8, i)
                    act.activation(v_hi[:, 2 * n:2 * n + 2, :], bank(bk, 0, 256).rearrange("p (k n) -> p k n", k=2),
                                   ACT.Copy).then_inc(tile_hi, 1)
                rotary(2 * i, 0)
                key(t0 + 2, 1, 8, i)
                query(t0 + 3, 1, 8, i)

                def e(c, n):
                    exps(u0 + 4 * c + n, 8, i, 1, P * (n + 1), QK ** -0.5)

                def p(c, n):
                    pt(u0 + 4 * c + n, 8, i,
                       pt_hi.rearrange("p (k q) -> p k q", k=4)[:, 0:n + 1, P * n:P * n + P],
                       bank(4 + n % 2, 0, P * (n + 1)).rearrange("p (k q) -> p k q", q=P))

                def o(c):
                    r = slice(64 * c, 64 * c + 64)
                    act.wait_ge(o_ready, E_MLA + c + 1 + 2 * i)
                    act.activation(o_hi[r, ds(i, 1), :], bank(6 + c)[r, :].rearrange("p (m n) -> p m n", m=1),
                                   ACT.Copy).then_inc(o_hi_done, 1)

                e(0, 0)
                e(0, 1)
                p(0, 0)
                e(0, 2)
                rotary(1 + 2 * i, 1)
                p(0, 1)
                e(0, 3)
                p(0, 2)
                p(0, 3)
                e(1, 0)
                e(1, 1)
                tanh(2 * i, MLA, t0 + 4, 8, i)
                split(b + 2, 2, i, n=BLK if final else N_A)
                act.wait_ge(o_ready, E_MLA + 1 + 2 * i)
                p(1, 0)
                e(1, 2)
                p(1, 1)
                e(1, 3)
                o(0)
                p(1, 2)
                p(1, 3)
                tanh(2 * i + 1, MLA, t0 + 5, 8, i)
                if not final:
                    key(t0 + 6, 0, 8, i)
                    query(t0 + 7, 0, 8, i)
                    split(b + 3, 2, i, n=N_GATE)
                o(1)
                if final:
                    split(b + 3, 2, i)

            with act.Fori(0, HA // 2 - 1) as i:
                two_heads(i)
            two_heads(HA // 2 - 1, True)

            def split_s(n, ring_hi, src, scale, c=0, per=0, i=0):
                act.activation(ring_hi[:, c % 2, :], src[:, ds(1024 * n, 1024)], ACT.Copy,
                               scale=scale).then_inc(s_hi_done, 1)

            ready(T_WO_MLA + 3)
            split(B_WO_MLA + 2)
            for n in range(2):
                act.wait_ge(y_done, KD + 2 * n + 2)
                split_s(n, yr_hi, ybuf, 0.5, n)
            ready(T_WO_MLA + 7)
            split(B_WO_MLA + 3)
            act.wait_ge(y_done, 2 * KD)
            for t in range(QT):
                act.dma_start(x_sb[:, t, :], xv[t]).then_inc(x_again, 16)
            act.dma_start(fgain, row(final_norm, D)).then_inc(fgain_in, 16)
            for n in range(3):
                act.wait_ge(acc_step, 8 * (n + 1))
                if n < 2:
                    split_s(n + 2, yr_hi, ybuf, 0.5, n)
                split(B_WOUT + n + 2)
            for t in range(QT):
                turned(t, R_H2 + 2 * t, N_H2 + KD * t, 2, lambda k: turned_x(t, k), h_hi, g_mlp)
            split(B_UP + 1)
            for t in range(QT):
                square(Q_X1 + t, x_sb[:, t, :])

            def up(i):
                for c in range(4):
                    slot, turn = ring(T_UP + c, 4, i)
                    ready(T_UP + c, 4, i)
                    wait(act, sq_act, c - 1 + 4 * i)
                    act.activation(relu[:, c % 2, :], bank(slot), ACT.Relu).then_inc(tile_done[slot], 1)
                    if c % 2:
                        split(B_UP + 2 + c // 2, 2, i)

            up(0)
            with act.Fori(1, FF // 512 - 1) as i:
                up(i)
            act.wait_ge(tp_ready, R_END)
            for n in range(2):
                act.wait_ge(sq_act, 2 * n + 2)
                split_s(n, ar_hi, act_sq, 1.0, n)
            up(FF // 512 - 1)
            act.wait_ge(sq_act, FF // P)
            with act.Fori(0, FF // 512 - 1) as i:
                for c in range(2):
                    act.wait_ge(acc_step, 32 + 8 * (c + 1) + 16 * i)
                    split_s(2 * i + c + 2, ar_hi, act_sq, 1.0, c)
                    split(B_DOWN + 2 + c, 2, i)
            for t in range(QT):
                for half in range(2):
                    act.wait_ge(added, 2 * (QT + t) + half + 1)
                    square(Q_X2 + 2 * t + half, x_sb[:, t, 512 * half:512 * half + 512])
                act.wait_ge(gained, t + 1)
                act.wait_ge(rstd_done, BATCH_X2 + t + 1)
                act.activation(fin[:, t, 512:], fin[:, t, 512:], ACT.Copy,
                               scale=rstd[:, Q_X2 + t:Q_X2 + t + 1]).then_inc(out_right, 1)

        @block.vector
        def _(dve):
            def f(ap):
                return ap.bitcast(F32)

            def split(c, per=0, i=0, n=BLK, start=0, stop=None):
                slot, _ = ring(c, per, i)
                stop = n if stop is None else stop
                a = slice(start, stop)
                if start == 0:
                    dve.wait_ge(w_hi_done, c + 1 + per * i)
                ins = dve.tensor_tensor(w_lo[:, slot, a], raw[:, slot, a], f(w_hi[:, slot, a]), ALU.subtract)
                if stop == n:
                    ins.then_inc(w_lo_done, 1)

            def lo(n, per, i, dst, src, hi, bk):
                dve.wait_ge(tile_hi, n + 1 + per * i)
                dve.tensor_tensor(dst, src, f(hi), ALU.subtract).then_inc(tile_done[bk], 1)

            def tp_part(n, dst, src, gain, hi):
                dve.wait_ge(tp_hi, n + 1)
                dve.scalar_tensor_tensor(dst, src, gain, f(hi), ALU.mult, ALU.subtract).then_inc(tp_lo, 1)

            def turned(t, n0, place, dst, gain, hi):
                for k in range(KD):
                    tk = slice(P * t, P * t + P)
                    tp_part(n0 + k, dst[:, k, tk], place(k), gain[:, k:k + 1], hi[:, k, tk])

            def turned_in(n):
                dve.wait_ge(gain_in, 32)
                t, dst, gain, hi = (n, mn_lo, g_mem, mn_hi) if n < MT else (n - MT, h_lo, g_attn, h_hi)
                turned(t, KD * n, lambda k: turned_bank(n, k), dst, gain, hi)

            def mean_sq(a, b, width, done=ms_done):
                dve.wait_ge(sq_done, b)
                dve.tensor_scalar(rstd[:, a:b], sumsq[:, a:b], 1.0 / width, EPS, ALU.mult,
                                  ALU.add).then_inc(done, 1)

            def peak(u, per, i, groups, n, scale, r=None):
                s = u % 2
                dve.wait_ge(s_ready, u + 1 + per * i)
                dve.tensor_reduce(mx[:, s, 0:groups], bank(2 + s, 0, groups * n).rearrange("p (g n) -> p g n", n=n),
                                  AX_X, ALU.max).then_inc(mx_done, 1)
                dve.wait_ge(mx_done, u + 1 + per * i)
                if r is None:
                    dve.tensor_scalar(negm[:, s, 0:groups], mx[:, s, 0:groups], -scale, None,
                                      ALU.mult).then_inc(neg_done, 1)
                    return
                sink = nsinks[:, :, ds(r, 1)]
                dve.scalar_tensor_tensor(negm[:, s:s + 1, :].rearrange("p a g -> p g a"),
                                         mx[:, s:s + 1, :].rearrange("p a g -> p g a"), -scale, sink,
                                         ALU.mult, ALU.min).then_inc(nsk_done, 1)
                dve.wait_ge(nsk_done, u - U_SWA + 1 + per * i)
                dve.tensor_tensor(snk[:, s:s + 1, :].rearrange("p a g -> p g a"),
                                  negm[:, s:s + 1, :].rearrange("p a g -> p g a"), sink,
                                  ALU.subtract).then_inc(neg_done, 1)

            def norm(u, per, i, groups, n, sink=False):
                s = u % 2
                dve.wait_ge(exp_done, u + 1 + per * i)
                den = rsum
                if sink:
                    dve.tensor_tensor(tot[:, s, :], rsum[:, s, :], esnk[:, s, :], ALU.add).then_inc(tot_done, 1)
                    dve.wait_ge(tot_done, u - U_SWA + 1 + per * i)
                    den = tot
                dve.reciprocal(rinv[:, s, 0:groups], den[:, s, 0:groups]).then_inc(rinv_done, 1)
                dve.wait_ge(rinv_done, u + 1 + per * i)
                for g in range(groups):
                    block_p = probs[:, s, g * n:(g + 1) * n]
                    last = dve.tensor_scalar(block_p, block_p, rinv[:, s, g:g + 1], None, ALU.mult)
                last.then_inc(p_done, 1)

            def pt(u, per, i, dst, src, hi):
                dve.wait_ge(pt_hi_done, u + 1 + per * i)
                dve.tensor_tensor(dst, src, f(hi), ALU.subtract).then_inc(pt_lo_done, 1)

            def merge(t0, first, m0=0, m1=KD):
                for m in range(m0, m1):
                    slot, turn = ring(t0 + m, 0, 0)
                    dve.wait_ge(tile_ready, t0 + m + 1)
                    if first:
                        dve.scalar_tensor_tensor(y[:, m, :], gate[:, m, :], 1.0, bank(slot), ALU.add,
                                                 ALU.mult).then_inc(tile_done[slot], 1)
                        continue
                    dve.scalar_tensor_tensor(tmp[:, m % 2, :], gate[:, m, :], 1.0, bank(slot), ALU.add,
                                             ALU.mult).then_inc(tile_done[slot], 1)
                    dve.wait_ge(tile_done[slot], turn + 1)
                    dve.tensor_tensor(y[:, m, :], y[:, m, :], tmp[:, m % 2, :], ALU.add).then_inc(y_done, 1)

            def norm_in(n):
                mean_sq(n, n + 1, D)
                dve.wait_ge(rstd_done, n + 1)
                dve.tensor_scalar(token_rows[n], token_rows[n], rstd[:, n:n + 1], None, ALU.mult).then_inc(xn_done, 1)

            norm_in(0)
            norm_in(1)
            turned_in(0)
            norm_in(2)
            turned_in(1)
            split(0)
            norm_in(3)
            turned_in(2)
            norm_in(4)
            turned_in(3)
            norm_in(5)
            turned_in(4)
            split(1)
            turned_in(5)
            split(2)
            for t in range(MT):
                dve.wait_ge(vm_hi_done, t + 1)
                dve.tensor_tensor(vm_lo[:, t, :], bank(6 + t), f(vm_hi[:, t, :]), ALU.subtract).then_inc(vm_lo_done, 1)
            split(3)
            dve.wait_ge(const_in, 16 * 5)
            dve.tensor_scalar(hb, hb_raw, 0.5, None, ALU.mult).then_inc(small_done, 1)
            dve.tensor_scalar(nsinks, sinks.rearrange("p (g r) -> p g r", g=2), -1.0, None,
                              ALU.mult).then_inc(small_done, 1)
            dve.wait_ge(small_done, 2)
            dve.wait_ge(rel_step, 3)
            rows_r = slice(0, BUCKETS + 1)
            dve.tensor_tensor(rel_lo[rows_r, :], rel[rows_r, :], f(rel_hi[rows_r, :]), ALU.subtract).then_inc(rel_step, 1)

            def bias_rows_of(a, b):
                for n in range(a, b):
                    dve.wait_ge(fbank_ready, n + 1)
                    dve.tensor_scalar(frep[:, n, :], bank(4 + n % 4, 0, TOE), DS ** 0.5, None,
                                      ALU.mult).then_inc(frep_done, 1)

            for h in range(HM):
                t0, u0, b, n0 = T_MEM + 4 * h, U_MEM + 2 * h, B_MEM + 2 + 2 * h, H_MEM + 2 * h
                lo(n0, 0, 0, q_lo[:, h % 2, :], bank(t0 % 2), q_hi[:, h % 2, :], t0 % 2)
                if h == 0:
                    bias_rows_of(0, 4)
                lo(n0 + 1, 0, 0, km_lo, bank((t0 + 1) % 2, 0, M), km_hi, (t0 + 1) % 2)
                if h == 0:
                    bias_rows_of(4, HS)
                for n in range(2):
                    peak(u0 + n, 0, 0, 2, M, DM ** -0.5)
                for n in range(2):
                    norm(u0 + n, 0, 0, 2, M)
                for n in range(2):
                    at = slice(512 * n, 512 * n + 512)
                    pt(u0 + n, 0, 0, pt_lo[:, at], bank(4 + n), pt_hi[:, at])
                split(b + 2)
                split(b + 3)
                dve.wait_ge(o_hi_done, E_MEM + h + 1)
                dve.tensor_tensor(o_lo[:, h, :], bank(6 + h % 2), f(o_hi[:, h, :]),
                                  ALU.subtract).then_inc(o_lo_done, 1)

            bk = T_KVS % 2
            dve.wait_ge(tile_hi, H_KVS + 1)
            dve.tensor_tensor(kz_lo[0:64, 0, :], bank(bk)[0:64, :], f(kz_hi[0:64, 0, :]), ALU.subtract)
            dve.tensor_tensor(kz_lo[64:128, 1, :], bank(bk)[64:128, :], f(kz_hi[64:128, 1, :]),
                              ALU.subtract).then_inc(tile_done[bk], 1)
            dve.wait_ge(rows_out, 16)
            dve.wait_ge(bias_hi_done, 1)
            dve.tensor_tensor(bias_lo, bias_raw.rearrange("p (g r n) -> p g r n", g=2, r=PAIRS), f(bias_hi),
                              ALU.subtract).then_inc(bias_lo_done, 1)
            split(B_KVS + 2)
            dve.wait_ge(vs_hi_done, 1)
            dve.tensor_tensor(v_lo, bank(4).rearrange("p (k n) -> p k n", k=4), f(v_hi),
                              ALU.subtract).then_inc(vs_lo_done, 1)
            merge(T_WO_MEM, True, 0, 5)
            split(B_WO_MEM + 2)
            merge(T_WO_MEM, True, 5)
            split(B_WO_MEM + 3)

            with dve.Fori(0, PAIRS // 2) as i:
                for c in range(2):
                    t0, u0, b = T_SWA + 3 * c, U_SWA + 4 * c, B_SWA + 2 * c
                    lo(H_SWA + c, 2, i, q_lo[:, c, :], bank(t0 % 2), q_hi[:, c, :], t0 % 2)

                    def pk(n):
                        peak(u0 + n, 8, i, 2, P if n == 0 else 2 * P, DS ** -0.5, 2 * i + c)

                    def nm(n):
                        norm(u0 + n, 8, i, 2, P if n == 0 else 2 * P, True)

                    def p(n):
                        z = 256 if n == 0 else 0
                        at = slice(512 * n + z, 512 * n + 512)
                        pt(u0 + n, 8, i, pt_lo[:, at], bank(4 + n % 2, z, 512), pt_hi[:, at])

                    pk(0)
                    pk(1)
                    nm(0)
                    nm(1)
                    p(0)
                    pk(2)
                    nm(2)
                    p(1)
                    pk(3)
                    nm(3)
                    p(2)
                    p(3)
                    split(b + 2, 4, i)
                    split(b + 3, 4, i, n=N_GATE if c == 0 else N_MLAP)
                    dve.wait_ge(o_hi_done, E_SWA + c + 1 + 2 * i)
                    for g in range(2):
                        r = slice(64 * g, 64 * g + 64)
                        last = dve.tensor_tensor(o_lo[r, ds(2 * i + c, 1), :],
                                                 bank(6 + g)[r, :].rearrange("p (m n) -> p m n", m=1),
                                                 f(o_hi[r, ds(2 * i + c, 1), :]), ALU.subtract)
                    last.then_inc(o_lo_done, 1)

            split(B_MLAP + 2)
            split(B_MLAP + 3)
            merge(T_WO_SWA, False, 0, 2)
            dve.wait_ge(pre_copied, QT)
            t1, t2 = kvq[:, :, 384:400], kvq[:, :, 400:416]
            for n, (a, b) in enumerate(((t1, cos_t), (t2, sin_t), (t2, cos_t), (t1, sin_t))):
                dve.tensor_tensor(rtmp[:, n, :, :], a, b, ALU.mult).then_inc(kr_step, 1)
            dve.wait_ge(kr_step, 4)
            dve.wait_ge(nhalf_done, 2)
            dve.tensor_tensor(kpad[:, :, 64:80], rtmp[:, 0, :, :], rtmp[:, 1, :, :], ALU.subtract).then_inc(kr_step, 1)
            dve.tensor_tensor(kpad[:, :, 80:96], rtmp[:, 2, :, :], rtmp[:, 3, :, :], ALU.add).then_inc(kr_step, 1)
            mean_sq(Q_CQ, Q_CKV, QL)
            mean_sq(Q_CKV, Q_X1, KVL)
            merge(T_WO_SWA, False, 2, 3)
            dve.wait_ge(rstd_done, BATCH_MLA + 1)
            for t in range(QT):
                for n, (a, b) in enumerate(((0, QL), (QL, QL + KVL))):
                    col_n = (Q_CKV if n else Q_CQ) + t
                    dve.tensor_scalar(kvq[:, t, a:b], kvq[:, t, a:b], rstd[:, col_n:col_n + 1], None,
                                      ALU.mult).then_inc(xn_done, 1)
            merge(T_WO_SWA, False, 3, 4)
            split(B_MLA, n=N_A)
            for k in range(2):
                tp_part(N_MLA + k, cq_lo[:, k, :], bank(2 + k), g_q[:, k:k + 1], cq_hi[:, k, :])
            tp_part(N_MLA + 2, ckv_lo, bank(4), g_kv[:, 0:1], ckv_hi)
            dve.wait_ge(tp_hi, N_MLA + 4)
            for c in range(2):
                last = dve.tensor_tensor(ka_lo[64:96, c, :], bank(5)[64:96, :], f(ka_hi[64:96, c, :]), ALU.subtract)
            last.then_inc(tp_lo, 1)

            def key(t, n, c, per=0, i=0):
                lo(n, per, i, ka_lo[0:64, c, :], bank(t % 2)[0:64, :], ka_hi[0:64, c, :], t % 2)

            def query(t, n, c, per=0, i=0, before=0):
                rows = bank(t % 2)[64:96, :]
                dve.wait_ge(tile_hi, n + 1 + per * i)
                wait(dve, q_done, before)
                dve.tensor_tensor(rope_b[64:96, :], rows, cos_f[64:96, :], ALU.mult)
                dve.stream_shuffle(rope_a[64:96, :], rows, [(p + 16) % 32 for p in range(32)]).then_inc(rope_step, 1)
                lo(n, per, i, q_lo[0:64, c, :], bank(t % 2)[0:64, :], q_hi[0:64, c, :], t % 2)

            def rotary(n, c, per=0, i=0):
                dve.wait_ge(tile_hi, n + 1 + per * i)
                dve.tensor_tensor(q_lo[64:96, c, :], rope_b[64:96, :], f(q_hi[64:96, c, :]),
                                  ALU.subtract).then_inc(q_done, 1)

            merge(T_WO_SWA, False, 4)
            split(B_MLA + 1, n=N_GATE)
            key(T_MLA, H_MLA, 0)
            query(T_MLA + 1, H_MLA + 1, 0)

            def two_heads(i, final=False):
                t0, u0, b, n0 = T_MLA + 2, U_MLA, B_MLA, H_MLA + 2
                for n in range(2):
                    bk = (t0 + n) % 2
                    lo(n0 + n, 8, i, v_lo[:, 2 * n:2 * n + 2, :],
                       bank(bk, 0, 256).rearrange("p (k n) -> p k n", k=2), v_hi[:, 2 * n:2 * n + 2, :], bk)
                rotary(n0 + 2, 0, 8, i)
                key(t0 + 2, n0 + 3, 1, 8, i)
                query(t0 + 3, n0 + 4, 1, 8, i, 1 + 2 * i)

                def pk(c, n):
                    peak(u0 + 4 * c + n, 8, i, 1, P * (n + 1), QK ** -0.5)

                def nm(c, n):
                    norm(u0 + 4 * c + n, 8, i, 1, P * (n + 1))

                def p(c, n):
                    at = (slice(None), slice(0, n + 1), slice(P * n, P * n + P))
                    pt(u0 + 4 * c + n, 8, i, pt_lo.rearrange("p (k q) -> p k q", k=4)[at],
                       bank(4 + n % 2, 0, P * (n + 1)).rearrange("p (k q) -> p k q", q=P),
                       pt_hi.rearrange("p (k q) -> p k q", k=4)[at])

                def o(c):
                    r = slice(64 * c, 64 * c + 64)
                    dve.wait_ge(o_hi_done, E_MLA + c + 1 + 2 * i)
                    dve.tensor_tensor(o_lo[r, ds(i, 1), :], bank(6 + c)[r, :].rearrange("p (m n) -> p m n", m=1),
                                      f(o_hi[r, ds(i, 1), :]), ALU.subtract).then_inc(o_lo_done, 1)

                n_a = BLK if final else N_A
                pk(0, 0)
                pk(0, 1)
                nm(0, 0)
                nm(0, 1)
                p(0, 0)
                pk(0, 2)
                nm(0, 2)
                rotary(n0 + 5, 1, 8, i)
                p(0, 1)
                pk(0, 3)
                nm(0, 3)
                p(0, 2)
                p(0, 3)
                pk(1, 0)
                pk(1, 1)
                nm(1, 0)
                nm(1, 1)
                split(b + 2, 2, i, n=n_a, stop=n_a // 2)
                p(1, 0)
                pk(1, 2)
                nm(1, 2)
                p(1, 1)
                pk(1, 3)
                nm(1, 3)
                o(0)
                split(b + 2, 2, i, n=n_a, start=n_a // 2)
                p(1, 2)
                p(1, 3)
                if not final:
                    key(t0 + 6, n0 + 6, 0, 8, i)
                    query(t0 + 7, n0 + 7, 0, 8, i, 2 + 2 * i)
                    split(b + 3, 2, i, n=N_GATE)
                o(1)
                if final:
                    split(b + 3, 2, i)

            with dve.Fori(0, HA // 2 - 1) as i:
                two_heads(i)
            two_heads(HA // 2 - 1, True)

            def split_s(n, ring_hi, ring_lo, src, scale, count, slot):
                dve.wait_ge(s_hi_done, count)
                part_n = src[:, ds(1024 * n, 1024)]
                if scale == 1.0:
                    ins = dve.tensor_tensor(ring_lo[:, slot, :], part_n, f(ring_hi[:, slot, :]), ALU.subtract)
                else:
                    ins = dve.scalar_tensor_tensor(ring_lo[:, slot, :], part_n, scale, f(ring_hi[:, slot, :]),
                                                   ALU.mult, ALU.subtract)
                ins.then_inc(s_lo_done, 1)

            merge(T_WO_MLA, False, 0, 4)
            dve.wait_ge(y_done, KD + 4)
            split_s(0, yr_hi, yr_lo, ybuf, 0.5, 1, 0)
            merge(T_WO_MLA, False, 4, 5)
            split(B_WO_MLA + 2)
            merge(T_WO_MLA, False, 5, 6)
            split_s(1, yr_hi, yr_lo, ybuf, 0.5, 2, 1)
            merge(T_WO_MLA, False, 6)
            split(B_WO_MLA + 3)
            dve.wait_ge(y_done, 2 * KD)
            for n in range(3):
                if n < 2:
                    split_s(n + 2, yr_hi, yr_lo, ybuf, 0.5, n + 3, n)
                split(B_WOUT + n + 2)

            def add(t, steps, scale=None):
                for half in range(2):
                    dve.wait_ge(acc_step, steps + 2 * t + half + 1)
                    dst, src = x_sb[:, t, 512 * half:512 * half + 512], bank(2 * t + half)
                    if scale is None:
                        ins = dve.tensor_tensor(dst, dst, src, ALU.add)
                    else:
                        ins = dve.scalar_tensor_tensor(dst, src, scale, dst, ALU.mult, ALU.add)
                    ins.then_inc(added, 1)

            def turned_again(t):
                turned(t, N_H2 + KD * t, lambda k: turned_x(t, k), h_lo, g_mlp, h_hi)

            dve.wait_ge(x_again, 16 * QT)
            for t in range(QT):
                add(t, 24)
                if t > 0:
                    turned_again(t - 1)
            turned_again(QT - 1)
            split(B_UP + 1)
            mean_sq(Q_X1, Q_X2, D, inv_step)
            dve.wait_ge(inv_step, 1)
            dve.reciprocal(rstd[:, Q_X1:Q_X2], rstd[:, Q_X1:Q_X2]).then_inc(inv_step, 1)

            def up(i):
                for c in range(4):
                    slot, turn = ring(T_UP + c, 4, i)
                    dve.wait_ge(tile_done[slot], turn + 1)
                    dve.tensor_tensor(act_sq[:, ds(2048 * i + 512 * c, 512)], relu[:, c % 2, :], relu[:, c % 2, :],
                                      ALU.mult).then_inc(sq_act, 1)
                    if c % 2:
                        split(B_UP + 2 + c // 2, 2, i)

            up(0)
            with dve.Fori(1, FF // 512 - 1) as i:
                up(i)
            for n in range(2):
                split_s(n, ar_hi, ar_lo, act_sq, 1.0, 5 + n, n)
            up(FF // 512 - 1)
            dve.wait_ge(sq_act, FF // P)
            with dve.Fori(0, FF // 512 - 1) as i:
                for c in range(2):
                    split_s(2 * i + c + 2, ar_hi, ar_lo, act_sq, 1.0, 7 + c + 2 * i, c)
                    split(B_DOWN + 2 + c, 2, i)
            dve.wait_ge(fgain_in, 16)
            dve.wait_ge(inv_step, 2)
            for t in range(QT):
                add(t, 32 + 120, rstd[:, Q_X1 + t:Q_X1 + t + 1])
                c = Q_X2 + t
                dve.wait_ge(sq_done, Q_X2 + 2 * t + 1)
                dve.tensor_scalar(rstd[:, c:c + 1], sumsq[:, c + t:c + t + 1], 1.0 / D, EPS, ALU.mult,
                                  ALU.add).then_inc(ms_done, 1)
                dve.wait_ge(added, 2 * (QT + t) + 2)
                dve.tensor_tensor(fin[:, t, :], x_sb[:, t, :], fgain, ALU.mult).then_inc(gained, 1)
                dve.wait_ge(sq_done, Q_X2 + 2 * t + 2)
                dve.wait_ge(ms_done, TURNS + 3 + 2 * t)
                dve.scalar_tensor_tensor(rstd[:, c:c + 1], sumsq[:, c + t + 1:c + t + 2], 1.0 / D, rstd[:, c:c + 1],
                                         ALU.mult, ALU.add).then_inc(ms_done, 1)
                dve.wait_ge(rstd_done, BATCH_X2 + t + 1)
                dve.tensor_scalar(fin[:, t, 0:512], fin[:, t, 0:512], rstd[:, c:c + 1], None,
                                  ALU.mult).then_inc(out_left, 1)

        @block.tensor
        def _(pe):
            def need(c, per=0, i=0):
                pe.wait_ge(w_lo_done, c + 1 + per * i)
                return c % 2

            def bank_of(c, per=0, i=0):
                slot, turn = ring(c, per, i)
                wait(pe, tile_done[slot], turn)
                return slot

            def have(c, per=0, i=0):
                slot, turn = ring(c, per, i)
                pe.wait_ge(tile_done[slot], turn + 1)

            def mm3(dst, a, b, first, last):
                pe.matmul(dst, a[0], b[1], start=first, stop=False, skip_group_check=True)
                pe.matmul(dst, a[1], b[0], start=False, stop=False, skip_group_check=True)
                return pe.matmul(dst, a[0], b[0], start=False, stop=last, skip_group_check=True)

            def wpair(slot, at, k, n, c0=0, cn=P):
                return w(w_hi, slot, at, k, n, c0, cn), w(w_lo, slot, at, k, n, c0, cn)

            def hpair(k):
                return h_hi[:, k, :], h_lo[:, k, :]

            def project(bk, slot, at, k0=0, k1=KD, n=P, c0=0, split_to=None):
                for k in range(k0, k1):
                    if split_to is not None:
                        pe.wait_ge(tp_lo, split_to + k + 1)
                    last = mm3(bank(bk), wpair(slot, at, k, n, c0), hpair(k), k == 0, k == KD - 1)
                if k1 == KD:
                    last.then_inc(tile_ready, 1)

            def t_bank(u, per, i):
                pe.wait_ge(p_done, u + 1 + per * i)
                wait(pe, pt_lo_done, u - 1 + per * i)

            def s_bank(u, per, i):
                wait(pe, exp_done, u - 1 + per * i)

            def turn(src, banks, place):
                for j in range(banks):
                    for k in range(j, KD, banks):
                        last = pe.transpose(place(k), src[:, P * k:P * k + P], ident)
                    last.then_inc(tp_ready, 1)

            def turn_in(n):
                pe.wait_ge(xn_done, n + 1)
                wait(pe, tp_lo, KD * (n - 1))
                turn(token_rows[n], 3, lambda k: turned_bank(n, k))

            def mem_values(half, t):
                slot = need(B_MEM + half)
                pe.wait_ge(tp_lo, KD * (t + 1))
                tk = slice(P * t, P * t + P)
                for k in range(4):
                    kk = 4 * half + k
                    last = mm3(bank(6 + t), (mn_hi[:, kk, tk], mn_lo[:, kk, tk]), wpair(slot, 0, k, 512, 0, 512),
                               kk == 0, kk == KD - 1)
                if half == 1:
                    last.then_inc(vm_ready, 1)

            pe.wait_ge(ident_in, 16)
            turn_in(0)
            turn_in(1)
            turn_in(2)
            mem_values(0, 0)
            turn_in(3)
            mem_values(0, 1)
            turn_in(4)
            turn_in(5)
            mem_values(1, 0)
            mem_values(1, 1)

            def out_proj(b, t0, heads, newest, m0=0, m1=KD, between=None):
                def rows_of(m, slot, bk, k0, k1):
                    for k in range(k0, k1):
                        last = mm3(bank(bk), wpair(slot, 0, k, 512, P * (m % 4)), (o_hi[:, k, :], o_lo[:, k, :]),
                                   k == 0, k == 3)
                    if k1 == 4:
                        last.then_inc(tile_ready, 1)

                if m0 == 0:
                    pe.wait_ge(o_lo_done, heads - newest)
                    slot = need(b)
                    for m in range(2):
                        rows_of(m, slot, bank_of(t0 + m), 0, 3)
                    pe.wait_ge(o_lo_done, heads)
                    for m in range(2):
                        rows_of(m, slot, (t0 + m) % 2, 3, 4)
                    if between is not None:
                        between()
                for m in range(max(m0, 2), m1):
                    rows_of(m, need(b + m // 4), bank_of(t0 + m), 0, 4)

            def bias_row(a, b):
                pe.wait_ge(rel_step, 4)
                for n in range(a, b):
                    if n >= 4:
                        pe.wait_ge(frep_done, n - 3)
                    for j, part_r in enumerate((rel_lo, rel_hi)):
                        last = pe.matmul(bank(4 + n % 4, 0, TOE),
                                         part_r[0:BUCKETS + 1, n:n + 1].to_broadcast([BUCKETS + 1, P]),
                                         toe_r[0:BUCKETS + 1, :], start=j == 0, stop=j == 1, skip_group_check=True)
                    last.then_inc(fbank_ready, 1)

            for h in range(HM):
                t0, u0, b, e = T_MEM + 4 * h, U_MEM + 2 * h, B_MEM + 2 + 2 * h, E_MEM + h
                slot = need(b)
                project(bank_of(t0), slot, 0, split_to=KD * (TURNS - 1) if h == 0 else None)
                if h == 0:
                    bias_row(0, 4)
                bk = bank_of(t0 + 1)
                for k in range(KD):
                    last = mm3(bank(bk, 0, M), wpair(slot, 1024, k, P), (mn_hi[:, k, :], mn_lo[:, k, :]),
                               k == 0, k == KD - 1)
                last.then_inc(tile_ready, 1)
                if h == 0:
                    bias_row(4, HS)
                slot, bk = need(b + 1), bank_of(t0 + 2)
                project(bk, slot, 0, 0, 3)
                have(t0 + 1)
                for n in range(2):
                    s_bank(u0 + n, 0, 0)
                    for t in range(2):
                        tk = slice(P * (2 * n + t), P * (2 * n + t + 1))
                        last = mm3(bank(2 + n, M * t, M * t + M), (q_hi[:, h % 2, tk], q_lo[:, h % 2, tk]),
                                   (km_hi, km_lo), True, True)
                    last.then_inc(s_ready, 1)
                project(bk, slot, 0, 3, 8)
                bk = bank_of(t0 + 3)
                project(bk, slot, 1024, 0, 1)
                if h == 0:
                    pe.wait_ge(frep_done, HS)
                for n in range(2):
                    t_bank(u0 + n, 0, 0)
                    for k in range(2):
                        for t in range(2):
                            last = pe.transpose(bank(4 + n, 256 * k + P * t, 256 * k + P * t + P),
                                                probs[:, n, M * t + P * k:M * t + P * k + P], ident)
                    last.then_inc(t_ready, 1)
                project(bk, slot, 1024, 1, 8)
                pe.wait_ge(pt_lo_done, u0 + 2)
                pe.wait_ge(vm_lo_done, MT)
                wait(pe, o_lo_done, e)
                ptk = [buf[:, 0:1024].rearrange("p (u k q) -> p k u q", u=2, k=2) for buf in (pt_hi, pt_lo)]
                for k in range(2):
                    last = mm3(bank(6 + h % 2).rearrange("p (u q) -> p u q", u=2),
                               (vm_hi[:, k, DM * h:DM * h + DM], vm_lo[:, k, DM * h:DM * h + DM]),
                               [a[:, k, :, :] for a in ptk], k == 0, k == 1)
                last.then_inc(o_ready, 1)

            slot = need(B_KVS)
            project(bank_of(T_KVS), slot, 0)
            project(bank_of(T_KVS + 1), slot, 1024)

            def turn_values():
                pe.wait_ge(tile_done[(T_KVS + 1) % 2], T_KVS // 2 + 1)
                pe.wait_ge(pt_lo_done, U_SWA)
                for t in range(QT):
                    last = pe.transpose(bank(4, P * t, P * t + P), tmp[:, 0, P * t:P * t + P], ident)
                last.then_inc(vs_turned, 1)

            out_proj(B_WO_MEM, T_WO_MEM, E_SWA, 1, between=turn_values)
            pe.wait_ge(bias_lo_done, 1)
            pe.wait_ge(kz_zero, 4)
            pe.wait_ge(idr_done, 2)

            with pe.Fori(0, PAIRS // 2) as i:
                for c in range(2):
                    t0, u0, b = T_SWA + 3 * c, U_SWA + 4 * c, B_SWA + 2 * c
                    slot = need(b, 4, i)
                    project(bank_of(t0, 6, i), slot, 0)
                    bk = bank_of(t0 + 1, 6, i)
                    project(bk, slot, 1024, 0, 2)
                    have(t0, 6, i)

                    def scores(n):
                        s_bank(u0 + n, 8, i)
                        wd = P if n == 0 else 2 * P
                        k0 = max(P * (n - 1), 0)
                        dst = bank(2 + n % 2, 0, 2 * wd).rearrange("p (g n) -> p g n", g=2)
                        for j, buf in enumerate((bias_lo, bias_hi)):
                            pe.matmul(dst, ident_r, buf[:, :, ds(2 * i + c, 1), 2 * P - wd:2 * P]
                                      .rearrange("p g r n -> p g (r n)"), start=j == 0, stop=False,
                                      skip_group_check=True)
                        tk = slice(P * n, P * n + P)
                        mm3(dst, (q_hi[:, c, tk], q_lo[:, c, tk]), (kz_hi[:, :, k0:k0 + wd], kz_lo[:, :, k0:k0 + wd]),
                            False, True).then_inc(s_ready, 1)

                    def turn_p(n):
                        t_bank(u0 + n, 8, i)
                        wd = P if n == 0 else 2 * P
                        for s in range(1 if n == 0 else 0, 2):
                            for g in range(2):
                                a = g * wd + (0 if n == 0 else P * s)
                                last = pe.transpose(bank(4 + n % 2, 256 * s + P * g, 256 * s + P * g + P),
                                                    probs[:, n % 2, a:a + P], ident)
                        last.then_inc(t_ready, 1)

                    scores(0)
                    scores(1)
                    project(bk, slot, 1024, 2, 6)
                    turn_p(0)
                    scores(2)
                    project(bk, slot, 1024, 6, 8)
                    turn_p(1)
                    scores(3)
                    slot, bk = need(b + 1, 4, i), bank_of(t0 + 2, 6, i)
                    project(bk, slot, 0, 0, 3)
                    turn_p(2)
                    project(bk, slot, 0, 3, 5)
                    turn_p(3)
                    project(bk, slot, 0, 5, 8)
                    pe.wait_ge(pt_lo_done, u0 + 4 + 8 * i)
                    pe.wait_ge(o_lo_done, E_SWA + c + 2 * i)
                    pe.wait_ge(vs_lo_done, 1)
                    ptg = [buf.rearrange("p (m g q) -> p g m q", g=2, q=P) for buf in (pt_hi, pt_lo)]
                    for k in range(QT):
                        n = 2 if k < QT - 1 else 1
                        for g in range(2):
                            last = mm3(bank(6 + g, P * k, P * (k + n)).rearrange("p (m q) -> p m q", q=P),
                                       (v_hi[:, k, :], v_lo[:, k, :]),
                                       [a[:, g, 2 * k + 1:2 * k + 1 + n, :] for a in ptg], k == 0, k == QT - 1)
                    last.then_inc(o_ready, 1)

            pe.wait_ge(exp_done, U_MLA)
            pe.wait_ge(pt_lo_done, U_MLA)
            for half in range(2):
                slot = need(B_MLAP + half)
                for t in range(QT):
                    tk = slice(P * t, P * t + P)
                    for k in range(4):
                        kk = 4 * half + k
                        last = mm3(bank(2 + t, 0, 416), (h_hi[:, kk, tk], h_lo[:, kk, tk]),
                                   wpair(slot, 0, k, 416, 0, 416), kk == 0, kk == KD - 1)
                    if half == 1 or t == QT - 1:
                        last.then_inc(pre_ready, 1)
            out_proj(B_WO_SWA, T_WO_SWA, E_MLA, 1, 0, 4)
            pe.wait_ge(pre_copied, QT)
            pe.wait_ge(xn_done, TURNS + 2 * QT)
            pe.wait_ge(kr_step, 6)
            for k in range(3):
                for t in range(QT):
                    last = pe.transpose(bank(2 + k, P * t, P * t + P), kvq[:, t, P * k:P * k + P], ident)
                last.then_inc(tp_ready, 1)
            for t in range(QT):
                last = pe.transpose(bank(5, P * t, P * t + P)[0:QK, :], kpad[:, t, :], ident)
            last.then_inc(tp_ready, 1)
            out_proj(B_WO_SWA, T_WO_SWA, E_MLA, 1, 4)
            pe.wait_ge(tp_lo, N_H2)

            def key(t, slot, c, per=0, i=0):
                mm3(bank(bank_of(t, per, i)), wpair(slot, 4 * QK, c, P), (ckv_hi, ckv_lo), True,
                    True).then_inc(tile_ready, 1)

            def query(t, slot, c, per=0, i=0):
                bk = bank_of(t, per, i)
                for k in range(2):
                    last = mm3(bank(bk)[0:QK, :], wpair(slot, 0, k, 2 * QK, QK * c, QK),
                               (cq_hi[:, k, :], cq_lo[:, k, :]), k == 0, k == 1)
                last.then_inc(tile_ready, 1)

            slot = need(B_MLA)
            key(T_MLA, slot, 0)
            query(T_MLA + 1, slot, 0)

            def two_heads(i, final=False):
                t0, u0, b = T_MLA + 2, U_MLA, B_MLA
                slot = b % 2
                vw = [buf[:, slot, 4 * QK:4 * QK + 2 * P].rearrange("p (h t c) -> p h t c", h=2, t=2)[:, :, 1, :]
                      for buf in (w_hi, w_lo)]
                for n in range(2):
                    bk = bank_of(t0 + n, 8, i)
                    for k in range(2):
                        tk = slice(P * (2 * n + k), P * (2 * n + k + 1))
                        last = mm3(bank(bk, P * k, P * k + P).rearrange("p (h c) -> p h c", h=2),
                                   (ckv_hi[:, tk], ckv_lo[:, tk]), vw, True, True)
                    last.then_inc(tile_ready, 1)
                key(t0 + 2, slot, 1, 8, i)
                query(t0 + 3, slot, 1, 8, i)

                def scores(c, n):
                    s_bank(u0 + 4 * c + n, 8, i)
                    tk, kw = slice(P * n, P * n + P), P * (n + 1)
                    mm3(bank(2 + n % 2, 0, kw), (q_hi[0:QK, c, tk], q_lo[0:QK, c, tk]),
                        (ka_hi[0:QK, c, 0:kw], ka_lo[0:QK, c, 0:kw]), True, False)
                    pe.matmul(bank(2 + n % 2, P * n, P * n + P), ident_r, mask_r, start=False, stop=True,
                              skip_group_check=True).then_inc(s_ready, 1)

                def turn_p(c, n):
                    t_bank(u0 + 4 * c + n, 8, i)
                    for k in range(n + 1):
                        last = pe.transpose(bank(4 + n % 2, P * k, P * k + P), probs[:, n % 2, P * k:P * k + P], ident)
                    last.then_inc(t_ready, 1)

                def values(c):
                    pe.wait_ge(pt_lo_done, u0 + 4 * c + 4 + 8 * i)
                    pe.wait_ge(o_lo_done, E_MLA + c + 2 * i)
                    for k in range(QT):
                        at = slice(512 * k + P * k, 512 * k + 512)
                        last = mm3(bank(6 + c, P * k, 512), (v_hi[:, k, :], v_lo[:, k, :]), (pt_hi[:, at], pt_lo[:, at]),
                                   k == 0, k == QT - 1)
                    last.then_inc(o_ready, 1)

                bk, at = bank_of(t0 + 4, 8, i), N_A - D
                project(bk, slot, at, 0, 1)
                pe.wait_ge(q_done, 2 * i + 1)
                scores(0, 0)
                scores(0, 1)
                project(bk, slot, at, 1, 3)
                turn_p(0, 0)
                scores(0, 2)
                project(bk, slot, at, 3, 4)
                turn_p(0, 1)
                scores(0, 3)
                project(bk, slot, at, 4, 5)
                turn_p(0, 2)
                project(bk, slot, at, 5, 8)
                turn_p(0, 3)
                pe.wait_ge(q_done, 2 * i + 2)
                scores(1, 0)
                scores(1, 1)
                slot, bk = need(b + 1, 2, i), bank_of(t0 + 5, 8, i)
                project(bk, slot, 0, 0, 1)
                values(0)
                turn_p(1, 0)
                scores(1, 2)
                project(bk, slot, 0, 1, 3)
                turn_p(1, 1)
                scores(1, 3)
                project(bk, slot, 0, 3, 5)
                turn_p(1, 2)
                project(bk, slot, 0, 5, 7)
                turn_p(1, 3)
                project(bk, slot, 0, 7, 8)
                if not final:
                    slot = need(b + 2, 2, i)
                    key(t0 + 6, slot, 0, 8, i)
                    query(t0 + 7, slot, 0, 8, i)
                values(1)

            with pe.Fori(0, HA // 2 - 1) as i:
                two_heads(i)
            two_heads(HA // 2 - 1, True)

            out_proj(B_WO_MLA, T_WO_MLA, E_END, 2)

            def accumulate(c, per, i, s_hi, s_lo, s_count, first=False, last=False, after=lambda t: None,
                           tiles=0):
                slot = need(c, per, i)
                pe.wait_ge(s_lo_done, s_count)
                n = (c - B_WOUT) % 2
                for t in [1, 2, 3, 0] if tiles else range(QT):
                    if tiles and t == 0:
                        pe.wait_ge(tile_done[0], tiles)
                        pe.wait_ge(tile_done[1], tiles)
                    for half in range(2):
                        for k in range(2):
                            a = slice(512 * k + P * t, 512 * k + P * t + P)
                            ins = mm3(bank(2 * t + half), (s_hi[:, n, a], s_lo[:, n, a]),
                                      wpair(slot, 0, k, D, 512 * half, 512), first and k == 0, last and k == 1)
                        ins.then_inc(acc_step, 1)
                    after(t)

            for n in range(D // 256 - 1):
                accumulate(B_WOUT + n, 0, 0, yr_hi, yr_lo, n + 1, n == 0, tiles=T_UP // 2 if n == 0 else 0)

            def turn_x(t):
                pe.wait_ge(added, 2 * t + 2)
                turn(x_sb[:, t, :], 2, lambda k: turned_x(t, k))

            accumulate(B_UP - 1, 0, 0, yr_hi, yr_lo, D // 256, last=True, after=lambda t: t > 0 and turn_x(t - 1))
            turn_x(QT - 1)

            def up(i, first=False):
                for c in range(2):
                    slot = need(B_UP + c, 2, i)
                    for m in range(2):
                        project(bank_of(T_UP + 2 * c + m, 4, i), slot, 0, n=256, c0=P * m,
                                split_to=N_H2 + 3 * KD if first and not c and not m else None)

            up(0, True)
            with pe.Fori(1, FF // 512) as i:
                up(i)
            for c in range(2):
                accumulate(B_DOWN + c, 0, 0, ar_hi, ar_lo, 5 + c, c == 0, tiles=T_UP // 2 + FF // 256 if c == 0 else 0)
            with pe.Fori(1, FF // 512 - 1) as i:
                for c in range(2):
                    accumulate(B_DOWN + c, 2, i, ar_hi, ar_lo, 5 + c + 2 * i)
            for c in range(2):
                accumulate(B_END - 2 + c, 0, 0, ar_hi, ar_lo, 5 + FF // 256 - 2 + c, last=c == 1)


def constants():
    con = np.zeros((P, C_END), np.float32)
    con[:, C_ID:C_ID + P] = np.eye(P)
    con[:, C_MASK:C_MASK + P] = np.where(np.arange(P)[None, :] <= np.arange(P)[:, None], 0.0, NEG)
    pos = np.arange(S, dtype=np.float32)
    inv = (1.0 / (np.float32(10000.0) ** (np.arange(0, ROPE, 2, dtype=np.float32) / ROPE))).astype(np.float32)
    ang = pos[:, None] * inv[None, :]
    cos, sin = np.cos(ang), np.sin(ang)
    con[:, C_COST:C_COST + 64] = cos.reshape(QT, P, 16).transpose(1, 0, 2).reshape(P, 64)
    con[:, C_SINT:C_SINT + 64] = sin.reshape(QT, P, 16).transpose(1, 0, 2).reshape(P, 64)
    con[64:80, C_COS:C_COS + S] = con[80:96, C_COS:C_COS + S] = cos.T
    con[64:80, C_SIN:C_SIN + S] = -sin.T
    con[80:96, C_SIN:C_SIN + S] = sin.T
    dist = 2 * P - 1 - np.arange(TOE)
    inside = (dist >= 0) & (dist < P)
    n = np.maximum(dist, 1)
    exact = BUCKETS // 2
    large = exact + (np.log(n.astype(np.float32) / exact) / np.float32(np.log(P / exact))
                     * (BUCKETS - exact)).astype(np.int32)
    bucket = np.where(dist < exact, np.maximum(dist, 0), np.minimum(large, BUCKETS - 1))
    toe = np.zeros((BUCKETS + 1, TOE), np.float32)
    toe[0:BUCKETS, 0:TOE] = (bucket[None, :] == np.arange(BUCKETS)[:, None]) & inside[None, :]
    toe[BUCKETS] = np.where(inside, 0.0, NEG / DS ** 0.5)
    return con, toe


_INS = ["x", "mem", "rel_bias", "attn_norm", "mem_norm", "w_in", "b_gate", "mla_q_norm", "w_uq", "mla_kv_norm",
        "w_ukv", "attn_sinks", "w_mem_kv", "w_o_mla", "w_o_swa", "w_o_mem", "w_out", "mlp_norm", "w_up", "w_down",
        "final_norm"]


def kernel(**inputs):
    import concourse.bacc as _bacc
    from concourse.bass_utils import run_bass_kernel_spmd as _run

    nc = _bacc.Bacc("TRN2", target_bir_lowering=False, num_devices=1)
    given = {name: np.ascontiguousarray(inputs[name]) for name in _INS}
    given["consts"], given["toeplitz"] = constants()
    arrays, args = {}, []
    for name, a in given.items():
        arrays[f"in_{name}_dram"] = a
        args.append(nc.dram_tensor(f"in_{name}_dram", a.shape, mybir.dt.from_np(a.dtype), kind="ExternalInput").ap())
    args.append(nc.dram_tensor("out_0_dram", (1, S, D), F32, kind="ExternalOutput").ap())
    hybrid_layer(nc, *args)
    r = _run(nc, [arrays], core_ids=[0])
    return r.results[0]["out_0_dram"]
```

```python
from contextlib import ExitStack

import numpy as np

import concourse.bass as bass
from concourse import mybir

F32 = mybir.dt.float32
F32R = mybir.dt.float32r
ALU = mybir.AluOpType
ACT = mybir.ActivationFunctionType
AX_X = mybir.AxisListType.X
ds = bass.ds

P = 128
D = 1024
S = 512
M = 256
KD = D // P
QT = S // P
FF = 4 * D
EPS = 1e-6
NEG = -(2.0 ** 100)
HM, DM = 4, 128
HS, DS = 8, 64
HA, NOPE, ROPE, DV = 8, 64, 32, 64
QK = NOPE + ROPE
QL, KVL = 256, 128
PAIRS = HS // 2
BUCKETS = 32
TOE = 3 * P

COL_KV = QL
COL_QS = COL_KV + KVL + ROPE
COL_KS = COL_QS + HS * DS
COL_QM = COL_KS + 2 * 2 * DS
COL_G = COL_QM + HM * DM
MLA, SWA, MEM = range(3)

BLK = 2048
N_MLAP, N_A, N_GATE = 4 * 416, 2 * 2 * QK + 2 * P + D, D
SHARES = {1: (48,), 2: (16, 32), 3: (16, 16, 16)}

B_MEM = 0
B_KVS = B_MEM + 2 + 2 * HM
B_WO_MEM = B_KVS + 1
B_SWA = B_WO_MEM + 2
B_MLAP = B_SWA + 2 * PAIRS
B_WO_SWA = B_MLAP + 2
B_MLA = B_WO_SWA + 2
B_WO_MLA = B_MLA + HA
B_WOUT = B_WO_MLA + 2
B_UP = B_WOUT + D // 256
B_DOWN = B_UP + FF // 256
B_END = B_DOWN + FF // 256

T_MEM = 0
T_KVS = T_MEM + 4 * HM
T_WO_MEM = T_KVS + 2
T_SWA = T_WO_MEM + KD
T_WO_SWA = T_SWA + 3 * PAIRS
T_MLA = T_WO_SWA + KD
T_WO_MLA = T_MLA + 3 * HA
T_UP = T_WO_MLA + KD

H_MEM = 0
H_KVS = 2 * HM
H_SWA = H_KVS + 1
H_MLA = H_SWA + PAIRS

U_MEM = 0
U_SWA = 2 * HM
U_MLA = U_SWA + QT * PAIRS
E_MEM, E_SWA, E_MLA = 0, HM, HM + PAIRS
E_END = E_MLA + HA

MT = M // P
TURNS = MT + QT

R_MLA, R_H2, R_END = np.cumsum([3 * TURNS, 4, 4 * QT - 2]).tolist()
N_MLA, N_H2 = np.cumsum([KD * TURNS, 4]).tolist()

Q_MEM, Q_X, Q_CQ, Q_CKV, Q_X1, Q_X2, Q_END = np.cumsum([0, MT, QT, QT, QT, QT, 2 * QT]).tolist()

C_ID, C_MASK, C_COST, C_SINT, C_COS, C_SIN, C_END = np.cumsum([0, P, P, 64, 64, S, S]).tolist()


def ring(c, per, i):
    return c % 2, c // 2 + (per // 2) * i


def wait(eng, sem, value):
    if not isinstance(value, int) or value > 0:
        eng.wait_ge(sem, value)


def hybrid_layer(nc, x, mem, rel_bias, attn_norm, mem_norm, w_in, b_gate, mla_q_norm, w_uq,
                 mla_kv_norm, w_ukv, attn_sinks, w_mem_kv, w_o_mla, w_o_swa, w_o_mem, w_out,
                 mlp_norm, w_up, w_down, final_norm, consts, toeplitz, out):
    ctx = ExitStack()
    with ctx:
        place = [-(-nc.sbuf_base // 32) * 32]

        def sb(name, width, dt=F32, at=None):
            off = place[0] if at is None else at
            if at is None:
                place[0] += -(-4 * width // 32) * 32
            t = nc.alloc_sbuf_tensor_at(name, [P, width], dt, offset=off)
            return t[:, :], off

        def sem(name):
            return ctx.enter_context(nc.semaphore(name))

        w_hi = sb("w_hi", 2 * BLK, F32R)[0].rearrange("p (s n) -> p s n", s=2)
        w_lo = sb("w_lo", 2 * BLK, F32R)[0].rearrange("p (s n) -> p s n", s=2)
        h_hi_flat, h_hi_at = sb("h_hi", KD * S, F32R)
        h_lo_flat, _ = sb("h_lo", KD * S, F32R)
        h_hi = h_hi_flat.rearrange("p (k n) -> p k n", k=KD)
        h_lo = h_lo_flat.rearrange("p (k n) -> p k n", k=KD)
        attn, attn_at = sb("attn", 17408, F32R)

        def part(lo, n):
            return attn[:, lo:lo + n]

        o_hi = part(0, 2048).rearrange("p (k n) -> p k n", k=4)
        o_lo = part(2048, 2048).rearrange("p (k n) -> p k n", k=4)
        pt_hi, pt_lo = part(4096, 2048), part(6144, 2048)
        q_hi = part(8192, 1024).rearrange("p (s n) -> p s n", s=2)
        q_lo = part(9216, 1024).rearrange("p (s n) -> p s n", s=2)
        v_hi = part(10240, 512).rearrange("p (k n) -> p k n", k=4)
        v_lo = part(10752, 512).rearrange("p (k n) -> p k n", k=4)
        vm_hi = part(10240, 1024).rearrange("p (t n) -> p t n", t=MT)
        vm_lo = part(15872, 1024).rearrange("p (t n) -> p t n", t=MT)
        km_hi, km_lo = part(11264, M), part(11264 + M, M)
        mn_hi = part(11776, 2048).rearrange("p (k n) -> p k n", k=KD)
        mn_lo = part(13824, 2048).rearrange("p (k n) -> p k n", k=KD)
        kz_hi = part(11264, 1024).rearrange("p (g n) -> p g n", g=2)
        kz_lo = part(12288, 1024).rearrange("p (g n) -> p g n", g=2)
        bias_hi = part(13312, 2048).rearrange("p (g r n) -> p g r n", g=2, r=PAIRS)
        bias_lo = part(15360, 2048).rearrange("p (g r n) -> p g r n", g=2, r=PAIRS)
        ka_hi = part(11264, 1024).rearrange("p (s n) -> p s n", s=2)
        ka_lo = part(12288, 1024).rearrange("p (s n) -> p s n", s=2)
        cq_hi = part(13312, 1024).rearrange("p (k n) -> p k n", k=2)
        cq_lo = part(14336, 1024).rearrange("p (k n) -> p k n", k=2)
        ckv_hi, ckv_lo = part(15360, 512), part(15872, 512)
        act_sq = sb("act_sq", FF // P * S, F32, at=attn_at)[0]
        mem_sb = act_sq[:, 8192:8192 + 2 * D].rearrange("p (t n) -> p t n", t=2)
        yr_hi = part(4096, 2048).rearrange("p (s n) -> p s n", s=2)
        yr_lo = part(6144, 2048).rearrange("p (s n) -> p s n", s=2)

        raw = sb("raw", 2 * BLK)[0].rearrange("p (s n) -> p s n", s=2)
        xg, _ = sb("xg", QT * D)
        x_sb = xg.rearrange("p (t n) -> p t n", t=QT)
        gate = xg.rearrange("p (m n) -> p m n", m=KD)
        ybuf, y_at = sb("ybuf", QT * D)
        ar_hi = sb("ar_hi", 2 * 1024, F32R, at=y_at)[0].rearrange("p (s n) -> p s n", s=2)
        ar_lo = sb("ar_lo", 2 * 1024, F32R, at=y_at + 4 * 2 * 1024)[0].rearrange("p (s n) -> p s n", s=2)
        fin = sb("fin", QT * D, at=h_hi_at)[0].rearrange("p (t n) -> p t n", t=QT)
        y = ybuf.rearrange("p (m n) -> p m n", m=KD)
        frep = ybuf[:, 0:HS * TOE].rearrange("p (h n) -> p h n", h=HS)
        scratch, _ = sb("scratch", BLK)
        toe = scratch[:, 0:TOE]
        bias_raw = scratch
        kvq = scratch[:, 0:4 * 416].rearrange("p (t n) -> p t n", t=QT)
        rope_a = [scratch[64:96, 1024 * c:1024 * c + S] for c in range(2)]
        rope_b = [scratch[64:96, 1024 * c + S:1024 * c + 2 * S] for c in range(2)]
        fgain = scratch[:, 0:D]
        relu = scratch[:, D:2 * D].rearrange("p (s n) -> p s n", s=2)
        probs_flat, _ = sb("probs", 2 * S)
        probs = probs_flat.rearrange("p (s n) -> p s n", s=2)
        junk = probs_flat
        tmp_flat, tmp_at = sb("tmp", 2 * S)
        tmp = tmp_flat.rearrange("p (s n) -> p s n", s=2)
        toe_r = sb("toe_r", TOE, F32R, at=tmp_at)[0]
        rel_hi, rel_lo = sb("rel_hi", HS, F32R)[0], sb("rel_lo", HS, F32R)[0]
        con, _ = sb("con", C_END)
        ident = con[:, C_ID:C_ID + P]
        cos_t = con[:, C_COST:C_COST + 64].rearrange("p (t n) -> p t n", t=QT)
        sin_t = con[:, C_SINT:C_SINT + 64].rearrange("p (t n) -> p t n", t=QT)
        cos_f, sin_f = con[:, C_COS:C_COS + S], con[:, C_SIN:C_SIN + S]
        ident_r, mask_r = sb("ident_r", P, F32R)[0], sb("mask_r", P, F32R)[0]
        kpad = sb("kpad", QT * QK)[0].rearrange("p (t n) -> p t n", t=QT)
        rtmp = sb("rtmp", 4 * 64)[0].rearrange("p (a t n) -> p a t n", a=4, t=QT)
        g_attn, g_mem, g_mlp = sb("g_attn", KD)[0], sb("g_mem", KD)[0], sb("g_mlp", KD)[0]
        g_q, g_kv = sb("g_q", 2)[0], sb("g_kv", 1)[0]
        hb, hb_raw = sb("hb", 3 * KD)[0], sb("hb_raw", 3 * KD)[0]
        sinks, nsinks = sb("sinks", HS)[0], sb("nsinks", HS)[0].rearrange("p (g r) -> p g r", g=2)
        rel = sb("rel", HS)[0]
        half_neg = sb("half_neg", 8)[0]
        sumsq, rstd = sb("sumsq", Q_END)[0], sb("rstd", Q_END)[0]
        mx = sb("mx", 4)[0].rearrange("p (s g) -> p s g", s=2)
        negm = sb("negm", 4)[0].rearrange("p (s g) -> p s g", s=2)
        snk = sb("snk", 4)[0].rearrange("p (s g) -> p s g", s=2)
        esnk = sb("esnk", 4)[0].rearrange("p (s g) -> p s g", s=2)
        rsum = sb("rsum", 4)[0].rearrange("p (s g) -> p s g", s=2)
        tot = sb("tot", 4)[0].rearrange("p (s g) -> p s g", s=2)
        rinv = sb("rinv", 4)[0].rearrange("p (s g) -> p s g", s=2)

        ps = ctx.enter_context(nc.psum_tensor("ps", [P, 8 * 512], F32))

        def bank(n, lo=0, hi=512):
            return ps[:, 512 * n + lo:512 * n + hi]

        bias_rows = nc.dram_tensor("bias_rows", [P, HS, TOE], F32)

        const_in, toe_in = sem("const_in"), sem("toe_in")
        ident_in, tab_in, gain_in = sem("ident_in"), sem("tab_in"), sem("gain_in")
        tokens_in = [sem(f"tokens_in{n}") for n in range(TURNS)]
        v_ready, v_lo_done = sem("v_ready"), sem("v_lo_done")
        vs_turned, vs_hi_done, vs_lo_done = sem("vs_turned"), sem("vs_hi_done"), sem("vs_lo_done")
        vm_ready, vm_hi_done, vm_lo_done = sem("vm_ready"), sem("vm_hi_done"), sem("vm_lo_done")
        inv_step, rel_step = sem("inv_step"), sem("rel_step")
        raw_in = [sem("raw_in0"), sem("raw_in1")]
        w_hi_done, w_lo_done = sem("w_hi_done"), sem("w_lo_done")
        tile_ready = sem("tile_ready")
        tile_done = [sem("tile_done0"), sem("tile_done1")]
        tile_hi = sem("tile_hi")
        tp_ready, tp_hi, tp_lo = sem("tp_ready"), sem("tp_hi"), sem("tp_lo")
        sq_done, ms_done, rstd_done, xn_done = sem("sq_done"), sem("ms_done"), sem("rstd_done"), sem("xn_done")
        s_ready, mx_done, neg_done, exp_done = sem("s_ready"), sem("mx_done"), sem("neg_done"), sem("exp_done")
        nsk_done, tot_done, rinv_done, p_done = sem("nsk_done"), sem("tot_done"), sem("rinv_done"), sem("p_done")
        t_ready, pt_hi_done, pt_lo_done = sem("t_ready"), sem("pt_hi_done"), sem("pt_lo_done")
        o_ready, o_hi_done, o_lo_done = sem("o_ready"), sem("o_hi_done"), sem("o_lo_done")
        fbank_ready, frep_done = sem("fbank_ready"), sem("frep_done")
        rows_out, bias_in = sem("rows_out"), sem("bias_in")
        idr_done, small_done, nhalf_done = sem("idr_done"), sem("small_done"), sem("nhalf_done")
        bias_hi_done, bias_lo_done, kz_zero = sem("bias_hi_done"), sem("bias_lo_done"), sem("kz_zero")
        pre_ready, pre_copied, kr_step = sem("pre_ready"), sem("pre_copied"), sem("kr_step")
        rope_in, rope_step, q_done = sem("rope_in"), sem("rope_step"), sem("q_done")
        y_done, x_again = sem("y_done"), sem("x_again")
        s_hi_done, s_lo_done, acc_step, added = sem("s_hi_done"), sem("s_lo_done"), sem("acc_step"), sem("added")
        sq_act, fgain_in, gained = sem("sq_act"), sem("fgain_in"), sem("gained")
        out_right_late = sem("out_right_late")
        gained_right = sem("gained_right")
        out_left, out_right, out_done = sem("out_left"), sem("out_right"), sem("out_done")

        win = w_in[0].rearrange("(k p) n -> p k n", p=P)
        wmk = w_mem_kv[0].rearrange("(k p) n -> p k n", p=P)
        wuq = w_uq[0].rearrange("(k p) n -> p k n", p=P)
        wup = w_up[0].rearrange("(k p) n -> p k n", p=P)
        wdn = w_down[0].rearrange("(k p) n -> p k n", p=P)
        wou = w_out[0].rearrange("(k p) n -> p k n", p=P)
        wo = {MLA: w_o_mla[0].rearrange("(k p) n -> p k n", p=P),
              MEM: w_o_mem[0].rearrange("(k p) n -> p k n", p=P)}
        wo_s = w_o_swa[0].rearrange("(g r d) n -> g d r n", g=2, r=PAIRS)
        xv = x[0].rearrange("(t p) n -> t p n", p=P)
        mv = mem[0].rearrange("(t p) n -> t p n", p=P)
        ov = out[0].rearrange("(t p) n -> t p n", p=P)

        def col(v):
            return v.rearrange("(k p) -> p k", p=P)

        def row(v, n):
            return bass.AP(v.tensor, v.offset, [[0, P], [1, n]])

        token_rows = [mem_sb[:, t, :] for t in range(MT)] + [x_sb[:, t, :] for t in range(QT)]

        block = ctx.enter_context(nc.Block())

        @block.sync
        def _(sp):
            def fetch(c, per, i, pieces):
                slot, _ = ring(c, per, i)
                wait(sp, w_lo_done, c - 1 + per * i)
                found = pieces(raw[:, slot, :])
                for (dst, src), share in zip(found, SHARES[len(found)]):
                    sp.dma_start(dst, src).then_inc(raw_in[slot], share)

            def cols(r, at, view, c0, n, k=KD):
                return r[:, at:at + k * n].rearrange("p (k c) -> p k c", k=k), view[:, :, ds(c0, n)]

            def gate_cols(r, at, branch, m):
                return cols(r, at, win, COL_G + branch * D + P * m, P)

            def fetch_wo(branch, b):
                for half in range(2):
                    c0 = half * 512
                    if branch == SWA:
                        fetch(b + half, 0, 0, lambda r: [
                            (r[64 * g:64 * g + 64, :].rearrange("p (k c) -> p k c", k=4),
                             wo_s[g][:, :, c0:c0 + 512]) for g in range(2)])
                    else:
                        fetch(b + half, 0, 0, lambda r: [cols(r, 0, wo[branch], c0, 512, 4)])


            def fetch_tokens(n):
                src = mv[n] if n < MT else xv[n - MT]
                sp.dma_start(token_rows[n], src).then_inc(tokens_in[n], 16)

            def fetch_vm(half):
                fetch(B_MEM + half, 0, 0, lambda r: [
                    (r.rearrange("p (k c) -> p k c", k=4), wmk[:, 4 * half:4 * half + 4, HM * DM:2 * HM * DM])])

            fetch_tokens(0)
            sp.dma_start(con[:, 0:C_MASK], consts[:, 0:C_MASK]).then_inc(ident_in, 16)
            for n in range(1, 4):
                fetch_tokens(n)
            fetch_vm(0)
            for n in range(4, TURNS):
                fetch_tokens(n)
            fetch_vm(1)
            sp.dma_start(toe[0:BUCKETS + 1, :], toeplitz).then_inc(toe_in, 16)
            sp.dma_start(rel[0:BUCKETS, :], rel_bias).then_inc(toe_in, 16)
            with nc.allow_non_contiguous_dma(reason="gains as columns: a few KiB in all"):
                for dst, src in ((hb_raw, col(b_gate[0])), (sinks, row(attn_sinks[0], HS)),
                                 (g_mlp, col(mlp_norm[0])), (g_q, col(mla_q_norm[0])),
                                 (g_kv, col(mla_kv_norm[0]))):
                    sp.dma_start(dst, src).then_inc(const_in, 16)
            for h in range(HM):
                b = B_MEM + 2 + 2 * h
                fetch(b, 0, 0, lambda r: [cols(r, 0, win, COL_QM + DM * h, P), cols(r, 1024, wmk, DM * h, P)])
                if h == 0:
                    sp.dma_start(con[:, C_MASK:C_COS], consts[:, C_MASK:C_COS]).then_inc(tab_in, 16)
                    sp.dma_start(con[64:96, C_COS:C_END], consts[64:96, C_COS:C_END]).then_inc(tab_in, 16)
                fetch(b + 1, 0, 0, lambda r: [gate_cols(r, 0, MEM, 2 * h), gate_cols(r, 1024, MEM, 2 * h + 1)])
                if h == 1:
                    sp.wait_ge(frep_done, HS)
                    sp.dma_start(bias_rows.ap(), frep).then_inc(rows_out, 16)
                if h == 2:
                    sp.wait_ge(rows_out, 16)
                    sp.dma_start(bias_raw.rearrange("p (h n) -> p h n", h=HS),
                                 bass.AP(bias_rows, P - 1, [[HS * TOE - 1, P], [TOE, HS], [1, 2 * P]])
                                 ).then_inc(bias_in, 16)
            fetch(B_KVS, 0, 0, lambda r: [cols(r, 0, win, COL_KS, P), cols(r, 1024, win, COL_KS + P, P)])
            fetch_wo(MEM, B_WO_MEM)
            with sp.Fori(0, PAIRS // 2) as i:
                for c in range(2):
                    fetch(B_SWA + 2 * c, 4, i, lambda r: [
                        (r[:, 0:1024].rearrange("p (k c) -> p k c", k=KD)[:, :, 64 * g:64 * g + 64],
                         win[:, :, ds(COL_QS + 256 * g + 64 * c + 128 * i, 64)]) for g in range(2)
                    ] + [gate_cols(r, 1024, SWA, 4 * i + 2 * c)])
                    fetch(B_SWA + 2 * c + 1, 4, i, lambda r: [gate_cols(r, 0, SWA, 4 * i + 2 * c + 1)])
            for half in range(2):
                fetch(B_MLAP + half, 0, 0, lambda r: [
                    (r[:, 0:4 * 416].rearrange("p (k c) -> p k c", k=4), win[:, 4 * half:4 * half + 4, 0:416])])
            fetch_wo(SWA, B_WO_SWA)
            with sp.Fori(0, HA // 2) as i:
                fetch(B_MLA, 2, i, lambda r: [cols(r, 0, wuq, 2 * QK * i, 2 * QK, 2),
                                              (r[:, 4 * QK:4 * QK + 2 * P], w_ukv[0][:, ds(2 * P * i, 2 * P)]),
                                              gate_cols(r, N_A - D, MLA, 2 * i)])
                fetch(B_MLA + 1, 2, i, lambda r: [gate_cols(r, 0, MLA, 2 * i + 1)])
            fetch_wo(MLA, B_WO_MLA)

            def rows(view, k):
                return lambda r: [(r.rearrange("p (k c) -> p k c", k=2), view[:, ds(k, 2), :])]

            with sp.Fori(0, D // 512) as i:
                for c in range(2):
                    fetch(B_WOUT + c, 2, i, rows(wou, 4 * i + 2 * c))
            with sp.Fori(0, FF // 512) as i:
                for c in range(2):
                    fetch(B_UP + c, 2, i, lambda r: [cols(r, 0, wup, 512 * i + 256 * c, 256)])
            with sp.Fori(0, FF // 512) as i:
                for c in range(2):
                    fetch(B_DOWN + c, 2, i, rows(wdn, 4 * i + 2 * c))
            for t in range(QT):
                for half in range(2):
                    if half == 0:
                        sp.wait_ge(out_left, t + 1)
                    elif t < 2:
                        sp.wait_ge(out_right, t + 1)
                    else:
                        sp.wait_ge(out_right_late, t - 1)
                    a = slice(512 * half, 512 * half + 512)
                    sp.dma_start(ov[t][:, a], fin[:, t, a]).then_inc(out_done, 16)
            sp.wait_ge(out_done, 32 * QT)

        BATCHES = ([(n, n + 1, n + 1) for n in range(TURNS)] + [(Q_CQ, Q_X1, TURNS + 2)]
                   + [(Q_X2 + t, Q_X2 + t + 1, TURNS + 4 + 2 * t) for t in range(QT)])
        BATCH_MLA, BATCH_X2 = TURNS, TURNS + 1

        def turned_bank(n, k):
            return bank(3 * (n % 2) + k % 3, P * (k // 3), P * (k // 3) + P)

        def turned_x(t, k):
            n, more = (4, 2 if t == QT - 1 else 0) if t else (2, 0)
            return bank([2 * t, 2 * t + 1, more, more + 1][k % n], P * (k // n), P * (k // n) + P)

        def w(buf, slot, at, k, n, c0=0, cn=P):
            return buf[:, slot, at + k * n + c0:at + k * n + c0 + cn]

        @block.gpsimd
        def _(pool):
            pool.memset(rel[BUCKETS:BUCKETS + 1, :], 1.0).then_inc(rel_step, 1)
            pool.wait_ge(rel_step, 1)
            pool.memset(half_neg, -0.5).then_inc(nhalf_done, 1)
            pool.memset(kpad, 0.0).then_inc(nhalf_done, 1)
            pool.wait_ge(nhalf_done, 1)

            def rsqrt(n):
                a, b, count = BATCHES[n]
                pool.wait_ge(ms_done, count)
                pool.tensor_tensor(rstd[:, a:b], rstd[:, a:b], half_neg[:, 0:b - a],
                                   ALU.pow).then_inc(rstd_done, 1)

            def split(c, per=0, i=0, n=BLK):
                slot, _ = ring(c, per, i)
                pool.wait_ge(w_lo_done, c + per * i)
                pool.wait_ge(w_hi_done, c + 1 + per * i)
                pool.tensor_tensor(w_lo[:, slot, 0:n], raw[:, slot, 0:n], w_hi[:, slot, 0:n].bitcast(F32),
                                   ALU.subtract).then_inc(w_lo_done, 1)
                pool.wait_ge(w_lo_done, c + 1 + per * i)

            for n in range(BATCH_MLA):
                rsqrt(n)
            split(B_MEM + 1)
            pool.wait_ge(tile_ready, T_KVS + 1)
            for buf in (kz_hi, kz_lo):
                pool.memset(buf[64:128, 0, :].bitcast(F32), 0.0).then_inc(kz_zero, 1)
                pool.memset(buf[0:64, 1, :].bitcast(F32), 0.0).then_inc(kz_zero, 1)
            rsqrt(BATCH_MLA)

            def rotate(j, c):
                pool.wait_ge(rope_in, j + 1)
                pool.tensor_tensor(rope_a[c], rope_a[c], sin_f[64:96, :], ALU.mult).then_inc(rope_step, 1)
                pool.wait_ge(rope_step, 2 * j + 1)
                pool.tensor_tensor(rope_b[c], rope_b[c], rope_a[c], ALU.add).then_inc(rope_step, 1)
                pool.wait_ge(rope_step, 2 * j + 2)

            rotate(0, 0)
            with pool.Fori(0, HA // 2 - 1) as i:
                rotate(2 * i + 1, 1)
                split(B_MLA + 1, 2, i, N_GATE)
                rotate(2 * i + 2, 0)
            rotate(HA - 1, 1)
            split(B_MLA + HA - 1, n=N_GATE)
            split(B_UP)
            for t in range(QT):
                rsqrt(BATCH_X2 + t)
                if t < 2:
                    if t == 0:
                        pool.wait_ge(fgain_in, 16)
                    pool.wait_ge(added, 2 * (QT + t) + 2)
                    pool.tensor_tensor(fin[:, t, 512:], x_sb[:, t, 512:], fgain[:, 512:],
                                       ALU.mult).then_inc(gained_right, 1)

        @block.scalar
        def _(act):
            def split(c, per=0, i=0, n=BLK, start=0, stop=None):
                slot, turn = ring(c, per, i)
                stop = n if stop is None else stop
                if start == 0:
                    act.wait_ge(raw_in[slot], 48 * (turn + 1))
                ins = act.activation(w_hi[:, slot, start:stop], raw[:, slot, start:stop], ACT.Copy)
                if stop == n:
                    ins.then_inc(w_hi_done, 1)

            def ready(c, per=0, i=0):
                act.wait_ge(tile_ready, c + 1 + per * i)
                return c % 2

            def square(n, src):
                wait(act, sq_done, n)
                act.activation(junk[:, 0:src.shape[-1]], src, ACT.Square,
                               accum_out=sumsq[:, n:n + 1]).then_inc(sq_done, 1)

            def tp_part(g, dst, src, gain):
                act.wait_ge(tp_ready, g + 1)
                act.activation(dst, src, ACT.Copy, scale=gain).then_inc(tp_hi, 1)

            def turned(t, r0, n0, banks, place, dst, gain):
                for k in range(KD):
                    if k >= banks:
                        act.wait_ge(tp_lo, n0 + k - banks + 1)
                    tp_part(r0 + k % banks, dst[:, k, P * t:P * t + P], place(k), gain[:, k:k + 1])

            def turned_in(n):
                act.wait_ge(gain_in, 32)
                t, dst, gain = (n, mn_hi, g_mem) if n < MT else (n - MT, h_hi, g_attn)
                turned(t, 3 * n, KD * n, 3, lambda k: turned_bank(n, k), dst, gain)

            def tanh(m, branch, c, per=0, i=0):
                bk = ready(c, per, i)
                act.activation(gate[:, ds(m, 1), :], bank(bk).rearrange("p (m n) -> p m n", m=1), ACT.Tanh,
                               bias=hb[:, ds(branch * KD + m, 1)], scale=0.5).then_inc(tile_done[bk], 1)

            def exps(u, per, i, groups, n, scale, sink=False):
                s = u % 2
                act.wait_ge(neg_done, u + 1 + per * i)
                if sink:
                    act.activation(esnk[:, s, :], snk[:, s, :], ACT.Exp)
                for g in range(groups):
                    last = act.activation(probs[:, s, g * n:(g + 1) * n], bank(2 + s, g * n, (g + 1) * n), ACT.Exp,
                                          bias=negm[:, s, g:g + 1], scale=scale, accum_out=rsum[:, s, g:g + 1])
                last.then_inc(exp_done, 1)

            def pt(u, per, i, dst, src):
                act.wait_ge(t_ready, u + 1 + per * i)
                act.activation(dst, src, ACT.Copy).then_inc(pt_hi_done, 1)

            with nc.allow_non_contiguous_dma(reason="gains as columns: a few KiB in all"):
                act.dma_start(g_mem, col(mem_norm[0])).then_inc(gain_in, 16)
                act.dma_start(g_attn, col(attn_norm[0])).then_inc(gain_in, 16)

            def square_in(n):
                act.wait_ge(tokens_in[n], 16)
                square(n, token_rows[n])

            square_in(0)
            square_in(1)
            square_in(2)
            turned_in(0)
            square_in(3)
            turned_in(1)
            split(0)
            square_in(4)
            square_in(5)
            turned_in(2)
            split(1)
            turned_in(3)
            turned_in(4)
            split(2)
            turned_in(5)
            for t in range(MT):
                act.wait_ge(vm_ready, t + 1)
                act.activation(vm_hi[:, t, :], bank(6 + t), ACT.Copy).then_inc(vm_hi_done, 1)
            split(3)
            act.wait_ge(tab_in, 32)
            act.wait_ge(toe_in, 32)
            act.wait_ge(rel_step, 1)
            act.activation(rel_hi[0:BUCKETS + 1, :], rel[0:BUCKETS + 1, :], ACT.Copy).then_inc(rel_step, 1)
            act.activation(toe_r[0:BUCKETS + 1, :], toe[0:BUCKETS + 1, :], ACT.Copy).then_inc(rel_step, 1)
            act.activation(ident_r, ident, ACT.Copy).then_inc(idr_done, 1)
            act.activation(mask_r, con[:, C_MASK:C_MASK + P], ACT.Copy).then_inc(idr_done, 1)
            act.wait_ge(small_done, 1)

            for h in range(HM):
                t0, u0, b = T_MEM + 4 * h, U_MEM + 2 * h, B_MEM + 2 + 2 * h
                bk = ready(t0)
                act.activation(q_hi[:, h % 2, :], bank(bk), ACT.Copy).then_inc(tile_hi, 1)
                bk = ready(t0 + 1)
                act.activation(km_hi, bank(bk, 0, M), ACT.Copy).then_inc(tile_hi, 1)
                exps(u0, 0, 0, 2, M, DM ** -0.5)
                exps(u0 + 1, 0, 0, 2, M, DM ** -0.5)
                tanh(2 * h, MEM, t0 + 2)
                for n in range(2):
                    pt(u0 + n, 0, 0, pt_hi[:, 512 * n:512 * n + 512], bank(4 + n))
                split(b + 2)
                tanh(2 * h + 1, MEM, t0 + 3)
                split(b + 3)
                act.wait_ge(o_ready, E_MEM + h + 1)
                act.activation(o_hi[:, h, :], bank(6 + h % 2), ACT.Copy).then_inc(o_hi_done, 1)

            bk = ready(T_KVS)
            act.activation(kz_hi[0:64, 0, :], bank(bk)[0:64, :], ACT.Copy)
            act.activation(kz_hi[64:128, 1, :], bank(bk)[64:128, :], ACT.Copy).then_inc(tile_hi, 1)
            act.wait_ge(bias_in, 16)
            act.activation(bias_hi, bias_raw.rearrange("p (g r n) -> p g r n", g=2, r=PAIRS),
                           ACT.Copy).then_inc(bias_hi_done, 1)
            bk = ready(T_KVS + 1)
            act.activation(tmp[:, 0, :], bank(bk), ACT.Copy).then_inc(tile_done[bk], 1)
            split(B_KVS + 2)
            act.wait_ge(vs_turned, 1)
            act.activation(v_hi, bank(4).rearrange("p (k n) -> p k n", k=4), ACT.Copy).then_inc(vs_hi_done, 1)
            ready(T_WO_MEM + 3)
            split(B_WO_MEM + 2)
            ready(T_WO_MEM + 7)
            split(B_WO_MEM + 3)
            for slot in range(2):
                act.wait_ge(tile_done[slot], (T_WO_MEM + KD) // 2)

            with act.Fori(0, PAIRS // 2) as i:
                for c in range(2):
                    t0, u0, b = T_SWA + 3 * c, U_SWA + 4 * c, B_SWA + 2 * c
                    bk = ready(t0, 6, i)
                    act.activation(q_hi[:, c, :], bank(bk), ACT.Copy).then_inc(tile_hi, 1)

                    def e(n):
                        exps(u0 + n, 8, i, 2, P if n == 0 else 2 * P, DS ** -0.5, True)

                    def p(n):
                        lo = 256 if n == 0 else 0
                        pt(u0 + n, 8, i, pt_hi[:, 512 * n + lo:512 * n + 512], bank(4 + n % 2, lo, 512))

                    e(0)
                    e(1)
                    p(0)
                    e(2)
                    p(1)
                    tanh(2 * c + 4 * i, SWA, t0 + 1, 6, i)
                    e(3)
                    split(b + 2, 4, i, stop=BLK // 2)
                    p(2)
                    p(3)
                    split(b + 2, 4, i, start=BLK // 2)
                    tanh(2 * c + 1 + 4 * i, SWA, t0 + 2, 6, i)
                    split(b + 3, 4, i, n=N_GATE if c == 0 else N_MLAP)
                    act.wait_ge(o_ready, E_SWA + c + 1 + 2 * i)
                    for g in range(2):
                        r = slice(64 * g, 64 * g + 64)
                        last = act.activation(o_hi[r, ds(2 * i + c, 1), :],
                                              bank(6 + g)[r, :].rearrange("p (m n) -> p m n", m=1), ACT.Copy)
                    last.then_inc(o_hi_done, 1)

            act.wait_ge(pre_ready, 1)
            split(B_MLAP + 2)
            act.wait_ge(bias_lo_done, 1)
            for t in range(QT):
                act.wait_ge(pre_ready, t + 2)
                act.activation(kvq[:, t, :], bank(2 + t, 0, 416), ACT.Copy).then_inc(pre_copied, 1)
            split(B_MLAP + 3)
            act.wait_ge(pre_copied, QT)
            for t in range(QT):
                square(Q_CQ + t, kvq[:, t, 0:QL])
            for t in range(QT):
                square(Q_CKV + t, kvq[:, t, QL:QL + KVL])
            ready(T_WO_SWA + 3)
            split(B_MLA, n=N_A)
            for k in range(2):
                tp_part(R_MLA + k, cq_hi[:, k, :], bank(2 + k), g_q[:, k:k + 1])
            tp_part(R_MLA + 2, ckv_hi, bank(4), g_kv[:, 0:1])
            act.wait_ge(tp_ready, R_MLA + 4)
            act.activation(ka_hi[64:96, 0, :], bank(5)[64:96, :], ACT.Copy)
            act.activation(ka_hi[64:96, 1, :], bank(5)[64:96, :], ACT.Copy).then_inc(tp_hi, 1)
            def key(n, c, per=0, i=0):
                bk = ready(n, per, i)
                act.activation(ka_hi[0:64, c, :], bank(bk)[0:64, :], ACT.Copy).then_inc(tile_hi, 1)

            def query(n, c, per=0, i=0):
                bk = ready(n, per, i)
                act.activation(q_hi[0:64, c, :], bank(bk)[0:64, :], ACT.Copy).then_inc(tile_hi, 1)

            def rotary(j, c):
                act.wait_ge(rope_step, 2 * j + 2)
                act.activation(q_hi[64:96, c, :], rope_b[c], ACT.Copy).then_inc(tile_hi, 1)

            query(T_MLA, 0)
            key(T_MLA + 1, 0)
            act.wait_ge(y_done, KD)

            def two_heads(i, final=False):
                t0, u0, b = T_MLA + 2, U_MLA, B_MLA
                key(t0, 1, 6, i)
                rotary(2 * i, 0)
                query(t0 + 1, 1, 6, i)
                act.wait_ge(v_ready, 1 + i)
                act.activation(v_hi, bank(6).rearrange("p (k n) -> p k n", k=4), ACT.Copy).then_inc(tile_hi, 1)
                split(b + 1, 2, i, n=N_GATE)

                n_a = BLK if final else N_A

                def e(c, n):
                    exps(u0 + 4 * c + n, 8, i, 1, P * (n + 1), QK ** -0.5)

                def p(c, n):
                    pt(u0 + 4 * c + n, 8, i,
                       pt_hi.rearrange("p (k q) -> p k q", k=4)[:, 0:n + 1, P * n:P * n + P],
                       bank(4 + n % 2, 0, P * (n + 1)).rearrange("p (k q) -> p k q", q=P))

                def o(c):
                    r = slice(64 * c, 64 * c + 64)
                    act.wait_ge(o_ready, E_MLA + c + 1 + 2 * i)
                    act.activation(o_hi[r, ds(i, 1), :], bank(6 + c)[r, :].rearrange("p (m n) -> p m n", m=1),
                                   ACT.Copy).then_inc(o_hi_done, 1)

                e(0, 0)
                e(0, 1)
                p(0, 0)
                e(0, 2)
                p(0, 1)
                rotary(1 + 2 * i, 1)
                e(0, 3)
                p(0, 2)
                p(0, 3)
                split(b + 2, 2, i, n=n_a, stop=n_a // 2)
                e(1, 0)
                e(1, 1)
                tanh(2 * i, MLA, t0 + 2, 6, i)
                act.wait_ge(o_ready, E_MLA + 1 + 2 * i)
                p(1, 0)
                split(b + 2, 2, i, n=n_a, start=n_a // 2)
                e(1, 2)
                p(1, 1)
                e(1, 3)
                o(0)
                p(1, 2)
                p(1, 3)
                tanh(2 * i + 1, MLA, t0 + 3, 6, i)
                if not final:
                    query(t0 + 4, 0, 6, i)
                    key(t0 + 5, 0, 6, i)
                o(1)
                if final:
                    split(b + 3, 2, i)

            with act.Fori(0, HA // 2 - 1) as i:
                two_heads(i)
            two_heads(HA // 2 - 1, True)

            def split_s(n, ring_hi, src, scale, c=0, per=0, i=0):
                act.activation(ring_hi[:, c % 2, :], src[:, ds(1024 * n, 1024)], ACT.Copy,
                               scale=scale).then_inc(s_hi_done, 1)

            ready(T_WO_MLA + 3)
            split(B_WO_MLA + 2)
            for n in range(2):
                act.wait_ge(y_done, KD + 2 * n + 2)
                split_s(n, yr_hi, ybuf, 0.5, n)
            ready(T_WO_MLA + 7)
            split(B_WO_MLA + 3)
            act.wait_ge(y_done, 2 * KD)
            for t in range(QT):
                act.dma_start(x_sb[:, t, :], xv[t]).then_inc(x_again, 16)
            act.dma_start(fgain, row(final_norm, D)).then_inc(fgain_in, 16)
            for n in range(3):
                act.wait_ge(acc_step, 8 * (n + 1))
                if n < 2:
                    split_s(n + 2, yr_hi, ybuf, 0.5, n)
                split(B_WOUT + n + 2)
            for t in range(QT):
                turned(t, R_H2 + max(4 * t - 2, 0), N_H2 + KD * t, 4 if t else 2,
                       lambda k: turned_x(t, k), h_hi, g_mlp)
            split(B_UP + 1)
            for t in range(QT):
                square(Q_X1 + t, x_sb[:, t, :])

            def up(i):
                for c in range(4):
                    slot, turn = ring(T_UP + c, 4, i)
                    ready(T_UP + c, 4, i)
                    wait(act, sq_act, c - 1 + 4 * i)
                    act.activation(relu[:, c % 2, :], bank(slot), ACT.Relu).then_inc(tile_done[slot], 1)
                    if c % 2:
                        split(B_UP + 2 + c // 2, 2, i)

            up(0)
            with act.Fori(1, FF // 512 - 1) as i:
                up(i)
            act.wait_ge(tp_ready, R_END)
            for n in range(2):
                act.wait_ge(sq_act, 2 * n + 2)
                split_s(n, ar_hi, act_sq, 1.0, n)
            up(FF // 512 - 1)
            act.wait_ge(sq_act, FF // P)
            with act.Fori(0, FF // 512 - 1) as i:
                for c in range(2):
                    act.wait_ge(acc_step, 32 + 8 * (c + 1) + 16 * i)
                    split_s(2 * i + c + 2, ar_hi, act_sq, 1.0, c)
                    split(B_DOWN + 2 + c, 2, i)
            def square_out(t):
                for half in range(2):
                    act.wait_ge(added, 2 * (QT + t) + half + 1)
                    square(Q_X2 + 2 * t + half, x_sb[:, t, 512 * half:512 * half + 512])

            def scale_out(t, half, gain_sem, count):
                act.wait_ge(rstd_done, BATCH_X2 + t + 1)
                act.wait_ge(gain_sem, count)
                a = slice(512 * half, 512 * half + 512)
                act.activation(fin[:, t, a], fin[:, t, a], ACT.Copy,
                               scale=rstd[:, Q_X2 + t:Q_X2 + t + 1]).then_inc([out_left, out_right][half], 1)

            square_out(0)
            square_out(1)
            scale_out(0, 0, gained, 1)
            scale_out(0, 1, gained_right, 1)
            square_out(2)
            scale_out(1, 0, gained, 2)
            scale_out(1, 1, gained_right, 2)
            scale_out(2, 0, gained, 3)
            square_out(3)
            scale_out(3, 0, gained, 5)

        @block.vector
        def _(dve):
            def f(ap):
                return ap.bitcast(F32)

            def split(c, per=0, i=0, n=BLK, start=0, stop=None):
                slot, _ = ring(c, per, i)
                stop = n if stop is None else stop
                a = slice(start, stop)
                if start == 0:
                    dve.wait_ge(w_hi_done, c + 1 + per * i)
                ins = dve.tensor_tensor(w_lo[:, slot, a], raw[:, slot, a], f(w_hi[:, slot, a]), ALU.subtract)
                if stop == n:
                    ins.then_inc(w_lo_done, 1)

            def lo(n, per, i, dst, src, hi, bk):
                dve.wait_ge(tile_hi, n + 1 + per * i)
                dve.tensor_tensor(dst, src, f(hi), ALU.subtract).then_inc(tile_done[bk], 1)

            def tp_part(n, dst, src, gain, hi):
                dve.wait_ge(tp_hi, n + 1)
                dve.scalar_tensor_tensor(dst, src, gain, f(hi), ALU.mult, ALU.subtract).then_inc(tp_lo, 1)

            def turned(t, n0, place, dst, gain, hi):
                for k in range(KD):
                    tk = slice(P * t, P * t + P)
                    tp_part(n0 + k, dst[:, k, tk], place(k), gain[:, k:k + 1], hi[:, k, tk])

            def turned_in(n):
                dve.wait_ge(gain_in, 32)
                t, dst, gain, hi = (n, mn_lo, g_mem, mn_hi) if n < MT else (n - MT, h_lo, g_attn, h_hi)
                turned(t, KD * n, lambda k: turned_bank(n, k), dst, gain, hi)

            def mean_sq(a, b, width, done=ms_done):
                dve.wait_ge(sq_done, b)
                dve.tensor_scalar(rstd[:, a:b], sumsq[:, a:b], 1.0 / width, EPS, ALU.mult,
                                  ALU.add).then_inc(done, 1)

            def peak(u, per, i, groups, n, scale, r=None):
                s = u % 2
                dve.wait_ge(s_ready, u + 1 + per * i)
                dve.tensor_reduce(mx[:, s, 0:groups], bank(2 + s, 0, groups * n).rearrange("p (g n) -> p g n", n=n),
                                  AX_X, ALU.max).then_inc(mx_done, 1)
                dve.wait_ge(mx_done, u + 1 + per * i)
                if r is None:
                    dve.tensor_scalar(negm[:, s, 0:groups], mx[:, s, 0:groups], -scale, None,
                                      ALU.mult).then_inc(neg_done, 1)
                    return
                sink = nsinks[:, :, ds(r, 1)]
                dve.scalar_tensor_tensor(negm[:, s:s + 1, :].rearrange("p a g -> p g a"),
                                         mx[:, s:s + 1, :].rearrange("p a g -> p g a"), -scale, sink,
                                         ALU.mult, ALU.min).then_inc(nsk_done, 1)
                dve.wait_ge(nsk_done, u - U_SWA + 1 + per * i)
                dve.tensor_tensor(snk[:, s:s + 1, :].rearrange("p a g -> p g a"),
                                  negm[:, s:s + 1, :].rearrange("p a g -> p g a"), sink,
                                  ALU.subtract).then_inc(neg_done, 1)

            def norm(u, per, i, groups, n, sink=False):
                s = u % 2
                dve.wait_ge(exp_done, u + 1 + per * i)
                den = rsum
                if sink:
                    dve.tensor_tensor(tot[:, s, :], rsum[:, s, :], esnk[:, s, :], ALU.add).then_inc(tot_done, 1)
                    dve.wait_ge(tot_done, u - U_SWA + 1 + per * i)
                    den = tot
                dve.reciprocal(rinv[:, s, 0:groups], den[:, s, 0:groups]).then_inc(rinv_done, 1)
                dve.wait_ge(rinv_done, u + 1 + per * i)
                for g in range(groups):
                    block_p = probs[:, s, g * n:(g + 1) * n]
                    last = dve.tensor_scalar(block_p, block_p, rinv[:, s, g:g + 1], None, ALU.mult)
                last.then_inc(p_done, 1)

            def pt(u, per, i, dst, src, hi):
                dve.wait_ge(pt_hi_done, u + 1 + per * i)
                dve.tensor_tensor(dst, src, f(hi), ALU.subtract).then_inc(pt_lo_done, 1)

            def merge(t0, first, m0=0, m1=KD):
                for m in range(m0, m1):
                    slot, turn = ring(t0 + m, 0, 0)
                    dve.wait_ge(tile_ready, t0 + m + 1)
                    if first:
                        dve.scalar_tensor_tensor(y[:, m, :], gate[:, m, :], 1.0, bank(slot), ALU.add,
                                                 ALU.mult).then_inc(tile_done[slot], 1)
                        continue
                    dve.scalar_tensor_tensor(tmp[:, m % 2, :], gate[:, m, :], 1.0, bank(slot), ALU.add,
                                             ALU.mult).then_inc(tile_done[slot], 1)
                    dve.wait_ge(tile_done[slot], turn + 1)
                    dve.tensor_tensor(y[:, m, :], y[:, m, :], tmp[:, m % 2, :], ALU.add).then_inc(y_done, 1)

            def norm_in(n):
                mean_sq(n, n + 1, D)
                scale_in(n)

            def scale_in(n):
                dve.wait_ge(rstd_done, n + 1)
                dve.tensor_scalar(token_rows[n], token_rows[n], rstd[:, n:n + 1], None, ALU.mult).then_inc(xn_done, 1)

            norm_in(0)
            norm_in(1)
            mean_sq(2, 3, D)
            turned_in(0)
            scale_in(2)
            mean_sq(3, 4, D)
            turned_in(1)
            scale_in(3)
            split(0)
            mean_sq(4, 5, D)
            mean_sq(5, 6, D)
            turned_in(2)
            scale_in(4)
            scale_in(5)
            turned_in(3)
            turned_in(4)
            dve.wait_ge(w_lo_done, 2)
            split(2)
            turned_in(5)
            for t in range(MT):
                dve.wait_ge(vm_hi_done, t + 1)
                dve.tensor_tensor(vm_lo[:, t, :], bank(6 + t), f(vm_hi[:, t, :]),
                                  ALU.subtract).then_inc(vm_lo_done, 1)
            split(3)
            dve.wait_ge(const_in, 16 * 5)
            dve.tensor_scalar(hb, hb_raw, 0.5, None, ALU.mult).then_inc(small_done, 1)
            dve.tensor_scalar(nsinks, sinks.rearrange("p (g r) -> p g r", g=2), -1.0, None,
                              ALU.mult).then_inc(small_done, 1)
            dve.wait_ge(small_done, 2)
            dve.wait_ge(rel_step, 3)
            rows_r = slice(0, BUCKETS + 1)
            dve.tensor_tensor(rel_lo[rows_r, :], rel[rows_r, :], f(rel_hi[rows_r, :]),
                              ALU.subtract).then_inc(rel_step, 1)

            def bias_rows_of(a, b):
                for n in range(a, b):
                    dve.wait_ge(fbank_ready, n + 1)
                    dve.tensor_scalar(frep[:, n, :], bank(4 + n % 4, 0, TOE), DS ** 0.5, None,
                                      ALU.mult).then_inc(frep_done, 1)

            for h in range(HM):
                t0, u0, b, n0 = T_MEM + 4 * h, U_MEM + 2 * h, B_MEM + 2 + 2 * h, H_MEM + 2 * h
                lo(n0, 0, 0, q_lo[:, h % 2, :], bank(t0 % 2), q_hi[:, h % 2, :], t0 % 2)
                lo(n0 + 1, 0, 0, km_lo, bank((t0 + 1) % 2, 0, M), km_hi, (t0 + 1) % 2)
                if h == 0:
                    bias_rows_of(0, HS)
                for n in range(2):
                    peak(u0 + n, 0, 0, 2, M, DM ** -0.5)
                for n in range(2):
                    norm(u0 + n, 0, 0, 2, M)
                for n in range(2):
                    at = slice(512 * n, 512 * n + 512)
                    pt(u0 + n, 0, 0, pt_lo[:, at], bank(4 + n), pt_hi[:, at])
                split(b + 2)
                split(b + 3)
                dve.wait_ge(o_hi_done, E_MEM + h + 1)
                dve.tensor_tensor(o_lo[:, h, :], bank(6 + h % 2), f(o_hi[:, h, :]),
                                  ALU.subtract).then_inc(o_lo_done, 1)

            bk = T_KVS % 2
            dve.wait_ge(tile_hi, H_KVS + 1)
            dve.tensor_tensor(kz_lo[0:64, 0, :], bank(bk)[0:64, :], f(kz_hi[0:64, 0, :]), ALU.subtract)
            dve.tensor_tensor(kz_lo[64:128, 1, :], bank(bk)[64:128, :], f(kz_hi[64:128, 1, :]),
                              ALU.subtract).then_inc(tile_done[bk], 1)
            dve.wait_ge(rows_out, 16)
            dve.wait_ge(bias_hi_done, 1)
            dve.tensor_tensor(bias_lo, bias_raw.rearrange("p (g r n) -> p g r n", g=2, r=PAIRS), f(bias_hi),
                              ALU.subtract).then_inc(bias_lo_done, 1)
            merge(T_WO_MEM, True, 0, 2)
            split(B_KVS + 2)
            merge(T_WO_MEM, True, 2, 4)
            dve.wait_ge(vs_hi_done, 1)
            dve.tensor_tensor(v_lo, bank(4).rearrange("p (k n) -> p k n", k=4), f(v_hi),
                              ALU.subtract).then_inc(vs_lo_done, 1)
            merge(T_WO_MEM, True, 4, 5)
            split(B_WO_MEM + 2)
            merge(T_WO_MEM, True, 5)
            split(B_WO_MEM + 3)

            with dve.Fori(0, PAIRS // 2) as i:
                for c in range(2):
                    t0, u0, b = T_SWA + 3 * c, U_SWA + 4 * c, B_SWA + 2 * c
                    lo(H_SWA + c, 2, i, q_lo[:, c, :], bank(t0 % 2), q_hi[:, c, :], t0 % 2)

                    def pk(n):
                        peak(u0 + n, 8, i, 2, P if n == 0 else 2 * P, DS ** -0.5, 2 * i + c)

                    def nm(n):
                        norm(u0 + n, 8, i, 2, P if n == 0 else 2 * P, True)

                    def p(n):
                        z = 256 if n == 0 else 0
                        at = slice(512 * n + z, 512 * n + 512)
                        pt(u0 + n, 8, i, pt_lo[:, at], bank(4 + n % 2, z, 512), pt_hi[:, at])

                    pk(0)
                    pk(1)
                    nm(0)
                    nm(1)
                    p(0)
                    pk(2)
                    nm(2)
                    pk(3)
                    p(1)
                    nm(3)
                    p(2)
                    p(3)
                    split(b + 2, 4, i)
                    split(b + 3, 4, i, n=N_GATE if c == 0 else N_MLAP)
                    dve.wait_ge(o_hi_done, E_SWA + c + 1 + 2 * i)
                    for g in range(2):
                        r = slice(64 * g, 64 * g + 64)
                        last = dve.tensor_tensor(o_lo[r, ds(2 * i + c, 1), :],
                                                 bank(6 + g)[r, :].rearrange("p (m n) -> p m n", m=1),
                                                 f(o_hi[r, ds(2 * i + c, 1), :]), ALU.subtract)
                    last.then_inc(o_lo_done, 1)

            split(B_MLAP + 2)
            split(B_MLAP + 3)
            merge(T_WO_SWA, False, 0, 2)
            dve.wait_ge(pre_copied, QT)
            t1, t2 = kvq[:, :, 384:400], kvq[:, :, 400:416]
            for n, (a, b) in enumerate(((t1, cos_t), (t2, sin_t), (t2, cos_t), (t1, sin_t))):
                dve.tensor_tensor(rtmp[:, n, :, :], a, b, ALU.mult).then_inc(kr_step, 1)
            dve.wait_ge(kr_step, 4)
            dve.wait_ge(nhalf_done, 2)
            dve.tensor_tensor(kpad[:, :, 64:80], rtmp[:, 0, :, :], rtmp[:, 1, :, :],
                              ALU.subtract).then_inc(kr_step, 1)
            dve.tensor_tensor(kpad[:, :, 80:96], rtmp[:, 2, :, :], rtmp[:, 3, :, :], ALU.add).then_inc(kr_step, 1)
            mean_sq(Q_CQ, Q_CKV, QL)
            mean_sq(Q_CKV, Q_X1, KVL)
            merge(T_WO_SWA, False, 2, 3)
            dve.wait_ge(rstd_done, BATCH_MLA + 1)
            for t in range(QT):
                for n, (a, b) in enumerate(((0, QL), (QL, QL + KVL))):
                    col_n = (Q_CKV if n else Q_CQ) + t
                    dve.tensor_scalar(kvq[:, t, a:b], kvq[:, t, a:b], rstd[:, col_n:col_n + 1], None,
                                      ALU.mult).then_inc(xn_done, 1)
            merge(T_WO_SWA, False, 3, 5)
            split(B_MLA, n=N_A)
            for k in range(2):
                tp_part(N_MLA + k, cq_lo[:, k, :], bank(2 + k), g_q[:, k:k + 1], cq_hi[:, k, :])
            tp_part(N_MLA + 2, ckv_lo, bank(4), g_kv[:, 0:1], ckv_hi)
            dve.wait_ge(tp_hi, N_MLA + 4)
            for c in range(2):
                last = dve.tensor_tensor(ka_lo[64:96, c, :], bank(5)[64:96, :], f(ka_hi[64:96, c, :]), ALU.subtract)
            last.then_inc(tp_lo, 1)

            def key(t, n, c, per=0, i=0):
                lo(n, per, i, ka_lo[0:64, c, :], bank(t % 2)[0:64, :], ka_hi[0:64, c, :], t % 2)

            def query_rotary(t, c, per=0, i=0):
                rows = bank(t % 2)[64:96, :]
                dve.wait_ge(tile_ready, t + 1 + per * i)
                dve.tensor_tensor(rope_b[c], rows, cos_f[64:96, :], ALU.mult)
                dve.stream_shuffle(rope_a[c], rows, [(p + 16) % 32 for p in range(32)]).then_inc(rope_in, 1)

            def query_plain(t, n, c, per=0, i=0):
                lo(n, per, i, q_lo[0:64, c, :], bank(t % 2)[0:64, :], q_hi[0:64, c, :], t % 2)

            def rotary(n, c, per=0, i=0):
                dve.wait_ge(tile_hi, n + 1 + per * i)
                dve.tensor_tensor(q_lo[64:96, c, :], rope_b[c], f(q_hi[64:96, c, :]),
                                  ALU.subtract).then_inc(q_done, 1)

            merge(T_WO_SWA, False, 5)
            query_rotary(T_MLA, 0)
            query_plain(T_MLA, H_MLA, 0)
            key(T_MLA + 1, H_MLA + 1, 0)

            def two_heads(i, final=False):
                t0, u0, b, n0 = T_MLA + 2, U_MLA, B_MLA, H_MLA + 2
                key(t0, n0, 1, 7, i)
                rotary(n0 + 1, 0, 7, i)
                query_rotary(t0 + 1, 1, 6, i)

                def pk(c, n):
                    peak(u0 + 4 * c + n, 8, i, 1, P * (n + 1), QK ** -0.5)

                def nm(c, n):
                    norm(u0 + 4 * c + n, 8, i, 1, P * (n + 1))

                def p(c, n):
                    at = (slice(None), slice(0, n + 1), slice(P * n, P * n + P))
                    pt(u0 + 4 * c + n, 8, i, pt_lo.rearrange("p (k q) -> p k q", k=4)[at],
                       bank(4 + n % 2, 0, P * (n + 1)).rearrange("p (k q) -> p k q", q=P),
                       pt_hi.rearrange("p (k q) -> p k q", k=4)[at])

                def o(c):
                    r = slice(64 * c, 64 * c + 64)
                    dve.wait_ge(o_hi_done, E_MLA + c + 1 + 2 * i)
                    dve.tensor_tensor(o_lo[r, ds(i, 1), :], bank(6 + c)[r, :].rearrange("p (m n) -> p m n", m=1),
                                      f(o_hi[r, ds(i, 1), :]), ALU.subtract).then_inc(o_lo_done, 1)

                n_a = BLK if final else N_A
                pk(0, 0)
                pk(0, 1)
                nm(0, 0)
                nm(0, 1)
                query_plain(t0 + 1, n0 + 2, 1, 7, i)
                p(0, 0)
                pk(0, 2)
                dve.wait_ge(tile_hi, n0 + 4 + 7 * i)
                dve.tensor_tensor(v_lo, bank(6).rearrange("p (k n) -> p k n", k=4), f(v_hi),
                                  ALU.subtract).then_inc(v_lo_done, 1)
                nm(0, 2)
                p(0, 1)
                pk(0, 3)
                rotary(n0 + 4, 1, 7, i)
                nm(0, 3)
                p(0, 2)
                p(0, 3)
                pk(1, 0)
                pk(1, 1)
                nm(1, 0)
                nm(1, 1)
                dve.wait_ge(w_lo_done, b + 2 + 2 * i)
                p(1, 0)
                pk(1, 2)
                split(b + 2, 2, i, n=n_a, stop=n_a // 3)
                nm(1, 2)
                p(1, 1)
                pk(1, 3)
                split(b + 2, 2, i, n=n_a, start=n_a // 3, stop=2 * n_a // 3)
                nm(1, 3)
                split(b + 2, 2, i, n=n_a, start=2 * n_a // 3)
                o(0)
                p(1, 2)
                p(1, 3)
                if not final:
                    query_rotary(t0 + 4, 0, 6, i)
                    query_plain(t0 + 4, n0 + 5, 0, 7, i)
                    key(t0 + 5, n0 + 6, 0, 7, i)
                o(1)
                if final:
                    merge(T_WO_MLA, False, 0, 2)
                    split(b + 3, 2, i)

            with dve.Fori(0, HA // 2 - 1) as i:
                two_heads(i)
            two_heads(HA // 2 - 1, True)

            def split_s(n, ring_hi, ring_lo, src, scale, count, slot):
                dve.wait_ge(s_hi_done, count)
                part_n = src[:, ds(1024 * n, 1024)]
                if scale == 1.0:
                    ins = dve.tensor_tensor(ring_lo[:, slot, :], part_n, f(ring_hi[:, slot, :]), ALU.subtract)
                else:
                    ins = dve.scalar_tensor_tensor(ring_lo[:, slot, :], part_n, scale, f(ring_hi[:, slot, :]),
                                                   ALU.mult, ALU.subtract)
                ins.then_inc(s_lo_done, 1)

            merge(T_WO_MLA, False, 2, 4)
            dve.wait_ge(y_done, KD + 4)
            split_s(0, yr_hi, yr_lo, ybuf, 0.5, 1, 0)
            merge(T_WO_MLA, False, 4, 5)
            split(B_WO_MLA + 2, stop=BLK // 2)
            merge(T_WO_MLA, False, 5, 6)
            split(B_WO_MLA + 2, start=BLK // 2)
            merge(T_WO_MLA, False, 6, 7)
            split_s(1, yr_hi, yr_lo, ybuf, 0.5, 2, 1)
            merge(T_WO_MLA, False, 7)
            split(B_WO_MLA + 3)
            dve.wait_ge(y_done, 2 * KD)
            for n in range(3):
                if n < 2:
                    split_s(n + 2, yr_hi, yr_lo, ybuf, 0.5, n + 3, n)
                    split(B_WOUT + n + 2)

            def add(t, steps, scale=None, halves=(0, 1)):
                for half in halves:
                    dve.wait_ge(acc_step, steps + 2 * t + half + 1)
                    dst, src = x_sb[:, t, 512 * half:512 * half + 512], bank(2 * t + half)
                    if scale is None:
                        ins = dve.tensor_tensor(dst, dst, src, ALU.add)
                    else:
                        ins = dve.scalar_tensor_tensor(dst, src, scale, dst, ALU.mult, ALU.add)
                    ins.then_inc(added, 1)

            def turned_again(t):
                turned(t, N_H2 + KD * t, lambda k: turned_x(t, k), h_lo, g_mlp, h_hi)

            dve.wait_ge(x_again, 16 * QT)
            add(0, 24)
            add(1, 24, halves=(0,))
            turned_again(0)
            add(1, 24, halves=(1,))
            for t in range(2, QT):
                add(t, 24)
                turned_again(t - 1)
            turned_again(QT - 1)
            dve.wait_ge(w_lo_done, B_UP + 1)
            split(B_UP + 1)
            mean_sq(Q_X1, Q_X2, D, inv_step)
            dve.wait_ge(inv_step, 1)
            dve.reciprocal(rstd[:, Q_X1:Q_X2], rstd[:, Q_X1:Q_X2]).then_inc(inv_step, 1)

            def up(i):
                for c in range(4):
                    slot, turn = ring(T_UP + c, 4, i)
                    dve.wait_ge(tile_done[slot], turn + 1)
                    dve.tensor_tensor(act_sq[:, ds(2048 * i + 512 * c, 512)], relu[:, c % 2, :], relu[:, c % 2, :],
                                      ALU.mult).then_inc(sq_act, 1)
                    if c % 2:
                        split(B_UP + 2 + c // 2, 2, i)

            up(0)
            with dve.Fori(1, FF // 512 - 1) as i:
                up(i)
            for n in range(2):
                split_s(n, ar_hi, ar_lo, act_sq, 1.0, 5 + n, n)
            up(FF // 512 - 1)
            dve.wait_ge(sq_act, FF // P)
            with dve.Fori(0, FF // 512 - 1) as i:
                for c in range(2):
                    split_s(2 * i + c + 2, ar_hi, ar_lo, act_sq, 1.0, 7 + c + 2 * i, c)
                    split(B_DOWN + 2 + c, 2, i)
            def gain(t, half):
                dve.wait_ge(added, 2 * (QT + t) + half + 1)
                a = slice(512 * half, 512 * half + 512)
                dve.tensor_tensor(fin[:, t, a], x_sb[:, t, a], fgain[:, a], ALU.mult).then_inc(gained, 1)

            dve.wait_ge(fgain_in, 16)
            dve.wait_ge(inv_step, 2)
            for t in range(QT):
                add(t, 32 + 120, rstd[:, Q_X1 + t:Q_X1 + t + 1])
                c = Q_X2 + t
                gain(t, 0)
                dve.wait_ge(sq_done, Q_X2 + 2 * t + 1)
                dve.tensor_scalar(rstd[:, c:c + 1], sumsq[:, c + t:c + t + 1], 1.0 / D, EPS, ALU.mult,
                                  ALU.add).then_inc(ms_done, 1)
                dve.wait_ge(sq_done, Q_X2 + 2 * t + 2)
                dve.wait_ge(ms_done, TURNS + 3 + 2 * t)
                dve.scalar_tensor_tensor(rstd[:, c:c + 1], sumsq[:, c + t + 1:c + t + 2], 1.0 / D, rstd[:, c:c + 1],
                                         ALU.mult, ALU.add).then_inc(ms_done, 1)
                if t >= 2:
                    gain(t, 1)
                    dve.wait_ge(rstd_done, BATCH_X2 + t + 1)
                    dve.wait_ge(gained, 2 * t)
                    dve.tensor_scalar(fin[:, t, 512:], fin[:, t, 512:], rstd[:, c:c + 1], None,
                                      ALU.mult).then_inc(out_right_late, 1)

        @block.tensor
        def _(pe):
            def need(c, per=0, i=0):
                pe.wait_ge(w_lo_done, c + 1 + per * i)
                return c % 2

            def bank_of(c, per=0, i=0):
                slot, turn = ring(c, per, i)
                wait(pe, tile_done[slot], turn)
                return slot

            def have(c, per=0, i=0):
                slot, turn = ring(c, per, i)
                pe.wait_ge(tile_done[slot], turn + 1)

            def mm3(dst, a, b, first, last):
                pe.matmul(dst, a[0], b[1], start=first, stop=False, skip_group_check=True)
                pe.matmul(dst, a[1], b[0], start=False, stop=False, skip_group_check=True)
                return pe.matmul(dst, a[0], b[0], start=False, stop=last, skip_group_check=True)

            def wpair(slot, at, k, n, c0=0, cn=P):
                return w(w_hi, slot, at, k, n, c0, cn), w(w_lo, slot, at, k, n, c0, cn)

            def hpair(k):
                return h_hi[:, k, :], h_lo[:, k, :]

            def project(bk, slot, at, k0=0, k1=KD, n=P, c0=0, split_to=None):
                for k in range(k0, k1):
                    if split_to is not None:
                        pe.wait_ge(tp_lo, split_to + k + 1)
                    last = mm3(bank(bk), wpair(slot, at, k, n, c0), hpair(k), k == 0, k == KD - 1)
                if k1 == KD:
                    last.then_inc(tile_ready, 1)

            def t_bank(u, per, i):
                pe.wait_ge(p_done, u + 1 + per * i)
                wait(pe, pt_lo_done, u - 1 + per * i)

            def s_bank(u, per, i):
                wait(pe, exp_done, u - 1 + per * i)

            def turn(src, banks, place):
                for j in range(banks):
                    for k in range(j, KD, banks):
                        last = pe.transpose(place(k), src[:, P * k:P * k + P], ident)
                    last.then_inc(tp_ready, 1)

            def turn_in(n):
                pe.wait_ge(xn_done, n + 1)
                wait(pe, tp_lo, KD * (n - 1))
                turn(token_rows[n], 3, lambda k: turned_bank(n, k))

            def mem_values(half, t):
                slot = need(B_MEM + half)
                pe.wait_ge(tp_lo, KD * (t + 1))
                tk = slice(P * t, P * t + P)
                for k in range(4):
                    kk = 4 * half + k
                    last = mm3(bank(6 + t), (mn_hi[:, kk, tk], mn_lo[:, kk, tk]), wpair(slot, 0, k, 512, 0, 512),
                               kk == 0, kk == KD - 1)
                if half == 1:
                    last.then_inc(vm_ready, 1)

            pe.wait_ge(ident_in, 16)
            turn_in(0)
            turn_in(1)
            turn_in(2)
            turn_in(3)
            mem_values(0, 0)
            mem_values(0, 1)
            turn_in(4)
            mem_values(1, 0)
            turn_in(5)
            mem_values(1, 1)

            def out_rows(m, slot, bk, k0, k1):
                for k in range(k0, k1):
                    last = mm3(bank(bk), wpair(slot, 0, k, 512, P * (m % 4)), (o_hi[:, k, :], o_lo[:, k, :]),
                               k == 0, k == 3)
                if k1 == 4:
                    last.then_inc(tile_ready, 1)

            def begin_out(b, t0, heads, newest, m):
                pe.wait_ge(o_lo_done, heads - newest)
                out_rows(m, need(b), bank_of(t0 + m), 0, 3)

            def out_proj(b, t0, heads, newest, m0=0, m1=KD, between=None, begun=0):
                if m0 == 0:
                    for m in range(begun, 2):
                        begin_out(b, t0, heads, newest, m)
                    pe.wait_ge(o_lo_done, heads)
                    for m in range(2):
                        out_rows(m, b % 2, (t0 + m) % 2, 3, 4)
                for m in range(max(m0, 2), m1):
                    out_rows(m, need(b + m // 4), bank_of(t0 + m), 0, 4)
                    if between is not None and m == 3:
                        between()

            def bias_row(a, b):
                pe.wait_ge(rel_step, 4)
                for n in range(a, b):
                    if n >= 4:
                        pe.wait_ge(frep_done, n - 3)
                    for j, part_r in enumerate((rel_lo, rel_hi)):
                        last = pe.matmul(bank(4 + n % 4, 0, TOE),
                                         part_r[0:BUCKETS + 1, n:n + 1].to_broadcast([BUCKETS + 1, P]),
                                         toe_r[0:BUCKETS + 1, :], start=j == 0, stop=j == 1, skip_group_check=True)
                    last.then_inc(fbank_ready, 1)

            for h in range(HM):
                t0, u0, b, e = T_MEM + 4 * h, U_MEM + 2 * h, B_MEM + 2 + 2 * h, E_MEM + h
                slot = need(b)
                project(bank_of(t0), slot, 0, split_to=KD * (TURNS - 1) if h == 0 else None)
                bk = bank_of(t0 + 1)
                for k in range(KD):
                    last = mm3(bank(bk, 0, M), wpair(slot, 1024, k, P), (mn_hi[:, k, :], mn_lo[:, k, :]),
                               k == 0, k == KD - 1)
                last.then_inc(tile_ready, 1)
                if h == 0:
                    bias_row(0, 4)
                slot, bk = need(b + 1), bank_of(t0 + 2)
                project(bk, slot, 0, 0, 3)
                if h == 0:
                    bias_row(4, HS)
                have(t0 + 1)
                for n in range(2):
                    s_bank(u0 + n, 0, 0)
                    for t in range(2):
                        tk = slice(P * (2 * n + t), P * (2 * n + t + 1))
                        last = mm3(bank(2 + n, M * t, M * t + M), (q_hi[:, h % 2, tk], q_lo[:, h % 2, tk]),
                                   (km_hi, km_lo), True, True)
                    last.then_inc(s_ready, 1)
                project(bk, slot, 0, 3, 8)
                bk = bank_of(t0 + 3)
                project(bk, slot, 1024, 0, 1)
                if h == 0:
                    pe.wait_ge(frep_done, HS)
                for n in range(2):
                    t_bank(u0 + n, 0, 0)
                    for k in range(2):
                        for t in range(2):
                            last = pe.transpose(bank(4 + n, 256 * k + P * t, 256 * k + P * t + P),
                                                probs[:, n, M * t + P * k:M * t + P * k + P], ident)
                    last.then_inc(t_ready, 1)
                project(bk, slot, 1024, 1, 8)
                pe.wait_ge(pt_lo_done, u0 + 2)
                pe.wait_ge(vm_lo_done, MT)
                wait(pe, o_lo_done, e)
                ptk = [buf[:, 0:1024].rearrange("p (u k q) -> p k u q", u=2, k=2) for buf in (pt_hi, pt_lo)]
                for k in range(2):
                    last = mm3(bank(6 + h % 2).rearrange("p (u q) -> p u q", u=2),
                               (vm_hi[:, k, DM * h:DM * h + DM], vm_lo[:, k, DM * h:DM * h + DM]),
                               [a[:, k, :, :] for a in ptk], k == 0, k == 1)
                last.then_inc(o_ready, 1)

            slot = need(B_KVS)
            project(bank_of(T_KVS), slot, 0)
            project(bank_of(T_KVS + 1), slot, 1024)

            def turn_values():
                pe.wait_ge(tile_done[(T_KVS + 1) % 2], T_KVS // 2 + 1)
                pe.wait_ge(pt_lo_done, U_SWA)
                for t in range(QT):
                    last = pe.transpose(bank(4, P * t, P * t + P), tmp[:, 0, P * t:P * t + P], ident)
                last.then_inc(vs_turned, 1)

            out_proj(B_WO_MEM, T_WO_MEM, E_SWA, 1, between=turn_values)
            pe.wait_ge(bias_lo_done, 1)
            pe.wait_ge(kz_zero, 4)
            pe.wait_ge(idr_done, 2)

            with pe.Fori(0, PAIRS // 2) as i:
                for c in range(2):
                    t0, u0, b = T_SWA + 3 * c, U_SWA + 4 * c, B_SWA + 2 * c
                    slot = need(b, 4, i)
                    project(bank_of(t0, 6, i), slot, 0)
                    bk = bank_of(t0 + 1, 6, i)
                    project(bk, slot, 1024, 0, 2)
                    have(t0, 6, i)

                    def scores(n):
                        s_bank(u0 + n, 8, i)
                        wd = P if n == 0 else 2 * P
                        k0 = max(P * (n - 1), 0)
                        dst = bank(2 + n % 2, 0, 2 * wd).rearrange("p (g n) -> p g n", g=2)
                        for j, buf in enumerate((bias_lo, bias_hi)):
                            pe.matmul(dst, ident_r, buf[:, :, ds(2 * i + c, 1), 2 * P - wd:2 * P]
                                      .rearrange("p g r n -> p g (r n)"), start=j == 0, stop=False,
                                      skip_group_check=True)
                        tk = slice(P * n, P * n + P)
                        mm3(dst, (q_hi[:, c, tk], q_lo[:, c, tk]), (kz_hi[:, :, k0:k0 + wd], kz_lo[:, :, k0:k0 + wd]),
                            False, True).then_inc(s_ready, 1)

                    def turn_p(n):
                        t_bank(u0 + n, 8, i)
                        wd = P if n == 0 else 2 * P
                        for s in range(1 if n == 0 else 0, 2):
                            for g in range(2):
                                a = g * wd + (0 if n == 0 else P * s)
                                last = pe.transpose(bank(4 + n % 2, 256 * s + P * g, 256 * s + P * g + P),
                                                    probs[:, n % 2, a:a + P], ident)
                        last.then_inc(t_ready, 1)

                    scores(0)
                    scores(1)
                    project(bk, slot, 1024, 2, 6)
                    turn_p(0)
                    scores(2)
                    project(bk, slot, 1024, 6, 8)
                    turn_p(1)
                    scores(3)
                    slot, bk = need(b + 1, 4, i), bank_of(t0 + 2, 6, i)
                    project(bk, slot, 0, 0, 3)
                    turn_p(2)
                    project(bk, slot, 0, 3, 5)
                    turn_p(3)
                    project(bk, slot, 0, 5, 8)
                    pe.wait_ge(pt_lo_done, u0 + 4 + 8 * i)
                    pe.wait_ge(o_lo_done, E_SWA + c + 2 * i)
                    pe.wait_ge(vs_lo_done, 1)
                    ptg = [buf.rearrange("p (m g q) -> p g m q", g=2, q=P) for buf in (pt_hi, pt_lo)]
                    for k in range(QT):
                        n = 2 if k < QT - 1 else 1
                        for g in range(2):
                            last = mm3(bank(6 + g, P * k, P * (k + n)).rearrange("p (m q) -> p m q", q=P),
                                       (v_hi[:, k, :], v_lo[:, k, :]),
                                       [a[:, g, 2 * k + 1:2 * k + 1 + n, :] for a in ptg], k == 0, k == QT - 1)
                    last.then_inc(o_ready, 1)

            pe.wait_ge(exp_done, U_MLA)
            pe.wait_ge(pt_lo_done, U_MLA)
            for half in range(2):
                slot = need(B_MLAP + half)
                for t in range(QT):
                    tk = slice(P * t, P * t + P)
                    for k in range(4):
                        kk = 4 * half + k
                        last = mm3(bank(2 + t, 0, 416), (h_hi[:, kk, tk], h_lo[:, kk, tk]),
                                   wpair(slot, 0, k, 416, 0, 416), kk == 0, kk == KD - 1)
                    if half == 1 or t == QT - 1:
                        last.then_inc(pre_ready, 1)
            out_proj(B_WO_SWA, T_WO_SWA, E_MLA, 1, 0, 5)
            pe.wait_ge(pre_copied, QT)
            pe.wait_ge(xn_done, TURNS + 2 * QT)
            pe.wait_ge(kr_step, 6)
            for k in range(3):
                for t in range(QT):
                    last = pe.transpose(bank(2 + k, P * t, P * t + P), kvq[:, t, P * k:P * k + P], ident)
                last.then_inc(tp_ready, 1)
            for t in range(QT):
                last = pe.transpose(bank(5, P * t, P * t + P)[0:QK, :], kpad[:, t, :], ident)
            last.then_inc(tp_ready, 1)
            out_proj(B_WO_SWA, T_WO_SWA, E_MLA, 1, 5)
            pe.wait_ge(tp_lo, N_H2)

            def key(t, slot, c, per=0, i=0):
                mm3(bank(bank_of(t, per, i)), wpair(slot, 4 * QK, c, P), (ckv_hi, ckv_lo), True,
                    True).then_inc(tile_ready, 1)

            def query(t, slot, c, per=0, i=0):
                bk = bank_of(t, per, i)
                for k in range(2):
                    last = mm3(bank(bk)[0:QK, :], wpair(slot, 0, k, 2 * QK, QK * c, QK),
                               (cq_hi[:, k, :], cq_lo[:, k, :]), k == 0, k == 1)
                last.then_inc(tile_ready, 1)

            slot = need(B_MLA)
            query(T_MLA, slot, 0)
            key(T_MLA + 1, slot, 0)

            def two_heads(i, final=False):
                t0, u0, b = T_MLA + 2, U_MLA, B_MLA
                slot = b % 2
                vw = [buf[:, slot, 4 * QK:4 * QK + 2 * P].rearrange("p (h t c) -> p h t c", h=2, t=2)[:, :, 1, :]
                      for buf in (w_hi, w_lo)]
                key(t0, slot, 1, 6, i)
                query(t0 + 1, slot, 1, 6, i)
                pe.wait_ge(o_lo_done, E_MLA - 1 + 2 * i)
                for k in range(QT):
                    tk = slice(P * k, P * k + P)
                    last = mm3(bank(6, P * k, P * k + P).rearrange("p (h c) -> p h c", h=2),
                               (ckv_hi[:, tk], ckv_lo[:, tk]), vw, True, True)
                last.then_inc(v_ready, 1)

                def scores(c, n):
                    s_bank(u0 + 4 * c + n, 8, i)
                    tk, kw = slice(P * n, P * n + P), P * (n + 1)
                    mm3(bank(2 + n % 2, 0, kw), (q_hi[0:QK, c, tk], q_lo[0:QK, c, tk]),
                        (ka_hi[0:QK, c, 0:kw], ka_lo[0:QK, c, 0:kw]), True, False)
                    pe.matmul(bank(2 + n % 2, P * n, P * n + P), ident_r, mask_r, start=False, stop=True,
                              skip_group_check=True).then_inc(s_ready, 1)

                def turn_p(c, n):
                    t_bank(u0 + 4 * c + n, 8, i)
                    for k in range(n + 1):
                        last = pe.transpose(bank(4 + n % 2, P * k, P * k + P), probs[:, n % 2, P * k:P * k + P], ident)
                    last.then_inc(t_ready, 1)

                def values(c):
                    pe.wait_ge(pt_lo_done, u0 + 4 * c + 4 + 8 * i)
                    pe.wait_ge(o_lo_done, E_MLA + c + 2 * i)
                    pe.wait_ge(v_lo_done, 1 + i)
                    for k in range(QT):
                        at = slice(512 * k + P * k, 512 * k + 512)
                        last = mm3(bank(6 + c, P * k, 512), (v_hi[:, k, :], v_lo[:, k, :]), (pt_hi[:, at], pt_lo[:, at]),
                                   k == 0, k == QT - 1)
                    last.then_inc(o_ready, 1)

                bk, at = bank_of(t0 + 2, 6, i), N_A - D
                project(bk, slot, at, 0, 1)
                pe.wait_ge(q_done, 2 * i + 1)
                scores(0, 0)
                scores(0, 1)
                project(bk, slot, at, 1, 4)
                turn_p(0, 0)
                scores(0, 2)
                project(bk, slot, at, 4, 5)
                turn_p(0, 1)
                scores(0, 3)
                project(bk, slot, at, 5, 6)
                turn_p(0, 2)
                project(bk, slot, at, 6, 8)
                slot, bk = need(b + 1, 2, i), bank_of(t0 + 3, 6, i)
                project(bk, slot, 0, 0, 1)
                turn_p(0, 3)
                pe.wait_ge(q_done, 2 * i + 2)
                scores(1, 0)
                scores(1, 1)
                project(bk, slot, 0, 1, 2)
                values(0)
                turn_p(1, 0)
                scores(1, 2)
                project(bk, slot, 0, 2, 4)
                turn_p(1, 1)
                scores(1, 3)
                project(bk, slot, 0, 4, 6)
                turn_p(1, 2)
                if not final:
                    project(bk, slot, 0, 6, 8)
                    turn_p(1, 3)
                else:
                    project(bk, slot, 0, 6, 7)
                    turn_p(1, 3)
                    project(bk, slot, 0, 7, 8)
                    begin_out(B_WO_MLA, T_WO_MLA, E_END, 2, 0)
                if not final:
                    slot = need(b + 2, 2, i)
                    query(t0 + 4, slot, 0, 6, i)
                    key(t0 + 5, slot, 0, 6, i)
                values(1)

            with pe.Fori(0, HA // 2 - 1) as i:
                two_heads(i)
            two_heads(HA // 2 - 1, True)

            out_proj(B_WO_MLA, T_WO_MLA, E_END, 2, begun=1)

            def accumulate(c, per, i, s_hi, s_lo, s_count, first=False, last=False, after=None,
                           tiles=0):
                slot = need(c, per, i)
                pe.wait_ge(s_lo_done, s_count)
                n = (c - B_WOUT) % 2
                for t in [1, 2, 3, 0] if tiles else range(QT):
                    if tiles and t == 0:
                        pe.wait_ge(tile_done[0], tiles)
                        pe.wait_ge(tile_done[1], tiles)
                    for half in range(2):
                        for k in range(2):
                            a = slice(512 * k + P * t, 512 * k + P * t + P)
                            ins = mm3(bank(2 * t + half), (s_hi[:, n, a], s_lo[:, n, a]),
                                      wpair(slot, 0, k, D, 512 * half, 512), first and k == 0, last and k == 1)
                        ins.then_inc(acc_step, 1)
                        if after is not None:
                            after(t, half)

            for n in range(D // 256 - 1):
                accumulate(B_WOUT + n, 0, 0, yr_hi, yr_lo, n + 1, n == 0, tiles=T_UP // 2 if n == 0 else 0)

            def turn_x(t):
                pe.wait_ge(added, 2 * t + 2)
                pe.wait_ge(tp_lo, N_H2 + KD * min(t, 2))
                turn(x_sb[:, t, :], 4 if t else 2, lambda k: turned_x(t, k))

            def turn_ready(t, half):
                if (t, half) in ((1, 0), (2, 1), (3, 1)):
                    turn_x(t - 1)

            accumulate(B_UP - 1, 0, 0, yr_hi, yr_lo, D // 256, last=True, after=turn_ready)
            turn_x(QT - 1)

            def up(i, first=False):
                for c in range(2):
                    slot = need(B_UP + c, 2, i)
                    for m in range(2):
                        project(bank_of(T_UP + 2 * c + m, 4, i), slot, 0, n=256, c0=P * m,
                                split_to=N_H2 + 3 * KD if first and not c and not m else None)

            up(0, True)
            with pe.Fori(1, FF // 512) as i:
                up(i)
            for c in range(2):
                accumulate(B_DOWN + c, 0, 0, ar_hi, ar_lo, 5 + c, c == 0, tiles=T_UP // 2 + FF // 256 if c == 0 else 0)
            with pe.Fori(1, FF // 512 - 1) as i:
                for c in range(2):
                    accumulate(B_DOWN + c, 2, i, ar_hi, ar_lo, 5 + c + 2 * i)
            for c in range(2):
                accumulate(B_END - 2 + c, 0, 0, ar_hi, ar_lo, 5 + FF // 256 - 2 + c, last=c == 1)


def constants():
    con = np.zeros((P, C_END), np.float32)
    con[:, C_ID:C_ID + P] = np.eye(P)
    con[:, C_MASK:C_MASK + P] = np.where(np.arange(P)[None, :] <= np.arange(P)[:, None], 0.0, NEG)
    pos = np.arange(S, dtype=np.float32)
    inv = (1.0 / (np.float32(10000.0) ** (np.arange(0, ROPE, 2, dtype=np.float32) / ROPE))).astype(np.float32)
    ang = pos[:, None] * inv[None, :]
    cos, sin = np.cos(ang), np.sin(ang)
    con[:, C_COST:C_COST + 64] = cos.reshape(QT, P, 16).transpose(1, 0, 2).reshape(P, 64)
    con[:, C_SINT:C_SINT + 64] = sin.reshape(QT, P, 16).transpose(1, 0, 2).reshape(P, 64)
    con[64:80, C_COS:C_COS + S] = con[80:96, C_COS:C_COS + S] = cos.T
    con[64:80, C_SIN:C_SIN + S] = -sin.T
    con[80:96, C_SIN:C_SIN + S] = sin.T
    dist = 2 * P - 1 - np.arange(TOE)
    inside = (dist >= 0) & (dist < P)
    n = np.maximum(dist, 1)
    exact = BUCKETS // 2
    large = exact + (np.log(n.astype(np.float32) / exact) / np.float32(np.log(P / exact))
                     * (BUCKETS - exact)).astype(np.int32)
    bucket = np.where(dist < exact, np.maximum(dist, 0), np.minimum(large, BUCKETS - 1))
    toe = np.zeros((BUCKETS + 1, TOE), np.float32)
    toe[0:BUCKETS, 0:TOE] = (bucket[None, :] == np.arange(BUCKETS)[:, None]) & inside[None, :]
    toe[BUCKETS] = np.where(inside, 0.0, NEG / DS ** 0.5)
    return con, toe


_INS = ["x", "mem", "rel_bias", "attn_norm", "mem_norm", "w_in", "b_gate", "mla_q_norm", "w_uq", "mla_kv_norm",
        "w_ukv", "attn_sinks", "w_mem_kv", "w_o_mla", "w_o_swa", "w_o_mem", "w_out", "mlp_norm", "w_up", "w_down",
        "final_norm"]


def kernel(**inputs):
    import concourse.bacc as _bacc
    from concourse.bass_utils import run_bass_kernel_spmd as _run

    nc = _bacc.Bacc("TRN2", target_bir_lowering=False, num_devices=1)
    given = {name: np.ascontiguousarray(inputs[name]) for name in _INS}
    given["consts"], given["toeplitz"] = constants()
    arrays, args = {}, []
    for name, a in given.items():
        arrays[f"in_{name}_dram"] = a
        args.append(nc.dram_tensor(f"in_{name}_dram", a.shape, mybir.dt.from_np(a.dtype), kind="ExternalInput").ap())
    args.append(nc.dram_tensor("out_0_dram", (1, S, D), F32, kind="ExternalOutput").ap())
    hybrid_layer(nc, *args)
    r = _run(nc, [arrays], core_ids=[0])
    return r.results[0]["out_0_dram"]
```
